# Optimizing a Trainium2 kernel written in Bass

```python
import math
import jax, jax.numpy as jnp
from jax import lax
import numpy as np

D_MODEL = 1024
BATCH = 1
SEQ = 256
DEPTH = 2

HEAD_DIM = 64
ROPE_DIM = HEAD_DIM // 4
ROPE_THETA = 500000.0
Q_BLOCK = 128
FOX_HEADS = D_MODEL // (2 * HEAD_DIM)
NSA_HEADS = D_MODEL // (2 * HEAD_DIM)
NSA_KV_GROUPS = 2
NSA_HPG = NSA_HEADS // NSA_KV_GROUPS
CMP_BLOCK = 32
CMP_STRIDE = 16
CMP_HIDDEN = 2 * HEAD_DIM
SLC_BLOCK = 64
SLC_TOPK = 16
WINDOW = 512
DIFF_HEADS = D_MODEL // (2 * HEAD_DIM)
MEM_TOKENS = 256
MEM_HEADS = 4
D_FF = 256 * math.ceil(8 * D_MODEL / 3 / 256)
N_EVEN = (DEPTH + 1) // 2
N_ODD = DEPTH // 2
RMS_EPS = 1e-6

FOX_W = FOX_HEADS * HEAD_DIM
NSA_W = NSA_HEADS * HEAD_DIM
NSA_KV_W = NSA_KV_GROUPS * HEAD_DIM
EVEN_SPLITS = (FOX_W, FOX_W, FOX_W, FOX_HEADS, NSA_W) + (NSA_KV_W,) * 6 + (3 * NSA_HEADS,)
EVEN_IN = sum(EVEN_SPLITS)
MIX_W = FOX_W + NSA_W
DIFF_QK_W = DIFF_HEADS * 2 * HEAD_DIM
DIFF_V_W = DIFF_HEADS * 2 * HEAD_DIM
ODD_IN = 2 * DIFF_QK_W + DIFF_V_W
MEM_W = MEM_HEADS * HEAD_DIM


def rms_norm(x, g):
    xf = x.astype(jnp.float32)
    y = xf * lax.rsqrt(jnp.mean(xf * xf, axis=-1, keepdims=True) + RMS_EPS)
    return (y * g.astype(jnp.float32)).astype(x.dtype)

def rope_tables(positions):
    inv = ROPE_THETA ** (-jnp.arange(0, ROPE_DIM, 2, dtype=jnp.float32) / ROPE_DIM)
    ang = positions.astype(jnp.float32)[..., None] * inv
    return jnp.cos(ang), jnp.sin(ang)

def apply_partial_rope(x, cos, sin):
    half = ROPE_DIM // 2
    x1, x2, rest = x[..., :half], x[..., half:ROPE_DIM], x[..., ROPE_DIM:]
    c = cos[:, :, None, :].astype(x.dtype)
    s = sin[:, :, None, :].astype(x.dtype)
    return jnp.concatenate([x1 * c - x2 * s, x2 * c + x1 * s, rest], axis=-1)

def masked_softmax(logits, mask):
    z = jnp.where(mask, logits.astype(jnp.float32), -jnp.inf)
    m = jnp.max(z, axis=-1, keepdims=True)
    m = jnp.where(jnp.isfinite(m), m, 0.0)
    p = jnp.exp(z - m)
    return p / jnp.maximum(jnp.sum(p, axis=-1, keepdims=True), 1e-30)

def stack_blocks(out, B, T):
    return jnp.moveaxis(out, 0, 1).reshape((B, T) + out.shape[3:])

def fox_attention(q, k, v, log_f):
    B, T, H, dh = q.shape
    c = jnp.cumsum(log_f, axis=1)
    c_k = jnp.transpose(c, (0, 2, 1))[:, :, None, :]
    kpos = jnp.arange(T)
    scale = dh ** -0.5

    def block(i):
        q0 = i * Q_BLOCK
        qb = lax.dynamic_slice_in_dim(q, q0, Q_BLOCK, 1)
        cq = jnp.transpose(lax.dynamic_slice_in_dim(c, q0, Q_BLOCK, 1), (0, 2, 1))[..., None]
        s = jnp.einsum('bqhd,bkhd->bhqk', qb, k).astype(jnp.float32) * scale + (cq - c_k)
        qpos = q0 + jnp.arange(Q_BLOCK)
        p = masked_softmax(s, kpos[None, :] <= qpos[:, None])
        return jnp.einsum('bhqk,bkhd->bqhd', p.astype(v.dtype), v)

    return stack_blocks(lax.map(block, jnp.arange(T // Q_BLOCK)), B, T)

def compress(x, pos, w1, w2):
    B, T, G, dh = x.shape
    nc = (T - CMP_BLOCK) // CMP_STRIDE + 1
    idx = np.arange(nc)[:, None] * CMP_STRIDE + np.arange(CMP_BLOCK)[None, :]
    blocks = x[:, idx] + pos[None, None, :, None, :].astype(x.dtype)
    flat = jnp.moveaxis(blocks, 3, 2).reshape(B, nc, G, CMP_BLOCK * dh)
    return jax.nn.gelu(flat @ w1) @ w2

def nsa_attention(q, kc, vc, ks, vs, kw, vw, gates):
    B, T, H, dh = q.shape
    G = NSA_KV_GROUPS
    nc = kc.shape[1]
    ns = T // SLC_BLOCK
    n_sel = min(SLC_TOPK, ns)
    scale = dh ** -0.5
    cmp_start = np.arange(nc) * CMP_STRIDE
    slc_start = np.arange(ns) * SLC_BLOCK
    cmp_end = jnp.asarray(cmp_start + CMP_BLOCK - 1)
    ov = np.clip(np.minimum(cmp_start[:, None] + CMP_BLOCK, slc_start[None, :] + SLC_BLOCK)
                 - np.maximum(cmp_start[:, None], slc_start[None, :]), 0, None) / CMP_BLOCK
    overlap = jnp.asarray(ov, dtype=jnp.float32)
    blk = jnp.arange(ns)
    k_blocks = jnp.transpose(ks.reshape(B, ns, SLC_BLOCK, G, dh), (0, 3, 1, 2, 4))
    v_blocks = jnp.transpose(vs.reshape(B, ns, SLC_BLOCK, G, dh), (0, 3, 1, 2, 4))
    kw_pad = jnp.pad(kw, ((0, 0), (WINDOW, 0), (0, 0), (0, 0)))
    vw_pad = jnp.pad(vw, ((0, 0), (WINDOW, 0), (0, 0), (0, 0)))
    bi = jnp.arange(B)[:, None, None, None]
    gi = jnp.arange(G)[None, :, None, None]

    def block(i):
        q0 = i * Q_BLOCK
        qpos = q0 + jnp.arange(Q_BLOCK)
        qg = lax.dynamic_slice_in_dim(q, q0, Q_BLOCK, 1).reshape(B, Q_BLOCK, G, NSA_HPG, dh)
        gb = lax.dynamic_slice_in_dim(gates, q0, Q_BLOCK, 1).reshape(B, Q_BLOCK, G, NSA_HPG, 3)
        s_c = jnp.einsum('bqgnd,bcgd->bgnqc', qg, kc).astype(jnp.float32) * scale
        p_c = masked_softmax(s_c, cmp_end[None, :] <= qpos[:, None])
        o_c = jnp.einsum('bgnqc,bcgd->bqgnd', p_c.astype(vc.dtype), vc)
        imp = jnp.einsum('bgnqc,cs->bgqs', p_c, overlap)
        cur = (qpos // SLC_BLOCK)[:, None]
        valid = blk[None, :] * SLC_BLOCK <= qpos[:, None]
        forced = (blk[None, :] == 0) | (blk[None, :] == cur) | (blk[None, :] == cur - 1)
        score = jnp.where(valid, jnp.where(forced, jnp.inf, imp), -jnp.inf)
        _, sel = lax.top_k(score, n_sel)
        k_sel = k_blocks[bi, gi, sel]
        v_sel = v_blocks[bi, gi, sel].reshape(B, G, Q_BLOCK, n_sel * SLC_BLOCK, dh)
        tok = sel[..., None] * SLC_BLOCK + jnp.arange(SLC_BLOCK)
        smask = (tok <= qpos[None, None, :, None, None]).reshape(B, G, 1, Q_BLOCK, n_sel * SLC_BLOCK)
        s_s = jnp.einsum('bqgnd,bgqkld->bgnqkl', qg, k_sel).astype(jnp.float32) * scale
        p_s = masked_softmax(s_s.reshape(B, G, NSA_HPG, Q_BLOCK, n_sel * SLC_BLOCK), smask)
        o_s = jnp.einsum('bgnqm,bgqmd->bqgnd', p_s.astype(v_sel.dtype), v_sel)
        kwb = lax.dynamic_slice_in_dim(kw_pad, q0, WINDOW + Q_BLOCK, 1)
        vwb = lax.dynamic_slice_in_dim(vw_pad, q0, WINDOW + Q_BLOCK, 1)
        kpos = q0 - WINDOW + jnp.arange(WINDOW + Q_BLOCK)
        wmask = ((kpos[None, :] <= qpos[:, None]) & (kpos[None, :] > qpos[:, None] - WINDOW)
                 & (kpos[None, :] >= 0))
        s_w = jnp.einsum('bqgnd,bkgd->bgnqk', qg, kwb).astype(jnp.float32) * scale
        p_w = masked_softmax(s_w, wmask)
        o_w = jnp.einsum('bgnqk,bkgd->bqgnd', p_w.astype(vwb.dtype), vwb)
        o = gb[..., 0:1] * o_c + gb[..., 1:2] * o_s + gb[..., 2:3] * o_w
        return o.reshape(B, Q_BLOCK, H, dh)

    return stack_blocks(lax.map(block, jnp.arange(T // Q_BLOCK)), B, T)

def diff_attention(q1, q2, k1, k2, v, lam):
    B, T, H, dh = q1.shape
    kpos = jnp.arange(T)
    scale = dh ** -0.5

    def block(i):
        q0 = i * Q_BLOCK
        qpos = q0 + jnp.arange(Q_BLOCK)
        mask = kpos[None, :] <= qpos[:, None]
        qb1 = lax.dynamic_slice_in_dim(q1, q0, Q_BLOCK, 1)
        qb2 = lax.dynamic_slice_in_dim(q2, q0, Q_BLOCK, 1)
        a1 = masked_softmax(jnp.einsum('bqhd,bkhd->bhqk', qb1, k1).astype(jnp.float32) * scale, mask)
        a2 = masked_softmax(jnp.einsum('bqhd,bkhd->bhqk', qb2, k2).astype(jnp.float32) * scale, mask)
        p = a1 - lam * a2
        return jnp.einsum('bhqk,bkhd->bqhd', p.astype(v.dtype), v)

    return stack_blocks(lax.map(block, jnp.arange(T // Q_BLOCK)), B, T)

def even_mixer(h, cos, sin, w_in, f_bias, cpk, c1k, c2k, cpv, c1v, c2v, w_out):
    B, T, _ = h.shape
    G = NSA_KV_GROUPS
    offsets = [int(o) for o in np.cumsum(EVEN_SPLITS)[:-1]]
    fq, fk, fv, fl, nq, kc, vc, ksl, vsl, kwn, vwn, gl = jnp.split(h @ w_in, offsets, axis=-1)
    heads = lambda t, n: t.reshape(B, T, n, HEAD_DIM)
    rope = lambda t: apply_partial_rope(t, cos, sin)
    log_f = jax.nn.log_sigmoid(fl.astype(jnp.float32) + f_bias.astype(jnp.float32))
    o_fox = fox_attention(heads(fq, FOX_HEADS), heads(fk, FOX_HEADS), heads(fv, FOX_HEADS), log_f)
    o_nsa = nsa_attention(
        rope(heads(nq, NSA_HEADS)),
        compress(rope(heads(kc, G)), cpk, c1k, c2k),
        compress(heads(vc, G), cpv, c1v, c2v),
        rope(heads(ksl, G)), heads(vsl, G),
        rope(heads(kwn, G)), heads(vwn, G),
        jax.nn.sigmoid(gl).reshape(B, T, NSA_HEADS, 3))
    o = jnp.concatenate([o_fox.reshape(B, T, FOX_W), o_nsa.reshape(B, T, NSA_W)], axis=-1)
    return o @ w_out

def diff_mixer(h, cos, sin, w_in, lam_p, subln_g, w_out, layer):
    B, T, _ = h.shape
    q, k, v = jnp.split(h @ w_in, [DIFF_QK_W, 2 * DIFF_QK_W], axis=-1)
    q = apply_partial_rope(q.reshape(B, T, 2 * DIFF_HEADS, HEAD_DIM), cos, sin).reshape(B, T, DIFF_HEADS, 2, HEAD_DIM)
    k = apply_partial_rope(k.reshape(B, T, 2 * DIFF_HEADS, HEAD_DIM), cos, sin).reshape(B, T, DIFF_HEADS, 2, HEAD_DIM)
    v = v.reshape(B, T, DIFF_HEADS, 2 * HEAD_DIM)
    lam_init = 0.8 - 0.6 * math.exp(-0.3 * layer)
    lp = lam_p.astype(jnp.float32)
    lam = jnp.exp(jnp.sum(lp[0] * lp[1])) - jnp.exp(jnp.sum(lp[2] * lp[3])) + lam_init
    o = diff_attention(q[..., 0, :], q[..., 1, :], k[..., 0, :], k[..., 1, :], v, lam)
    o = rms_norm(o, subln_g) * (1.0 - lam_init)
    return o.reshape(B, T, DIFF_V_W) @ w_out

def memory_cross_attention(h, mem_n, wq, wk, wv, wo):
    B, T, _ = h.shape
    M = mem_n.shape[1]
    q = (h @ wq).reshape(B, T, MEM_HEADS, HEAD_DIM)
    k = (mem_n @ wk).reshape(B, M, MEM_HEADS, HEAD_DIM)
    v = (mem_n @ wv).reshape(B, M, MEM_HEADS, HEAD_DIM)
    s = jnp.einsum('bqhd,bmhd->bhqm', q, k).astype(jnp.float32) * HEAD_DIM ** -0.5
    p = jax.nn.softmax(s, axis=-1)
    o = jnp.einsum('bhqm,bmhd->bqhd', p.astype(v.dtype), v).reshape(B, T, MEM_W)
    return o @ wo

def swiglu(h, wg, wu, wd):
    return (jax.nn.silu(h @ wg) * (h @ wu)) @ wd

def first_inputs(seed: int = 0) -> dict:
    key = jax.random.key(seed)
    ks = jax.random.split(key, 32)

    def nrm(k, shape, fan_in):
        return jax.random.normal(k, shape, jnp.float32) * (fan_in ** -0.5)

    def gain(k, shape):
        return 1.0 + 0.02 * jax.random.normal(k, shape, jnp.float32)

    D = D_MODEL
    flat_cmp = CMP_BLOCK * HEAD_DIM
    return {
        'x': jax.random.normal(ks[0], (BATCH, SEQ, D), jnp.float32),
        'mem': jax.random.normal(ks[1], (BATCH, MEM_TOKENS, D), jnp.float32),
        'positions': jnp.broadcast_to(jnp.arange(SEQ, dtype=jnp.int32), (BATCH, SEQ)),
        'sandwich_g': gain(ks[2], (DEPTH, 6, D)),
        'mem_norm_g': gain(ks[3], (DEPTH, D)),
        'ev_w_in': nrm(ks[4], (N_EVEN, D, EVEN_IN), D),
        'ev_fox_fbias': 4.0 + 0.5 * jax.random.normal(ks[5], (N_EVEN, FOX_HEADS), jnp.float32),
        'ev_cmp_pos_k': 0.02 * jax.random.normal(ks[6], (N_EVEN, CMP_BLOCK, HEAD_DIM), jnp.float32),
        'ev_cmp_w1_k': nrm(ks[7], (N_EVEN, flat_cmp, CMP_HIDDEN), flat_cmp),
        'ev_cmp_w2_k': nrm(ks[8], (N_EVEN, CMP_HIDDEN, HEAD_DIM), CMP_HIDDEN),
        'ev_cmp_pos_v': 0.02 * jax.random.normal(ks[9], (N_EVEN, CMP_BLOCK, HEAD_DIM), jnp.float32),
        'ev_cmp_w1_v': nrm(ks[10], (N_EVEN, flat_cmp, CMP_HIDDEN), flat_cmp),
        'ev_cmp_w2_v': nrm(ks[11], (N_EVEN, CMP_HIDDEN, HEAD_DIM), CMP_HIDDEN),
        'ev_w_out': nrm(ks[12], (N_EVEN, MIX_W, D), MIX_W),
        'od_w_in': nrm(ks[13], (N_ODD, D, ODD_IN), D),
        'od_lambda': 0.1 * jax.random.normal(ks[14], (N_ODD, 4, HEAD_DIM), jnp.float32),
        'od_subln_g': gain(ks[15], (N_ODD, 2 * HEAD_DIM)),
        'od_w_out': nrm(ks[16], (N_ODD, DIFF_V_W, D), DIFF_V_W),
        'ca_wq': nrm(ks[17], (DEPTH, D, MEM_W), D),
        'ca_wk': nrm(ks[18], (DEPTH, D, MEM_W), D),
        'ca_wv': nrm(ks[19], (DEPTH, D, MEM_W), D),
        'ca_wo': nrm(ks[20], (DEPTH, MEM_W, D), MEM_W),
        'ffn_wg': nrm(ks[21], (DEPTH, D, D_FF), D),
        'ffn_wu': nrm(ks[22], (DEPTH, D, D_FF), D),
        'ffn_wd': nrm(ks[23], (DEPTH, D_FF, D), D_FF),
    }

def first_block(x, mem, positions, sandwich_g, mem_norm_g, ev_w_in, ev_fox_fbias,
              ev_cmp_pos_k, ev_cmp_w1_k, ev_cmp_w2_k, ev_cmp_pos_v, ev_cmp_w1_v, ev_cmp_w2_v,
              ev_w_out, od_w_in, od_lambda, od_subln_g, od_w_out,
              ca_wq, ca_wk, ca_wv, ca_wo, ffn_wg, ffn_wu, ffn_wd):
    cos, sin = rope_tables(positions)
    for layer in range(DEPTH):
        g = sandwich_g[layer]
        h = rms_norm(x, g[0])
        if layer % 2 == 0:
            e = layer // 2
            y = even_mixer(h, cos, sin, ev_w_in[e], ev_fox_fbias[e],
                           ev_cmp_pos_k[e], ev_cmp_w1_k[e], ev_cmp_w2_k[e],
                           ev_cmp_pos_v[e], ev_cmp_w1_v[e], ev_cmp_w2_v[e], ev_w_out[e])
        else:
            o = layer // 2
            y = diff_mixer(h, cos, sin, od_w_in[o], od_lambda[o], od_subln_g[o], od_w_out[o], layer)
        x = x + rms_norm(y, g[1])
        mem_n = rms_norm(mem, mem_norm_g[layer])
        y = memory_cross_attention(rms_norm(x, g[2]), mem_n, ca_wq[layer], ca_wk[layer], ca_wv[layer], ca_wo[layer])
        x = x + rms_norm(y, g[3])
        y = swiglu(rms_norm(x, g[4]), ffn_wg[layer], ffn_wu[layer], ffn_wd[layer])
        x = x + rms_norm(y, g[5])
    return x


GRID_W = 64
EPS = 1e-6
NA_HEADS = 8
NA_HEAD_DIM = 64
NA_WIN_R = 8
NA_WIN_C = 16
NA_QCOLS = 16
NA_KCOLS = 2 * NA_WIN_C
GLA_HEADS = 4
GLA_DK = 64
GLA_DV = 128
GLA_GATE_RANK = 16
GLA_GATE_TAU = 16.0
GLA_CHUNK = 64
MLA_HEADS = 4
MLA_Q_RANK = 256
MLA_KV_RANK = 256
MLA_NOPE = 128
MLA_ROPE = 64
MLA_V = 128
MLA_QBLOCK = 128
ROPE_THETA_2 = 10000.0
D_FF_2 = 2816
N_BRANCH = 3
NA_W = NA_HEADS * NA_HEAD_DIM
GLA_QK_W = GLA_HEADS * GLA_DK
GLA_V_W = GLA_HEADS * GLA_DV
MLA_QK_HEAD = MLA_NOPE + MLA_ROPE
MLA_V_W = MLA_HEADS * MLA_V
IN_SPLITS = (NA_W, NA_W, NA_W,
             GLA_QK_W, GLA_QK_W, GLA_V_W, GLA_V_W, GLA_GATE_RANK, GLA_GATE_RANK,
             MLA_Q_RANK, MLA_KV_RANK, MLA_ROPE,
             N_BRANCH * D_MODEL)
D_IN = 6752


def rms_norm_2(x, g):
    xf = x.astype(jnp.float32)
    y = xf * lax.rsqrt(jnp.mean(xf * xf, axis=-1, keepdims=True) + EPS)
    return (y * g.astype(jnp.float32)).astype(x.dtype)

def swiglu_2(h, w1, w3, w2):
    return (jax.nn.silu(h @ w1) * (h @ w3)) @ w2

def split_cols(z, sizes):
    out, start = [], 0
    for n in sizes:
        out.append(z[..., start:start + n])
        start += n
    return out

def neighborhood_attention(q, k, v, rpb):
    B, S, H, d = q.shape
    rows = S // GRID_W
    win_r = min(NA_WIN_R, rows)
    nj = GRID_W // NA_QCOLS
    r = np.arange(rows)
    r0 = np.clip(r - win_r // 2, 0, rows - win_r)
    ridx = r0[:, None] + np.arange(win_r)
    j = np.arange(nj)
    k0 = np.clip(j * NA_QCOLS - NA_WIN_C // 2, 0, GRID_W - NA_KCOLS)
    cidx = k0[:, None] + np.arange(NA_KCOLS)
    qc = j[:, None] * NA_QCOLS + np.arange(NA_QCOLS)
    c0 = np.clip(qc - NA_WIN_C // 2, 0, GRID_W - NA_WIN_C)
    col_ok = (cidx[:, None, :] >= c0[..., None]) & (cidx[:, None, :] < c0[..., None] + NA_WIN_C)
    mask = np.broadcast_to(col_ok[:, :, None, :], (nj, NA_QCOLS, win_r, NA_KCOLS)).reshape(nj, NA_QCOLS, win_r * NA_KCOLS)
    dr = ridx - r[:, None] + (NA_WIN_R - 1)
    dc = np.clip(cidx[:, None, :] - qc[:, :, None] + (NA_WIN_C - 1), 0, 2 * NA_WIN_C - 2)
    bias = rpb[:, dr[:, None, None, :, None], dc[None, :, :, None, :]]
    bias = bias.reshape(H, rows, nj, NA_QCOLS, win_r * NA_KCOLS)

    ri = ridx[:, None, :, None]
    ci = cidx[None, :, None, :]
    kg = k.reshape(B, rows, GRID_W, H, d)[:, ri, ci].reshape(B, rows, nj, win_r * NA_KCOLS, H, d)
    vg = v.reshape(B, rows, GRID_W, H, d)[:, ri, ci].reshape(B, rows, nj, win_r * NA_KCOLS, H, d)
    qg = q.reshape(B, rows, nj, NA_QCOLS, H, d)
    s = jnp.einsum('brjqhd,brjkhd->bhrjqk', qg, kg).astype(jnp.float32) * (d ** -0.5)
    s = jnp.where(mask, s + bias.astype(jnp.float32), -1e30)
    p = jax.nn.softmax(s, axis=-1).astype(v.dtype)
    o = jnp.einsum('bhrjqk,brjkhd->brjqhd', p, vg)
    return o.reshape(B, S, H * d)

def gla_chunked(q, k, v, g, strict):
    B, H, S, dk = q.shape
    dv = v.shape[-1]
    n = S // GLA_CHUNK
    q = q.reshape(B, H, n, GLA_CHUNK, dk)
    k = k.reshape(B, H, n, GLA_CHUNK, dk)
    g = g.reshape(B, H, n, GLA_CHUNK, dk)
    v = v.reshape(B, H, n, GLA_CHUNK, dv)
    b = jnp.cumsum(g, axis=3)
    b_last = b[:, :, :, -1:, :]
    qe = q * jnp.exp(b)
    ke = k * jnp.exp(-b)
    k_end = k * jnp.exp(b_last - b)
    tri = np.tril(np.ones((GLA_CHUNK, GLA_CHUNK), dtype=bool), -1 if strict else 0)
    a = jnp.where(tri, jnp.einsum('bhnid,bhnjd->bhnij', qe, ke), 0.0)
    o_intra = jnp.einsum('bhnij,bhnjv->bhniv', a, v)
    upd = jnp.einsum('bhncd,bhncv->bhndv', k_end, v)
    decay = jnp.exp(b_last[:, :, :, 0, :])

    def step(state, inp):
        dec, u = inp
        return dec[..., None] * state + u, state

    init = jnp.zeros((B, H, dk, dv), q.dtype)
    _, s_prev = lax.scan(step, init, (jnp.moveaxis(decay, 2, 0), jnp.moveaxis(upd, 2, 0)))
    s_prev = jnp.moveaxis(s_prev, 0, 2)
    o = o_intra + jnp.einsum('bhnid,bhndv->bhniv', qe, s_prev)
    return o.reshape(B, H, S, dv)

def gla_bidirectional(q, k, v, g_fwd, g_bwd):
    t = lambda a: jnp.swapaxes(a.astype(jnp.float32), 1, 2)
    q, k, v, g_fwd, g_bwd = t(q), t(k), t(v), t(g_fwd), t(g_bwd)
    q = q * (GLA_DK ** -0.5)
    flip = lambda a: a[:, :, ::-1]
    o_f = gla_chunked(q, k, v, g_fwd, False)
    o_b = flip(gla_chunked(flip(q), flip(k), flip(v), flip(g_bwd), True))
    return jnp.swapaxes(o_f + o_b, 1, 2)

def rope_tables_2(S):
    half = MLA_ROPE // 2
    inv = ROPE_THETA_2 ** (-jnp.arange(half, dtype=jnp.float32) / half)
    ang = jnp.arange(S, dtype=jnp.float32)[:, None] * inv[None, :]
    return jnp.cos(ang), jnp.sin(ang)

def apply_rope(x, cos, sin):
    xf = x.astype(jnp.float32)
    x1, x2 = xf[..., :MLA_ROPE // 2], xf[..., MLA_ROPE // 2:]
    c, s = cos[None, :, None, :], sin[None, :, None, :]
    return jnp.concatenate([x1 * c - x2 * s, x1 * s + x2 * c], axis=-1).astype(x.dtype)

def blocked_softmax_attention(q, k, v, scale):
    B, S, H, dq = q.shape
    nb = S // MLA_QBLOCK
    qb = jnp.moveaxis(q.reshape(B, nb, MLA_QBLOCK, H, dq), 1, 0)

    def one(qblk):
        s = jnp.einsum('bqhd,bkhd->bhqk', qblk, k).astype(jnp.float32) * scale
        p = jax.nn.softmax(s, axis=-1).astype(v.dtype)
        return jnp.einsum('bhqk,bkhd->bqhd', p, v)

    o = lax.map(one, qb)
    return jnp.moveaxis(o, 0, 1).reshape(B, S, H * v.shape[-1])

def mla_attention(c_q, c_kv, k_rope, cq_norm, ckv_norm, w_uq, w_ukv, q_norm, k_norm, cos, sin):
    B, S, _ = c_q.shape
    q = (rms_norm_2(c_q, cq_norm) @ w_uq).reshape(B, S, MLA_HEADS, MLA_QK_HEAD)
    kv = (rms_norm_2(c_kv, ckv_norm) @ w_ukv).reshape(B, S, MLA_HEADS, MLA_NOPE + MLA_V)
    k_nope, v = kv[..., :MLA_NOPE], kv[..., MLA_NOPE:]
    k_r = jnp.broadcast_to(k_rope[:, :, None, :], (B, S, MLA_HEADS, MLA_ROPE))
    k = jnp.concatenate([k_nope, k_r], axis=-1)
    q = rms_norm_2(q, q_norm)
    k = rms_norm_2(k, k_norm)
    q = jnp.concatenate([q[..., :MLA_NOPE], apply_rope(q[..., MLA_NOPE:], cos, sin)], axis=-1)
    k = jnp.concatenate([k[..., :MLA_NOPE], apply_rope(k[..., MLA_NOPE:], cos, sin)], axis=-1)
    return blocked_softmax_attention(q, k, v, MLA_QK_HEAD ** -0.5)

def second_inputs(seed: int = 0) -> dict:
    key = jax.random.key(seed)
    ks = iter(jax.random.split(key, 32))
    L = DEPTH
    f32 = jnp.float32

    def w(shape, fan_in):
        return jax.random.normal(next(ks), shape, f32) * (fan_in ** -0.5)

    def gain(shape):
        return 1.0 + 0.05 * jax.random.normal(next(ks), shape, f32)

    def small(shape, scale, offset=0.0):
        return offset + scale * jax.random.normal(next(ks), shape, f32)

    return {
        "x": jax.random.normal(next(ks), (BATCH, SEQ, D_MODEL), f32),
        "ffn1_norm": gain((L, D_MODEL)),
        "ffn1_w1": w((L, D_MODEL, D_FF_2), D_MODEL),
        "ffn1_w3": w((L, D_MODEL, D_FF_2), D_MODEL),
        "ffn1_w2": w((L, D_FF_2, D_MODEL), D_FF_2),
        "mix_norm": gain((L, D_MODEL)),
        "w_in": w((L, D_MODEL, D_IN), D_MODEL),
        "na_q_norm": gain((L, NA_HEAD_DIM)),
        "na_k_norm": gain((L, NA_HEAD_DIM)),
        "na_rpb": small((L, NA_HEADS, 2 * NA_WIN_R - 1, 2 * NA_WIN_C - 1), 0.1),
        "gla_gf_up": w((L, GLA_GATE_RANK, GLA_QK_W), GLA_GATE_RANK),
        "gla_gf_bias": small((L, GLA_QK_W), 0.1, 2.0),
        "gla_gb_up": w((L, GLA_GATE_RANK, GLA_QK_W), GLA_GATE_RANK),
        "gla_gb_bias": small((L, GLA_QK_W), 0.1, 2.0),
        "gla_out_norm": gain((L, GLA_DV)),
        "mla_cq_norm": gain((L, MLA_Q_RANK)),
        "mla_ckv_norm": gain((L, MLA_KV_RANK)),
        "mla_w_uq": w((L, MLA_Q_RANK, MLA_HEADS * MLA_QK_HEAD), MLA_Q_RANK),
        "mla_w_ukv": w((L, MLA_KV_RANK, MLA_HEADS * (MLA_NOPE + MLA_V)), MLA_KV_RANK),
        "mla_q_norm": gain((L, MLA_QK_HEAD)),
        "mla_k_norm": gain((L, MLA_QK_HEAD)),
        "w_br_na": w((L, NA_W, D_MODEL), NA_W),
        "w_br_gla": w((L, GLA_V_W, D_MODEL), GLA_V_W),
        "w_br_mla": w((L, MLA_V_W, D_MODEL), MLA_V_W),
        "w_out": w((L, D_MODEL, D_MODEL), D_MODEL),
        "ffn2_norm": gain((L, D_MODEL)),
        "ffn2_w1": w((L, D_MODEL, D_FF_2), D_MODEL),
        "ffn2_w3": w((L, D_MODEL, D_FF_2), D_MODEL),
        "ffn2_w2": w((L, D_FF_2, D_MODEL), D_FF_2),
    }

def second_block(x, ffn1_norm, ffn1_w1, ffn1_w3, ffn1_w2, mix_norm, w_in,
              na_q_norm, na_k_norm, na_rpb,
              gla_gf_up, gla_gf_bias, gla_gb_up, gla_gb_bias, gla_out_norm,
              mla_cq_norm, mla_ckv_norm, mla_w_uq, mla_w_ukv, mla_q_norm, mla_k_norm,
              w_br_na, w_br_gla, w_br_mla, w_out,
              ffn2_norm, ffn2_w1, ffn2_w3, ffn2_w2):
    B, S, D = x.shape
    cos, sin = rope_tables_2(S)
    for l in range(DEPTH):
        x = x + 0.5 * swiglu_2(rms_norm_2(x, ffn1_norm[l]), ffn1_w1[l], ffn1_w3[l], ffn1_w2[l])

        h = rms_norm_2(x, mix_norm[l])
        z = h @ w_in[l]
        (na_q, na_k, na_v, gq, gk, gv, gr, gfl, gbl, c_q, c_kv, k_rope, gates) = split_cols(z, IN_SPLITS)

        qa = rms_norm_2(na_q.reshape(B, S, NA_HEADS, NA_HEAD_DIM), na_q_norm[l])
        ka = rms_norm_2(na_k.reshape(B, S, NA_HEADS, NA_HEAD_DIM), na_k_norm[l])
        va = na_v.reshape(B, S, NA_HEADS, NA_HEAD_DIM)
        y_na = neighborhood_attention(qa, ka, va, na_rpb[l])

        g_f = jax.nn.log_sigmoid((gfl @ gla_gf_up[l] + gla_gf_bias[l]).astype(jnp.float32)) / GLA_GATE_TAU
        g_b = jax.nn.log_sigmoid((gbl @ gla_gb_up[l] + gla_gb_bias[l]).astype(jnp.float32)) / GLA_GATE_TAU
        o_gla = gla_bidirectional(gq.reshape(B, S, GLA_HEADS, GLA_DK), gk.reshape(B, S, GLA_HEADS, GLA_DK),
                                  gv.reshape(B, S, GLA_HEADS, GLA_DV),
                                  g_f.reshape(B, S, GLA_HEADS, GLA_DK), g_b.reshape(B, S, GLA_HEADS, GLA_DK))
        o_gla = rms_norm_2(o_gla, gla_out_norm[l]).astype(x.dtype).reshape(B, S, GLA_V_W)
        y_gla = o_gla * jax.nn.silu(gr)

        y_mla = mla_attention(c_q, c_kv, k_rope, mla_cq_norm[l], mla_ckv_norm[l], mla_w_uq[l], mla_w_ukv[l],
                              mla_q_norm[l], mla_k_norm[l], cos, sin)

        gt = jax.nn.sigmoid(gates.reshape(B, S, N_BRANCH, D))
        mixed = (gt[:, :, 0] * (y_na @ w_br_na[l])
                 + gt[:, :, 1] * (y_gla @ w_br_gla[l])
                 + gt[:, :, 2] * (y_mla @ w_br_mla[l]))
        x = x + mixed @ w_out[l]

        x = x + 0.5 * swiglu_2(rms_norm_2(x, ffn2_norm[l]), ffn2_w1[l], ffn2_w3[l], ffn2_w2[l])
    return x


def setup_inputs(seed=0):
    out = dict(first_inputs(seed))
    for name, value in second_inputs(seed + 1).items():
        if name != "x":
            out[name + "_2"] = value
    return out


def reference(
    x, mem, positions, sandwich_g, mem_norm_g, ev_w_in, ev_fox_fbias, ev_cmp_pos_k, ev_cmp_w1_k,
    ev_cmp_w2_k, ev_cmp_pos_v, ev_cmp_w1_v, ev_cmp_w2_v, ev_w_out, od_w_in, od_lambda,
    od_subln_g, od_w_out, ca_wq, ca_wk, ca_wv, ca_wo, ffn_wg, ffn_wu, ffn_wd, ffn1_norm_2,
    ffn1_w1_2, ffn1_w3_2, ffn1_w2_2, mix_norm_2, w_in_2, na_q_norm_2, na_k_norm_2, na_rpb_2,
    gla_gf_up_2, gla_gf_bias_2, gla_gb_up_2, gla_gb_bias_2, gla_out_norm_2, mla_cq_norm_2,
    mla_ckv_norm_2, mla_w_uq_2, mla_w_ukv_2, mla_q_norm_2, mla_k_norm_2, w_br_na_2, w_br_gla_2,
    w_br_mla_2, w_out_2, ffn2_norm_2, ffn2_w1_2, ffn2_w3_2, ffn2_w2_2,
):
    x = first_block(
        x, mem, positions, sandwich_g, mem_norm_g, ev_w_in, ev_fox_fbias, ev_cmp_pos_k,
        ev_cmp_w1_k, ev_cmp_w2_k, ev_cmp_pos_v, ev_cmp_w1_v, ev_cmp_w2_v, ev_w_out, od_w_in,
        od_lambda, od_subln_g, od_w_out, ca_wq, ca_wk, ca_wv, ca_wo, ffn_wg, ffn_wu, ffn_wd,
    )
    return second_block(
        x, ffn1_norm_2, ffn1_w1_2, ffn1_w3_2, ffn1_w2_2, mix_norm_2, w_in_2, na_q_norm_2,
        na_k_norm_2, na_rpb_2, gla_gf_up_2, gla_gf_bias_2, gla_gb_up_2, gla_gb_bias_2,
        gla_out_norm_2, mla_cq_norm_2, mla_ckv_norm_2, mla_w_uq_2, mla_w_ukv_2, mla_q_norm_2,
        mla_k_norm_2, w_br_na_2, w_br_gla_2, w_br_mla_2, w_out_2, ffn2_norm_2, ffn2_w1_2,
        ffn2_w3_2, ffn2_w2_2,
    )


_drawn_inputs = setup_inputs


def setup_inputs(seed=0):
    import zlib

    import numpy as np

    out = dict(_drawn_inputs(seed))
    spreads = {}
    factors = {'ev_cmp_pos_k': 8.0,
     'ev_cmp_pos_v': 3.152,
     'od_subln_g': 4.622,
     'ffn1_norm_2': 4.678,
     'na_q_norm_2': 8.0,
     'na_k_norm_2': 8.0,
     'na_rpb_2': 26.411,
     'gla_gf_bias_2': 55.808,
     'gla_gb_bias_2': 57.512,
     'gla_out_norm_2': 7.679,
     'mla_cq_norm_2': 8.0,
     'mla_ckv_norm_2': 6.295,
     'mla_q_norm_2': 8.0,
     'mla_k_norm_2': 8.0,
     'ffn2_norm_2': 4.799,
     'gla_gf_up_2': 8.0,
     'gla_gb_up_2': 8.0}
    for name, (base, spread) in spreads.items():
        noise = np.random.default_rng([zlib.crc32(name.encode()), seed]).standard_normal(out[name].shape)
        drawn = base * np.exp(spread * noise) if base else spread * noise
        out[name] = __import__('jax').numpy.asarray(drawn.astype(out[name].dtype))
    for name, factor in factors.items():
        out[name] = (out[name] * factor).astype(out[name].dtype)
    return out
```

```python
import math
from collections import namedtuple
from contextlib import ExitStack

import numpy as np
import concourse.bass as bass
from concourse import mybir

F32 = mybir.dt.float32
I32 = mybir.dt.int32
ALU = mybir.AluOpType
ACT = mybir.ActivationFunctionType
AX = mybir.AxisListType

P = 128
T = 256
TT = T // P
D = 1024
KD = D // P
HD = 64
EPS = 1e-6
NEG = -1e30

ROPE_HALF = HD // 8
ROPE_THETA = 500000.0
FOX_H = 8
NSA_H = 8
CMP_BLOCK, CMP_STRIDE = 32, 16
NC = (T - CMP_BLOCK) // CMP_STRIDE + 1
D_FF = 2816
MEM_H = 4
DIFF_H = 8
LAM_INIT = 0.8 - 0.6 * math.exp(-0.3 * 1)
DEPTH = 2
EV, at = {}, 0
for _name, _w in (("fq", 512), ("fk", 512), ("fv", 512), ("fl", 8), ("nq", 512), ("kc", 128), ("vc", 128),
                  ("ks", 128), ("vs", 128), ("kw", 128), ("vw", 128), ("gl", 24)):
    EV[_name] = at
    at += _w
EV_IN = at

GRID_W = 64
NA_H = 8
NA_WIN_R, NA_WIN_C = 8, 16
RPB_R, RPB_C = 2 * NA_WIN_R - 1, 2 * NA_WIN_C - 1
GLA_H, GLA_DK, GLA_DV, GLA_CHUNK, GLA_RANK, GLA_TAU = 4, 64, 128, 64, 16, 16.0
MLA_H, MLA_NOPE, MLA_ROPE, MLA_V = 4, 128, 64, 128
MLA_QK = MLA_NOPE + MLA_ROPE
ROPE_THETA_2 = 10000.0
ZC, at = {}, 0
for _name, _w in (("naq", 512), ("nak", 512), ("nav", 512), ("gq", 256), ("gk", 256), ("gv", 512), ("gr", 512),
                  ("gfl", 16), ("gbl", 16), ("cq", 256), ("ckv", 256), ("kr", 64), ("gates", 3 * D)):
    ZC[_name] = at
    at += _w

TBL_LO = (NA_WIN_R - T // GRID_W) * RPB_C + NA_WIN_C - 1 - (GRID_W - 1)
TBL_HI = (NA_WIN_R - 2 + T // GRID_W) * RPB_C + NA_WIN_C - 1 + GRID_W
TBL_W = TBL_HI - TBL_LO

SLOT = 2048
SLOTS = 8
FF_CHUNK = 256


def constants():
    p = np.arange(P)
    t = np.arange(T)
    parts = {}
    parts["ident"] = np.eye(P)
    tok = np.arange(TT)[:, None] * P + p[None, :]
    parts["causal"] = np.where(t[None, None, :] <= tok.T[:, :, None], 0.0, NEG)
    cmp_end = np.arange(NC) * CMP_STRIDE + CMP_BLOCK - 1
    parts["cmp"] = np.where(cmp_end[None, None, :] <= tok.T[:, :, None], 0.0, NEG)
    qc = p % GRID_W
    kc = t % GRID_W
    c0 = np.clip(qc - NA_WIN_C // 2, 0, GRID_W - NA_WIN_C)
    parts["na"] = np.where((kc[None] >= c0[:, None]) & (kc[None] < c0[:, None] + NA_WIN_C), 0.0, NEG)
    parts["upto"] = (tok.T[:, :, None] <= t[None, None, :]) * 1.0
    parts["shift"] = (tok.T[:, :, None] == t[None, None, :] + 1) * 1.0
    same = (p[:, None] // GLA_CHUNK) == (p[None, :] // GLA_CHUNK)
    parts["tri_f"] = (same & (p[:, None] <= p[None, :])) / GLA_TAU
    parts["tri_b"] = (same & (p[:, None] >= p[None, :])) / GLA_TAU
    parts["strict_b"] = (same & (p[:, None] > p[None, :])) * 1.0
    parts["chunk_all"] = same / GLA_TAU
    parts["chunk_of"] = ((p[:, None] // GLA_CHUNK) == np.arange(P // GLA_CHUNK)[None, :]) / GLA_TAU
    half = MLA_ROPE // 2
    inv2 = (np.float32(ROPE_THETA_2) ** (-np.arange(half, dtype=np.float32) / np.float32(half))).astype(np.float32)
    ang = tok.T[:, :, None].astype(np.float32) * inv2
    parts["cos2"] = np.cos(ang.astype(np.float64))
    parts["sin2"] = np.sin(ang.astype(np.float64))
    inv = np.float32(ROPE_THETA) ** (-np.arange(0, 2 * ROPE_HALF, 2, dtype=np.float32) / np.float32(2 * ROPE_HALF))
    parts["inv"] = np.broadcast_to(inv[None, :], (P, ROPE_HALF))
    parts["minus_half"] = np.full((P, 16), -0.5)
    parts["one"] = np.ones((P, 1))
    where, cols, c = {}, [], 0
    for name, a in parts.items():
        a = np.ascontiguousarray(a, dtype=np.float32).reshape(P, -1)
        where[name] = (c, a.shape[1])
        cols.append(a)
        c += a.shape[1]
    return np.concatenate(cols, axis=1), where




class Signal:

    def __init__(self, sem):
        self.sem, self.n = sem, 0

    def up(self, k=1):
        self.n += k
        return self.sem, k

    def now(self):
        return self.sem, self.n


Marks = namedtuple("Marks", "pe act dve pool")


class Bank:

    def __init__(self, tensor, start):
        self.t, self.drained = tensor, start


class Chunk:

    def __init__(self, view, landed, slots):
        self.view, self.landed, self.slots = view, landed, slots


def program(nc, a, const_where, out):
    ctx = ExitStack()
    with ctx:
        def sb(name, shape, dt=F32):
            return ctx.enter_context(nc.sbuf_tensor(name, shape, dt))

        def signal(name):
            return Signal(ctx.enter_context(nc.semaphore(name)))

        CONST_N = sum(w for _, w in const_where.values())
        const = sb("const", [P, CONST_N])
        x = sb("x", [P, TT, D])
        hT = sb("hT", [P, KD, T])
        hT2 = sb("hT2", [P, KD, T])
        o_buf = sb("o_buf", [P, TT, D])
        sq = sb("sq", [P, TT, D])
        z = sb("z", [P, TT, ZC["gates"]])
        gate = sb("gate", [P, TT, D])
        qT = sb("qT", [P, KD, T])
        kT = sb("kT", [P, KD, T])
        tmp = sb("tmp", [P, TT, D])
        ring = sb("ring", [P, SLOTS, SLOT])
        gain = sb("gain", [P, TT, D])
        smask = sb("smask", [P, 2, T])
        probs = sb("probs", [P, 3, T])
        pT = sb("pT", [P, 2, TT, P])
        rows = sb("rows", [P, 2, P])
        cols = sb("cols", [P, 2, P])
        stat = sb("stat", [P, 64])
        rs = sb("rs", [P, 32])
        jobstat = sb("jobstat", [P, 8, 4])
        rope = sb("rope", [P, 8, TT, ROPE_HALF])
        small = sb("small", [P, 128])
        up = sb("up", [GLA_RANK + 1, 2, T])
        posi = sb("posi", [P, TT], I32)
        rgain = sb("rgain", [P, 4, MLA_ROPE])


        pe_did = signal("pe_did")
        act_did = signal("act_did")
        dve_did = signal("dve_did")
        pool_did = signal("pool_did")
        const_landed = signal("const_landed")
        gain_landed = [signal(f"gain_landed{i}") for i in range(4)]
        slot_landed = [signal(f"slot_landed{i}") for i in range(SLOTS)]
        out_landed = signal("out_landed")
        misc_landed = signal("misc_landed")
        slot_used = [pe_did.now()] * SLOTS
        banks = [Bank(ctx.enter_context(nc.psum_tensor(f"bank{i}", [P, 512], F32)), dve_did.now()) for i in range(8)]
        turn = {"bank": 0, "slot": 0, "evac": 0, "gain": 0}

        block = ctx.enter_context(nc.Block())

        def C(name, shape=None, rows_=P):
            c, w = const_where[name]
            v = const[0:rows_, c:c + w]
            return v if shape is None else v.rearrange("p (a b) -> p a b", a=shape[0])

        ident = C("ident")

        def marks():
            return Marks(pe_did.now(), act_did.now(), dve_did.now(), pool_did.now())

        def next_bank():
            b = banks[turn["bank"] % 8]
            turn["bank"] += 1
            return b


        def load_weights(parts, shape):
            need = -(-shape[1] * shape[2] // SLOT)
            if turn["slot"] % SLOTS + need > SLOTS:
                turn["slot"] += SLOTS - turn["slot"] % SLOTS
            s0 = turn["slot"] % SLOTS
            turn["slot"] += need
            view = ring[0:shape[0], s0:s0 + need, :].rearrange("p s n -> p (s n)")[:, 0:shape[1] * shape[2]]
            view = view.rearrange("p (a b) -> p a b", a=shape[1])

            @block.sync
            def _(sp):
                for s in range(s0, s0 + need):
                    sp.wait_ge(*slot_used[s])
                for dst, src in parts(view):
                    sp.dma_start(dst, src).then_inc(*slot_landed[s0].up(16))
            return Chunk(view, slot_landed[s0].now(), range(s0, s0 + need))

        def release(chunk):
            for s in chunk.slots:
                slot_used[s] = pe_did.now()

        def to_T(nblk, src, dst, width=P, scale=None, group=2):
            before = marks()
            for b0 in range(0, nblk, group):
                n = min(group, nblk - b0)
                bank = next_bank()

                @block.tensor
                def _(pe):
                    pe.wait_ge(*bank.drained)
                    pe.wait_ge(*before.act)
                    pe.wait_ge(*before.dve)
                    pe.wait_ge(*before.pool)
                    for b in range(n):
                        for tt in range(TT):
                            m = pe.transpose(bank.t[0:width, (b * TT + tt) * P:(b * TT + tt + 1) * P],
                                             src(b0 + b, tt), ident)
                    m.then_inc(*pe_did.up())
                full = pe_did.now()
                turn["evac"] += 1
                if turn["evac"] % 2:
                    @block.vector
                    def _(dve):
                        dve.wait_ge(*full)
                        dve.wait_ge(*before.pe)
                        dve.wait_ge(*before.act)
                        dve.wait_ge(*before.dve)
                        dve.wait_ge(*before.pool)
                        ps = bank.t[0:width, 0:n * T].rearrange("p (a b) -> p a b", a=n)
                        if scale is None:
                            dve.tensor_copy(dst(b0, n), ps).then_inc(*dve_did.up())
                        else:
                            for b in range(n):
                                dve.tensor_scalar(dst(b0 + b, 1), ps[:, b:b + 1, :], scale(b0 + b), None,
                                                  ALU.mult).then_inc(*dve_did.up())
                    bank.drained = dve_did.now()
                else:
                    @block.scalar
                    def _(act):
                        act.wait_ge(*full)
                        act.wait_ge(*before.pe)
                        act.wait_ge(*before.act)
                        act.wait_ge(*before.dve)
                        act.wait_ge(*before.pool)
                        ps = bank.t[0:width, 0:n * T].rearrange("p (a b) -> p a b", a=n)
                        if scale is None:
                            act.copy(dst(b0, n), ps).then_inc(*act_did.up())
                        else:
                            for b in range(n):
                                act.activation(dst(b0 + b, 1), ps[:, b:b + 1, :], ACT.Copy,
                                               scale=scale(b0 + b)).then_inc(*act_did.up())
                    bank.drained = act_did.now()

        def gemm(lhsT, nk, W, lo, hi, evac, ready=None):
            ready = ready or marks()
            for c in range(lo, hi, 512):
                n = min(512, hi - c)
                src = W[:, c:c + n].rearrange("(k p) n -> p k n", p=P)
                chunk = load_weights(lambda v: [(v, src)], (P, nk, n))
                for tt in range(TT):
                    bank = next_bank()

                    @block.tensor
                    def _(pe):
                        pe.wait_ge(*chunk.landed)
                        pe.wait_ge(*bank.drained)
                        pe.wait_ge(*ready.act)
                        pe.wait_ge(*ready.dve)
                        pe.wait_ge(*ready.pool)
                        for k in range(nk):
                            m = pe.matmul(bank.t[:, 0:n], lhsT(k, tt), chunk.view[:, k, :],
                                          start=(k == 0), stop=(k == nk - 1))
                        m.then_inc(*pe_did.up())
                    evac(tt, c - lo, n, bank, pe_did.now())
                release(chunk)

        def to_sbuf(dst, r=None, bias_before=None):
            before = marks()

            def evac(tt, c, n, bank, full):
                if tt == 0:
                    @block.vector
                    def _(dve):
                        dve.wait_ge(*full)
                        dve.wait_ge(*before.pe)
                        dve.wait_ge(*before.act)
                        dve.wait_ge(*before.dve)
                        dve.wait_ge(*before.pool)
                        if r is None:
                            dve.tensor_copy(dst(tt, c, n), bank.t[:, 0:n]).then_inc(*dve_did.up())
                        else:
                            dve.tensor_scalar(dst(tt, c, n), bank.t[:, 0:n], r(tt), None,
                                              ALU.mult).then_inc(*dve_did.up())
                    bank.drained = dve_did.now()
                else:
                    @block.scalar
                    def _(act):
                        act.wait_ge(*full)
                        act.wait_ge(*before.pe)
                        act.wait_ge(*before.act)
                        act.wait_ge(*before.dve)
                        act.wait_ge(*before.pool)
                        if r is None:
                            act.copy(dst(tt, c, n), bank.t[:, 0:n]).then_inc(*act_did.up())
                        else:
                            act.activation(dst(tt, c, n), bank.t[:, 0:n], ACT.Copy,
                                           scale=r(tt)).then_inc(*act_did.up())
                    bank.drained = act_did.now()
            return evac

        def power(dst, n, scale):
            @block.vector
            def _(dve):
                dve.wait_ge(*pe_did.now())
                dve.wait_ge(*act_did.now())
                dve.wait_ge(*dve_did.now())
                dve.wait_ge(*pool_did.now())
                dve.tensor_scalar(dst, dst, scale, EPS, ALU.mult, ALU.add).then_inc(*dve_did.up())

            @block.gpsimd
            def _(pool):
                pool.wait_ge(*pe_did.now())
                pool.wait_ge(*act_did.now())
                pool.wait_ge(*dve_did.now())
                pool.wait_ge(*pool_did.now())
                pool.tensor_tensor(dst, dst, C("minus_half")[:, 0:n], ALU.pow).then_inc(*pool_did.up())

        def rstd_rows(src, dst):
            @block.scalar
            def _(act):
                act.wait_ge(*pe_did.now())
                act.wait_ge(*act_did.now())
                act.wait_ge(*dve_did.now())
                act.wait_ge(*pool_did.now())
                for tt in range(TT):
                    act.activation(sq[:, tt, :], src[:, tt, :], ACT.Square,
                                   accum_out=dst[:, tt:tt + 1]).then_inc(*act_did.up())
            power(dst, TT, 1.0 / D)

        def rstd_heads(src, dst, heads, w):
            v = sq[:, :, 0:heads * w].rearrange("p t (h w) -> p t h w", h=heads)

            @block.scalar
            def _(act):
                act.wait_ge(*pe_did.now())
                act.wait_ge(*act_did.now())
                act.wait_ge(*dve_did.now())
                act.wait_ge(*pool_did.now())
                for tt in range(TT):
                    act.activation(v[:, tt], src[:, tt], ACT.Square).then_inc(*act_did.up())

            @block.vector
            def _(dve):
                dve.wait_ge(*pe_did.now())
                dve.wait_ge(*act_did.now())
                dve.wait_ge(*dve_did.now())
                dve.wait_ge(*pool_did.now())
                for tt in range(TT):
                    dve.tensor_reduce(dst[:, tt * heads:(tt + 1) * heads], v[:, tt], AX.X,
                                      ALU.add).then_inc(*dve_did.up())
            power(dst, TT * heads, 1.0 / w)

        def scale_heads(dst, src, r, heads):
            w = src.shape[3]

            def part(eng, tt):
                return eng.tensor_tensor(dst[:, tt], src[:, tt],
                                         r[:, tt * heads:(tt + 1) * heads].unsqueeze(2).broadcast_to([P, heads, w]),
                                         ALU.mult)
            before = marks()

            @block.vector
            def _(dve):
                dve.wait_ge(*before.pe)
                dve.wait_ge(*before.act)
                dve.wait_ge(*before.dve)
                dve.wait_ge(*before.pool)
                part(dve, 0).then_inc(*dve_did.up())

            @block.gpsimd
            def _(pool):
                pool.wait_ge(*before.pe)
                pool.wait_ge(*before.act)
                pool.wait_ge(*before.dve)
                pool.wait_ge(*before.pool)
                part(pool, 1).then_inc(*pool_did.up())

        def attention(jobs):
            before = marks()
            st = [dict() for _ in jobs]

            def scores(i):
                j, s = jobs[i], st[i]
                bank = s["bank"] = next_bank()

                @block.tensor
                def _(pe):
                    pe.wait_ge(*bank.drained)
                    pe.wait_ge(*before.act)
                    pe.wait_ge(*before.dve)
                    pe.wait_ge(*before.pool)
                    for m, (l, r) in enumerate(j["qk"]):
                        mm = pe.matmul(bank.t[:, 0:j["n"]], l, r, start=(m == 0), stop=(m == len(j["qk"]) - 1))
                    mm.then_inc(*pe_did.up())
                scored = pe_did.now()
                n, js = j["n"], jobstat[:, i % 8, :]

                @block.vector
                def _(dve):
                    dve.wait_ge(*scored)
                    if i >= 2:
                        dve.wait_ge(*st[i - 2]["exped"])
                    if i < 2:
                        dve.wait_ge(*before.pe)
                        dve.wait_ge(*before.act)
                        dve.wait_ge(*before.dve)
                        dve.wait_ge(*before.pool)
                    if j["bias"] is not None:
                        dve.scalar_tensor_tensor(smask[:, i % 2, 0:n], bank.t[:, 0:n], j["scale"], j["bias"],
                                                 ALU.mult, ALU.add).then_inc(*dve_did.up())
                        dve.wait_ge(*dve_did.now())
                        dve.tensor_reduce(js[:, 0:1], smask[:, i % 2, 0:n], AX.X, ALU.max,
                                          negate=True).then_inc(*dve_did.up())
                        if j.get("guard"):
                            dve.wait_ge(*dve_did.now())
                            dve.tensor_scalar(js[:, 0:1], js[:, 0:1], -NEG / 10, None,
                                              ALU.min).then_inc(*dve_did.up())
                    else:
                        dve.tensor_reduce(js[:, 1:2], bank.t[:, 0:n], AX.X, ALU.max,
                                          negate=True).then_inc(*dve_did.up())
                        dve.wait_ge(*dve_did.now())
                        dve.tensor_scalar(js[:, 0:1], js[:, 1:2], j["scale"], None, ALU.mult).then_inc(*dve_did.up())
                maxed = dve_did.now()

                @block.scalar
                def _(act):
                    act.wait_ge(*maxed)
                    if i >= 3:
                        act.wait_ge(*st[i - 3]["turned"])
                    if i < 3:
                        act.wait_ge(*before.pe)
                        act.wait_ge(*before.act)
                        act.wait_ge(*before.dve)
                        act.wait_ge(*before.pool)
                    if j["bias"] is not None:
                        act.activation(probs[:, i % 3, 0:n], smask[:, i % 2, 0:n], ACT.Exp, bias=js[:, 0:1],
                                       accum_out=js[:, 2:3]).then_inc(*act_did.up())
                    else:
                        act.activation(probs[:, i % 3, 0:n], bank.t[:, 0:n], ACT.Exp, bias=js[:, 0:1],
                                       scale=j["scale"], accum_out=js[:, 2:3]).then_inc(*act_did.up())
                s["exped"] = act_did.now()
                bank.drained = act_did.now()

            def turned(i):
                j, s = jobs[i], st[i]
                bank = next_bank()

                @block.tensor
                def _(pe):
                    pe.wait_ge(*s["exped"])
                    pe.wait_ge(*bank.drained)
                    for b, v in enumerate(j["v"]):
                        kb = v.shape[0]
                        m = pe.transpose(bank.t[0:kb, b * P:(b + 1) * P], probs[:, i % 3, b * P:b * P + kb], ident)
                    m.then_inc(*pe_did.up())
                s["turned"] = pe_did.now()
                nb, kb = len(j["v"]), j["v"][0].shape[0]

                @block.scalar
                def _(act):
                    act.wait_ge(*s["turned"])
                    if i >= 2:
                        act.wait_ge(*st[i - 2]["summed"])
                    act.copy(pT[0:kb, i % 2, 0:nb, :],
                             bank.t[0:kb, 0:nb * P].rearrange("p (a b) -> p a b", a=nb)).then_inc(*act_did.up())
                s["copied"] = bank.drained = act_did.now()
                js = jobstat[:, i % 8, :]

                @block.vector
                def _(dve):
                    dve.wait_ge(*s["exped"])
                    if j.get("guard"):
                        dve.tensor_scalar(js[:, 2:3], js[:, 2:3], 1e-30, None, ALU.max).then_inc(*dve_did.up())
                        dve.wait_ge(*dve_did.now())
                    dve.reciprocal(js[:, 3:4], js[:, 2:3]).then_inc(*dve_did.up())
                    if j.get("mul") is not None:
                        dve.wait_ge(*dve_did.now())
                        dve.tensor_tensor(js[:, 3:4], js[:, 3:4], j["mul"], ALU.mult).then_inc(*dve_did.up())
                s["inverse"] = dve_did.now()

            def summed(i):
                j, s = jobs[i], st[i]
                bank = next_bank()

                @block.tensor
                def _(pe):
                    pe.wait_ge(*s["copied"])
                    pe.wait_ge(*bank.drained)
                    for b, v in enumerate(j["v"]):
                        m = pe.matmul(bank.t[:, 0:j["dv"]], pT[0:v.shape[0], i % 2, b, :], v,
                                      start=(b == 0), stop=(b == len(j["v"]) - 1))
                    m.then_inc(*pe_did.up())
                s["summed"] = pe_did.now()
                js = jobstat[:, i % 8, :]

                @block.vector
                def _(dve):
                    dve.wait_ge(*s["summed"])
                    dve.wait_ge(*s["inverse"])
                    if j.get("add"):
                        dve.wait_ge(*st[i - 1]["written"])
                    if j.get("add"):
                        dve.scalar_tensor_tensor(j["out"], bank.t[:, 0:j["dv"]], js[:, 3:4], j["out"],
                                                 ALU.mult, ALU.add).then_inc(*dve_did.up())
                    else:
                        dve.tensor_scalar(j["out"], bank.t[:, 0:j["dv"]], js[:, 3:4], None,
                                          ALU.mult).then_inc(*dve_did.up())
                s["written"] = bank.drained = dve_did.now()

            for i in range(len(jobs) + 2):
                if i < len(jobs):
                    scores(i)
                if 1 <= i <= len(jobs):
                    turned(i - 1)
                if i >= 2:
                    summed(i - 2)

        def ffn(wg, wu, wd, r, finish):
            before = marks()
            NF = D_FF // FF_CHUNK
            KB = FF_CHUNK // P
            pair = [banks[0:2], banks[2:4]]
            acc = banks[4:8]
            turn["bank"] = 0
            hid = tmp[:, 0, :].rearrange("p (s t n) -> p s t n", s=2, t=TT)
            silu = tmp[:, 1, :].rearrange("p (s t n) -> p s t n", s=2, t=TT)
            hidT = sq[:, 0, :].rearrange("p (s b n) -> p s b n", s=2, b=KB)
            down_w, hid_done, turned, copied = {}, {}, {}, {}
            down_done = {}

            def gate_up(c, tt, gu):
                bank = pair[c % 2][tt]

                @block.tensor
                def _(pe):
                    pe.wait_ge(*gu.landed)
                    pe.wait_ge(*bank.drained)
                    if c == 0:
                        pe.wait_ge(*before.act)
                        pe.wait_ge(*before.dve)
                        pe.wait_ge(*before.pool)
                    for k in range(KD):
                        m = pe.matmul(bank.t[:, :], hT[:, k, tt * P:(tt + 1) * P], gu.view[:, k, :],
                                      start=(k == 0), stop=(k == KD - 1))
                    m.then_inc(*pe_did.up())
                full = pe_did.now()

                @block.scalar
                def _(act):
                    act.wait_ge(*full)
                    if c >= 2:
                        act.wait_ge(*hid_done[(c - 2, tt)])
                    if c == 0:
                        act.wait_ge(*before.pe)
                        act.wait_ge(*before.act)
                        act.wait_ge(*before.dve)
                        act.wait_ge(*before.pool)
                    act.activation(silu[:, c % 2, tt, :], bank.t[:, 0:FF_CHUNK], ACT.Silu,
                                   scale=r(tt)).then_inc(*act_did.up())
                silued = act_did.now()

                @block.vector
                def _(dve):
                    dve.wait_ge(*full)
                    dve.wait_ge(*silued)
                    if c >= 2:
                        dve.wait_ge(*turned[c - 2])
                    if c == 0:
                        dve.wait_ge(*before.pe)
                        dve.wait_ge(*before.act)
                        dve.wait_ge(*before.dve)
                        dve.wait_ge(*before.pool)
                    dve.scalar_tensor_tensor(hid[:, c % 2, tt, :], bank.t[:, FF_CHUNK:2 * FF_CHUNK], r(tt),
                                             silu[:, c % 2, tt, :], ALU.mult, ALU.mult).then_inc(*dve_did.up())
                hid_done[(c, tt)] = bank.drained = dve_did.now()

            def transposes(c):
                bank = pair[c % 2][0]

                @block.tensor
                def _(pe):
                    pe.wait_ge(*hid_done[(c, 0)])
                    pe.wait_ge(*hid_done[(c, 1)])
                    for b in range(KB):
                        for tt in range(TT):
                            m = pe.transpose(bank.t[:, (b * TT + tt) * P:(b * TT + tt + 1) * P],
                                             hid[:, c % 2, tt, b * P:(b + 1) * P], ident)
                    m.then_inc(*pe_did.up())
                turned[c] = pe_did.now()

                @block.scalar
                def _(act):
                    act.wait_ge(*turned[c])
                    if c >= 2:
                        act.wait_ge(*down_done[c - 2])
                    act.copy(hidT[:, c % 2, :, :].rearrange("p b n -> p (b n)"),
                             bank.t[:, 0:KB * T]).then_inc(*act_did.up())
                copied[c] = bank.drained = act_did.now()

            def down(c):
                w = down_w[c]

                @block.tensor
                def _(pe):
                    pe.wait_ge(*w.landed)
                    pe.wait_ge(*copied[c])
                    if c == 0:
                        for b in acc:
                            pe.wait_ge(*b.drained)
                    for tt in range(TT):
                        for half in range(2):
                            for b in range(KB):
                                m = pe.matmul(acc[tt * 2 + half].t[:, :], hidT[:, c % 2, b, tt * P:(tt + 1) * P],
                                              w.view[:, b, half * 512:(half + 1) * 512],
                                              start=(c == 0 and b == 0), stop=(c == NF - 1 and b == KB - 1))
                    m.then_inc(*pe_did.up())
                down_done[c] = pe_did.now()
                release(w)

            for c in range(NF + 1):
                if c < NF:
                    cs = slice(c * FF_CHUNK, (c + 1) * FF_CHUNK)
                    gu = load_weights(lambda v: [
                        (v[:, :, 0:FF_CHUNK], wg[:, cs].rearrange("(k p) n -> p k n", p=P)),
                        (v[:, :, FF_CHUNK:2 * FF_CHUNK], wu[:, cs].rearrange("(k p) n -> p k n", p=P))],
                        (P, KD, 2 * FF_CHUNK))
                    down_w[c] = load_weights(
                        lambda v: [(v, wd[cs, :].rearrange("(k p) n -> p k n", p=P))], (P, KB, D))
                    gate_up(c, 0, gu)
                if c >= 1:
                    transposes(c - 1)
                if c < NF:
                    gate_up(c, 1, gu)
                    release(gu)
                if c >= 1:
                    down(c - 1)
            for tt in range(TT):
                for half in range(2):
                    finish(tt, half, acc[tt * 2 + half], pe_did.now())

        def add_half(tt, half, bank, full):
            @block.vector
            def _(dve):
                dve.wait_ge(*full)
                dve.wait_ge(*pe_did.now())
                dve.wait_ge(*act_did.now())
                dve.wait_ge(*dve_did.now())
                dve.wait_ge(*pool_did.now())
                xs = x[:, tt, half * 512:(half + 1) * 512]
                dve.scalar_tensor_tensor(xs, bank.t[:, :], 0.5, xs, ALU.mult, ALU.add).then_inc(*dve_did.up())
            bank.drained = dve_did.now()

        def finish_to_o(tt, half, bank, full):
            to_sbuf(lambda t, c, n: o_buf[:, t, half * 512:(half + 1) * 512])(tt, 0, 512, bank, full)

        def pre_norm(src, col, r):
            rstd_rows(src, r)
            to_T(KD, lambda b, tt: src[:, tt, b * P:(b + 1) * P], lambda b, n: hT[:, b:b + n, :],
                 scale=lambda b: cols[:, col // P, col % P + b:col % P + b + 1])

        def load_gain(src):
            g = turn["gain"] % 2
            turn["gain"] += 1
            before = marks()

            @block.sync
            def _(sp):
                sp.wait_ge(*before.pe)
                sp.wait_ge(*before.act)
                sp.wait_ge(*before.dve)
                sp.wait_ge(*before.pool)
                sp.dma_start(gain[:, g, :], src.partition_broadcast(P)).then_inc(*gain_landed[g].up(16))
            return gain[:, g, :], gain_landed[g].now()

        def post_norm(y, g):
            gv, landed = g
            rstd_rows(y, rs[:, 30:32])
            before = marks()

            @block.vector
            def _(dve):
                dve.wait_ge(*landed)
                dve.wait_ge(*before.pe)
                dve.wait_ge(*before.act)
                dve.wait_ge(*before.dve)
                dve.wait_ge(*before.pool)
                for tt in range(TT):
                    dve.scalar_tensor_tensor(y[:, tt, :], y[:, tt, :], rs[:, 30 + tt:31 + tt], gv,
                                             ALU.mult, ALU.mult).then_inc(*dve_did.up())
                dve.wait_ge(*dve_did.now())
                dve.tensor_tensor(x[:, 0, :], x[:, 0, :], y[:, 0, :], ALU.add).then_inc(*dve_did.up())

            @block.gpsimd
            def _(pool):
                pool.wait_ge(*dve_did.now())
                pool.wait_ge(*before.pe)
                pool.wait_ge(*before.act)
                pool.wait_ge(*before.dve)
                pool.wait_ge(*before.pool)
                pool.tensor_tensor(x[:, 1, :], x[:, 1, :], y[:, 1, :], ALU.add).then_inc(*pool_did.up())

        def rs_of(c):
            return lambda tt: rs[:, c + tt:c + tt + 1]

        hT_of = lambda k, tt: hT[:, k, tt * P:(tt + 1) * P]

        row_at = [0, P]
        col_of = {}

        @block.scalar
        def _(act):
            act.dma_start(const[:, :], a["const"]).then_inc(*const_landed.up(16))

            def row(name, src, n, tile):
                r = row_at[tile]
                act.dma_start(rows[r % P:r % P + n, tile, :], src.rearrange("(a b) -> a b", a=n)).then_inc(
                    *const_landed.up(16))
                col_of[name] = r
                row_at[tile] += n
            for l in range(DEPTH):
                for g in (0, 2, 4):
                    row(("pre", l, g), a["sandwich_g"][l, g, :], KD, 0)
                row(("mem", l), a["mem_norm_g"][l, :], KD, 0)
                for name in ("ffn1_norm_2", "mix_norm_2", "ffn2_norm_2"):
                    row((name, l), a[name][l, :], KD, 0)
            for name in ("ev_cmp_pos_k", "ev_cmp_pos_v"):
                row(name, a[name][0].rearrange("a b -> (a b)"), CMP_BLOCK // 2, 1)
            row("subln", a["od_subln_g"][0, :], 1, 1)
            for l in range(DEPTH):
                row(("gla_out", l), a["gla_out_norm_2"][l, :], 1, 1)
                row(("cq", l), a["mla_cq_norm_2"][l, :], 2, 1)
                row(("ckv", l), a["mla_ckv_norm_2"][l, :], 2, 1)
                row(("mla_q", l), a["mla_q_norm_2"][l, 0:P], 1, 1)
                row(("mla_k", l), a["mla_k_norm_2"][l, 0:P], 1, 1)
                for m, name in enumerate(("na_q_norm_2", "na_k_norm_2")):
                    r = row_at[1] - P
                    for h in range(2):
                        act.dma_start(rows[r:r + 1, 1, h * HD:(h + 1) * HD], a[name][l:l + 1, :]).then_inc(
                            *const_landed.up(16))
                    col_of[(name, l)] = row_at[1]
                    row_at[1] += 1
                    act.dma_start(rgain[:, l * 2 + m, :],
                                  a[("mla_q_norm_2", "mla_k_norm_2")[m]][l, P:MLA_QK].partition_broadcast(P)).then_inc(
                        *const_landed.up(16))
            act.dma_start(small[:, 0:FOX_H], a["ev_fox_fbias"][0, :].partition_broadcast(P)).then_inc(
                *const_landed.up(16))
            act.dma_start(tmp[:, 0, 0:4 * HD], a["od_lambda"][0].rearrange("a b -> (a b)").partition_broadcast(P)).then_inc(
                *const_landed.up(16))

            with nc.allow_non_contiguous_dma(reason="256 positions, once"):
                act.dma_start(posi[:, :], a["positions"][0, :].rearrange("(t p) -> p t", p=P)).then_inc(
                    *const_landed.up(16))

        table = nc.dram_tensor("bias_table", [DEPTH, NA_H, GRID_W, TBL_W], F32, kind="Internal").ap()
        table_landed = signal("table_landed")

        @block.gpsimd
        def _(pool):
            for l in range(DEPTH):
                flat = a["na_rpb_2"][l].rearrange("h r c -> h (r c)")[:, TBL_LO:TBL_HI]
                pool.dma_start(table[l], flat.unsqueeze(1).broadcast_to([NA_H, GRID_W, TBL_W])).then_inc(
                    *table_landed.up(16))

        @block.sync
        def _(sp):
            sp.dma_start(x[:, :, :], a["x"][0].rearrange("(t p) d -> p t d", p=P)).then_inc(*const_landed.up(16))
            sp.dma_start(gate[:, :, :], a["mem"][0].rearrange("(t p) d -> p t d", p=P)).then_inc(*const_landed.up(16))

        landed = const_landed.now()

        @block.vector
        def _(dve):
            dve.wait_ge(*landed)

        @block.scalar
        def _(act):
            act.wait_ge(*landed)

        @block.gpsimd
        def _(pool):
            pool.wait_ge(*landed)
            pool.memset(rs[:, :], 1.0).then_inc(*pool_did.up())

        used = [row_at[0], row_at[1] - P]
        bank = next_bank()

        @block.tensor
        def _(pe):
            pe.wait_ge(*landed)
            for tile in range(2):
                n = used[tile]
                m = pe.transpose(bank.t[:, tile * P:tile * P + n], rows[0:n, tile, :], ident[0:n, 0:n])
            m.then_inc(*pe_did.up())
        full = pe_did.now()

        @block.vector
        def _(dve):
            dve.wait_ge(*full)
            for tile in range(2):
                dve.tensor_copy(cols[:, tile, 0:used[tile]],
                                bank.t[:, tile * P:tile * P + used[tile]]).then_inc(*dve_did.up())
            dve.wait_ge(*dve_did.now())
            c = col_of["subln"] % P
            dve.tensor_scalar(cols[:, 1, c:c + 1], cols[:, 1, c:c + 1], 1.0 - LAM_INIT, None,
                              ALU.mult).then_inc(*dve_did.up())
        bank.drained = dve_did.now()

        cos1, sin1 = rope[:, 0], rope[:, 1]
        ang, turns, half_a, sin_h = rope[:, 2], rope[:, 3], rope[:, 4], rope[:, 5]
        TWO_PI = 2 * math.pi
        hi = float(np.float32(6.28125))
        mid = float(np.float32(TWO_PI - hi))
        lo_ = float(np.float32(TWO_PI - hi - mid))
        ROUND = float(3 << 22)

        @block.vector
        def _(dve):
            def then(i):
                i.then_inc(*dve_did.up())
                dve.wait_ge(*dve_did.now())
            then(dve.tensor_copy(small[:, 16:16 + TT], posi[:, :]))
            then(dve.tensor_tensor(ang, small[:, 16:16 + TT].unsqueeze(2).broadcast_to([P, TT, ROPE_HALF]),
                                   C("inv").unsqueeze(1).broadcast_to([P, TT, ROPE_HALF]), ALU.mult))
            then(dve.tensor_scalar(turns, ang, 1.0 / TWO_PI, ROUND, ALU.mult, ALU.add))
            then(dve.tensor_scalar(turns, turns, -ROUND, None, ALU.add))
            for part in (hi, mid, lo_):
                then(dve.scalar_tensor_tensor(ang, turns, -part, ang, ALU.mult, ALU.add))
            then(dve.tensor_scalar(ang, ang, math.pi, -math.pi, ALU.min, ALU.max))
            then(dve.tensor_scalar(half_a, ang, 0.5, None, ALU.mult))
            lp = tmp[:, 0, 0:4 * HD].rearrange("p (a b) -> p a b", a=4)
            for m in range(2):
                then(dve.tensor_tensor(tmp[:, 1, m * HD:(m + 1) * HD], lp[:, 2 * m, :], lp[:, 2 * m + 1, :], ALU.mult))
            then(dve.tensor_reduce(small[:, 20:22], tmp[:, 1, 0:2 * HD].rearrange("p (a b) -> p a b", a=2), AX.X,
                                   ALU.add))

        @block.scalar
        def _(act):
            act.wait_ge(*pe_did.now())
            act.wait_ge(*act_did.now())
            act.wait_ge(*dve_did.now())
            act.wait_ge(*pool_did.now())
            act.activation(sin1, ang, ACT.Sin).then_inc(*act_did.up())
            act.activation(sin_h, half_a, ACT.Sin).then_inc(*act_did.up())
            act.activation(small[:, 22:24], small[:, 20:22], ACT.Exp).then_inc(*act_did.up())
        neg_lam = small[:, 25:26]

        @block.vector
        def _(dve):
            dve.wait_ge(*pe_did.now())
            dve.wait_ge(*act_did.now())
            dve.wait_ge(*dve_did.now())
            dve.wait_ge(*pool_did.now())
            dve.tensor_tensor(cos1, sin_h, sin_h, ALU.mult).then_inc(*dve_did.up())
            dve.wait_ge(*dve_did.now())
            dve.tensor_scalar(cos1, cos1, -2.0, 1.0, ALU.mult, ALU.add).then_inc(*dve_did.up())
            dve.tensor_tensor(small[:, 24:25], small[:, 23:24], small[:, 22:23], ALU.subtract).then_inc(*dve_did.up())
            dve.wait_ge(*dve_did.now())
            dve.tensor_scalar(neg_lam, small[:, 24:25], -LAM_INIT, None, ALU.add).then_inc(*dve_did.up())

        def rotate(v, heads, half, cos, sin, second=False):
            x1, x2 = v[:, :, :, 0:half], v[:, :, :, half:2 * half]
            shape = [P, heads, half]
            sz = heads * half
            t = [sq[:, :, m * sz:(m + 1) * sz].rearrange("p t (h w) -> p t h w", h=heads) for m in range(4)]
            before = marks()

            def products(eng, sig, tt, pairs):
                for dst, xx, table in pairs:
                    eng.tensor_tensor(t[dst][:, tt], xx[:, tt], table[:, tt, :].unsqueeze(1).broadcast_to(shape),
                                      ALU.mult).then_inc(*sig.up())

            @block.vector
            def _(dve):
                dve.wait_ge(*before.pe)
                dve.wait_ge(*before.act)
                dve.wait_ge(*before.dve)
                dve.wait_ge(*before.pool)
                for tt in range(TT):
                    products(dve, dve_did, tt, ((0, x1, cos), (1, x2, sin)))

            @block.gpsimd
            def _(pool):
                pool.wait_ge(*before.pe)
                pool.wait_ge(*before.act)
                pool.wait_ge(*before.dve)
                pool.wait_ge(*before.pool)
                for tt in range(TT):
                    products(pool, pool_did, tt, ((2, x2, cos), (3, x1, sin)))
            after = marks()

            @block.vector
            def _(dve):
                dve.wait_ge(*after.pe)
                dve.wait_ge(*after.act)
                dve.wait_ge(*after.dve)
                dve.wait_ge(*after.pool)
                for tt in range(TT):
                    dve.tensor_tensor(x1[:, tt], t[0][:, tt], t[1][:, tt], ALU.subtract).then_inc(*dve_did.up())

            @block.gpsimd
            def _(pool):
                pool.wait_ge(*after.pe)
                pool.wait_ge(*after.act)
                pool.wait_ge(*after.dve)
                pool.wait_ge(*after.pool)
                for tt in range(TT):
                    pool.tensor_tensor(x2[:, tt], t[2][:, tt], t[3][:, tt], ALU.add).then_inc(*pool_did.up())

        def heads_of(c, n, w=HD, buf=z):
            return buf[:, :, c:c + n * w].rearrange("p t (h w) -> p t h w", h=n)

        def log_sigmoid(dst, src, n, t1, t2, from_psum=()):
            @block.scalar
            def _(act):
                act.wait_ge(*pe_did.now())
                act.wait_ge(*act_did.now())
                act.wait_ge(*dve_did.now())
                act.wait_ge(*pool_did.now())
                act.activation(t1, src, ACT.Abs).then_inc(*act_did.up())
                act.wait_ge(*act_did.now())
                act.activation(t2, t1, ACT.Exp, scale=-1.0).then_inc(*act_did.up())
                act.wait_ge(*act_did.now())
                act.activation(t1, t2, ACT.Ln, bias=C("one")).then_inc(*act_did.up())

            @block.vector
            def _(dve):
                dve.wait_ge(*pe_did.now())
                dve.wait_ge(*act_did.now())
                dve.wait_ge(*dve_did.now())
                dve.wait_ge(*pool_did.now())
                dve.scalar_tensor_tensor(dst, src, 0.0, t1, ALU.min, ALU.subtract).then_inc(*dve_did.up())

        causal = C("causal", (TT,))

        def even_mixer(g1):
            pre_norm(x, col_of[("pre", 0, 0)], rs[:, 0:2])
            gemm(hT_of, KD, a["ev_w_in"][0], 0, EV_IN, to_sbuf(lambda tt, c, n: z[:, tt, c:c + n], rs_of(0)))
            lf = small[:, 32:48].rearrange("p (t h) -> p t h", t=TT)

            @block.vector
            def _(dve):
                dve.wait_ge(*pe_did.now())
                dve.wait_ge(*act_did.now())
                dve.wait_ge(*dve_did.now())
                dve.wait_ge(*pool_did.now())
                dve.tensor_tensor(lf, z[:, :, EV["fl"]:EV["fl"] + FOX_H],
                                  small[:, 0:FOX_H].unsqueeze(1).broadcast_to([P, TT, FOX_H]),
                                  ALU.add).then_inc(*dve_did.up())
            log_sigmoid(small[:, 80:96], small[:, 32:48], 16, small[:, 48:64], small[:, 64:80])
            lfs = small[:, 80:96].rearrange("p (t h) -> p t h", t=TT)
            bank = next_bank()

            @block.tensor
            def _(pe):
                pe.wait_ge(*bank.drained)
                pe.wait_ge(*act_did.now())
                pe.wait_ge(*dve_did.now())
                pe.wait_ge(*pool_did.now())
                for tt in range(TT):
                    m = pe.matmul(bank.t[0:FOX_H, 0:T], lfs[:, tt, :], C("upto", (TT,))[:, tt, :],
                                  start=(tt == 0), stop=(tt == TT - 1))
                m.then_inc(*pe_did.up())
            c_neg = hT2[0:FOX_H, 7, :]

            @block.vector
            def _(dve):
                dve.wait_ge(*pe_did.now())
                dve.wait_ge(*act_did.now())
                dve.wait_ge(*dve_did.now())
                dve.wait_ge(*pool_did.now())
                dve.tensor_scalar(c_neg, bank.t[0:FOX_H, 0:T], -(HD ** 0.5), None, ALU.mult).then_inc(*dve_did.up())
            bank.drained = dve_did.now()

            rotate(heads_of(EV["nq"], 10), 10, ROPE_HALF, cos1, sin1)
            rotate(heads_of(EV["ks"], 2), 2, ROPE_HALF, cos1, sin1)
            rotate(heads_of(EV["kw"], 2), 2, ROPE_HALF, cos1, sin1)
            sg = small[:, 96:96 + 2 * 3 * NSA_H // 2]
            sgate = rows[:, 0, 0:TT * 3 * NSA_H].rearrange("p (t h) -> p t h", t=TT)

            @block.scalar
            def _(act):
                act.wait_ge(*pe_did.now())
                act.wait_ge(*act_did.now())
                act.wait_ge(*dve_did.now())
                act.wait_ge(*pool_did.now())
                act.activation(sgate, z[:, :, EV["gl"]:EV["gl"] + 3 * NSA_H], ACT.Sigmoid).then_inc(*act_did.up())
            kd = tmp[:, :, 0:512].rearrange("p t (b c d) -> p t b c d", b=4, c=2)

            @block.gpsimd
            def _(pool):
                pool.wait_ge(*pe_did.now())
                pool.wait_ge(*act_did.now())
                pool.wait_ge(*dve_did.now())
                pool.wait_ge(*pool_did.now())
                for m, name in enumerate(("ks", "kw")):
                    for c in range(2):
                        for tt in range(TT):
                            pool.tensor_copy(kd[:, tt, 2 * m:2 * m + 2, c, :],
                                             heads_of(EV[name], 2)[:, tt]).then_inc(*pool_did.up())
            to_T(4, lambda b, tt: z[:, tt, EV["fq"] + b * P:EV["fq"] + (b + 1) * P], lambda b, n: qT[:, b:b + n, :])
            to_T(4, lambda b, tt: z[:, tt, EV["fk"] + b * P:EV["fk"] + (b + 1) * P], lambda b, n: kT[:, b:b + n, :])
            to_T(4, lambda b, tt: z[:, tt, EV["nq"] + b * P:EV["nq"] + (b + 1) * P],
                 lambda b, n: qT[:, 4 + b:4 + b + n, :])
            to_T(4, lambda b, tt: tmp[:, tt, b * P:(b + 1) * P], lambda b, n: kT[:, 4 + b:4 + b + n, :])

            kcT = hT2[:, 4:6, :].rearrange("p a b -> p (a b)")[:, 0:2 * NC]
            vcmp = hT2[:, 6, 0:2 * HD]
            for m, (name, pos, w1, w2) in enumerate((("kc", "ev_cmp_pos_k", "ev_cmp_w1_k", "ev_cmp_w2_k"),
                                                     ("vc", "ev_cmp_pos_v", "ev_cmp_w1_v", "ev_cmp_w2_v"))):
                win = hT2[:, 2 * m:2 * m + 2, :]
                before = marks()
                for g in range(2):
                    bank = next_bank()

                    @block.tensor
                    def _(pe):
                        pe.wait_ge(*bank.drained)
                        pe.wait_ge(*before.act)
                        pe.wait_ge(*before.dve)
                        pe.wait_ge(*before.pool)
                        for tt in range(TT):
                            src = z[:, tt, EV[name] + g * HD:EV[name] + (g + 1) * HD]
                            pe.matmul(bank.t[0:HD, tt * P:(tt + 1) * P], src, ident, start=True, stop=True)
                        for tt in range(TT):
                            src = z[:, tt, EV[name] + g * HD:EV[name] + (g + 1) * HD]
                            mm = pe.matmul(bank.t[HD:P, 0:T], src, C("shift", (TT,))[:, tt, :],
                                           start=(tt == 0), stop=(tt == TT - 1))
                        mm.then_inc(*pe_did.up())

                    @block.vector
                    def _(dve):
                        dve.wait_ge(*pe_did.now())
                        dve.wait_ge(*before.pe)
                        dve.wait_ge(*before.act)
                        dve.wait_ge(*before.dve)
                        dve.wait_ge(*before.pool)
                        dve.tensor_copy(win[:, g, :], bank.t[:, 0:T]).then_inc(*dve_did.up())
                    bank.drained = dve_did.now()
                NL = CMP_BLOCK // 2
                cw1 = load_weights(lambda v: [(v, a[w1][0].rearrange("(k p) n -> p k n", p=P))], (P, NL, P))
                cw2 = load_weights(lambda v: [(v[:, :, c * HD:(c + 1) * HD], a[w2][0].unsqueeze(1)) for c in range(2)],
                                   (P, 1, 2 * HD))
                bank, bank2 = next_bank(), next_bank()
                pc = col_of[pos] % P

                @block.tensor
                def _(pe):
                    pe.wait_ge(*cw1.landed)
                    pe.wait_ge(*bank.drained)
                    pe.wait_ge(*bank2.drained)
                    pe.wait_ge(*act_did.now())
                    pe.wait_ge(*dve_did.now())
                    pe.wait_ge(*pool_did.now())
                    for l in range(NL):
                        pe.matmul(bank.t[:, 0:2 * NC].rearrange("p (g c) -> p g c", g=2), cw1.view[:, l, :],
                                  win[:, :, 2 * l:2 * l + CMP_STRIDE * (NC - 1) + 1:CMP_STRIDE],
                                  start=(l == 0), stop=(l == NL - 1))
                    for l in range(NL):
                        mm = pe.matmul(bank2.t[:, 0:1], cw1.view[:, l, :], cols[:, 1, pc + l:pc + l + 1],
                                       start=(l == 0), stop=(l == NL - 1))
                    mm.then_inc(*pe_did.up())
                release(cw1)
                hidden = sq[:, 0, m * 32:m * 32 + 2 * NC]
                pos_h = sq[:, 0, 64 + m:65 + m]

                @block.vector
                def _(dve):
                    dve.wait_ge(*pe_did.now())
                    dve.wait_ge(*act_did.now())
                    dve.wait_ge(*dve_did.now())
                    dve.wait_ge(*pool_did.now())
                    dve.tensor_copy(pos_h, bank2.t[:, 0:1]).then_inc(*dve_did.up())
                bank2.drained = dve_did.now()

                @block.scalar
                def _(act):
                    act.wait_ge(*pe_did.now())
                    act.wait_ge(*act_did.now())
                    act.wait_ge(*dve_did.now())
                    act.wait_ge(*pool_did.now())
                    act.activation(hidden, bank.t[:, 0:2 * NC], ACT.Gelu_apprx_tanh, bias=pos_h).then_inc(*act_did.up())
                bank.drained = act_did.now()
                bank3 = next_bank()

                @block.tensor
                def _(pe):
                    pe.wait_ge(*cw2.landed)
                    pe.wait_ge(*bank3.drained)
                    pe.wait_ge(*act_did.now())
                    pe.wait_ge(*dve_did.now())
                    pe.wait_ge(*pool_did.now())
                    if m == 0:
                        mm = pe.matmul(bank3.t[:, 0:2 * NC], cw2.view[:, 0, :], hidden, start=True, stop=True)
                    else:
                        for g in range(2):
                            mm = pe.matmul(bank3.t[0:NC, g * HD:(g + 1) * HD], hidden[:, g * NC:(g + 1) * NC],
                                           cw2.view[:, 0, 0:HD], start=True, stop=True)
                    mm.then_inc(*pe_did.up())
                release(cw2)

                @block.vector
                def _(dve):
                    dve.wait_ge(*pe_did.now())
                    dve.wait_ge(*act_did.now())
                    dve.wait_ge(*dve_did.now())
                    dve.wait_ge(*pool_did.now())
                    if m == 0:
                        dve.tensor_copy(kcT, bank3.t[:, 0:2 * NC]).then_inc(*dve_did.up())
                    else:
                        dve.tensor_copy(vcmp[0:NC, :], bank3.t[0:NC, 0:2 * HD]).then_inc(*dve_did.up())
                bank3.drained = dve_did.now()

            jobs = []
            for h in range(FOX_H):
                b = HD * (h % 2)
                for tt in range(TT):
                    n = (tt + 1) * P
                    jobs.append(dict(
                        qk=[(qT[b:b + HD, h // 2, tt * P:(tt + 1) * P], kT[b:b + HD, h // 2, 0:n]),
                            (ident[0:FOX_H, h:h + 1].broadcast_to([FOX_H, P]), c_neg[:, 0:n])],
                        n=n, bias=causal[:, tt, 0:n], scale=HD ** -0.5, dv=HD,
                        v=[z[:, kb, EV["fv"] + h * HD:EV["fv"] + (h + 1) * HD] for kb in range(tt + 1)],
                        out=o_buf[:, tt, h * HD:(h + 1) * HD]))
            for h in range(NSA_H):
                b, g = HD * (h % 2), h // (NSA_H // 2)
                for tt in range(TT):
                    q = qT[b:b + HD, 4 + h // 2, tt * P:(tt + 1) * P]
                    dst = o_buf[:, tt, 512 + h * HD:512 + (h + 1) * HD]
                    jobs.append(dict(qk=[(q, kcT[b:b + HD, g * NC:(g + 1) * NC])], n=NC,
                                     bias=C("cmp", (TT,))[:, tt, :], scale=HD ** -0.5, dv=HD,
                                     v=[vcmp[0:NC, g * HD:(g + 1) * HD]], out=dst, guard=True,
                                     mul=sgate[:, tt, 3 * h:3 * h + 1]))
                    n = (tt + 1) * P
                    for m, name in enumerate(("vs", "vw")):
                        jobs.append(dict(qk=[(q, kT[b:b + HD, 4 + 2 * m + g, 0:n])], n=n, bias=causal[:, tt, 0:n],
                                         scale=HD ** -0.5, dv=HD,
                                         v=[z[:, kb, EV[name] + g * HD:EV[name] + (g + 1) * HD] for kb in range(tt + 1)],
                                         out=dst, add=True, mul=sgate[:, tt, 3 * h + 1 + m:3 * h + 2 + m]))
            attention(jobs)
            project_o(a["ev_w_out"][0])

        def project_o(w):
            to_T(KD, lambda b, tt: o_buf[:, tt, b * P:(b + 1) * P], lambda b, n: hT[:, b:b + n, :])
            gemm(hT_of, KD, w, 0, D, to_sbuf(lambda tt, c, n: o_buf[:, tt, c:c + n]))

        def diff_mixer():
            pre_norm(x, col_of[("pre", 1, 0)], rs[:, 0:2])
            gemm(hT_of, KD, a["od_w_in"][0], 0, 3 * D, to_sbuf(lambda tt, c, n: z[:, tt, c:c + n], rs_of(0)))
            rotate(heads_of(0, 32), 32, ROPE_HALF, cos1, sin1)
            to_T(KD, lambda b, tt: z[:, tt, b * P:(b + 1) * P], lambda b, n: qT[:, b:b + n, :])
            to_T(KD, lambda b, tt: z[:, tt, D + b * P:D + (b + 1) * P], lambda b, n: kT[:, b:b + n, :])
            jobs = []
            for h in range(DIFF_H):
                for tt in range(TT):
                    n = (tt + 1) * P
                    for m in range(2):
                        b = HD * m
                        jobs.append(dict(qk=[(qT[b:b + HD, h, tt * P:(tt + 1) * P], kT[b:b + HD, h, 0:n])], n=n,
                                         bias=causal[:, tt, 0:n], scale=HD ** -0.5, dv=2 * HD,
                                         v=[z[:, kb, 2 * D + h * P:2 * D + (h + 1) * P] for kb in range(tt + 1)],
                                         out=o_buf[:, tt, h * P:(h + 1) * P], add=(m == 1),
                                         mul=neg_lam if m == 1 else None))
            attention(jobs)
            ov = o_buf[:, :, :].rearrange("p t (h w) -> p t h w", h=DIFF_H)
            rstd_heads(ov, rs[:, 2:2 + TT * DIFF_H], DIFF_H, P)
            scale_heads(ov, ov, rs[:, 2:2 + TT * DIFF_H], DIFF_H)
            c = col_of["subln"] % P
            to_T(KD, lambda b, tt: o_buf[:, tt, b * P:(b + 1) * P], lambda b, n: hT[:, b:b + n, :],
                 scale=lambda b: cols[:, 1, c:c + 1])
            gemm(hT_of, KD, a["od_w_out"][0], 0, D, to_sbuf(lambda tt, c, n: o_buf[:, tt, c:c + n]))

        def memory_attention(l):
            W = MEM_H * HD
            c = col_of[("mem", l)]
            to_T(KD, lambda b, tt: gate[:, tt, b * P:(b + 1) * P], lambda b, n: hT2[:, b:b + n, :],
                 scale=lambda b: cols[:, 0, c + b:c + b + 1])
            m_of = lambda k, tt: hT2[:, k, tt * P:(tt + 1) * P]
            gemm(m_of, KD, a["ca_wk"][l], 0, W, to_sbuf(lambda tt, c, n: z[:, tt, W + c:W + c + n], rs_of(28)))
            gemm(m_of, KD, a["ca_wv"][l], 0, W, to_sbuf(lambda tt, c, n: z[:, tt, 2 * W + c:2 * W + c + n], rs_of(28)))
            pre_norm(x, col_of[("pre", l, 2)], rs[:, 0:2])
            gemm(hT_of, KD, a["ca_wq"][l], 0, W, to_sbuf(lambda tt, c, n: z[:, tt, c:c + n], rs_of(0)))
            to_T(2, lambda b, tt: z[:, tt, b * P:(b + 1) * P], lambda b, n: qT[:, b:b + n, :])
            to_T(2, lambda b, tt: z[:, tt, W + b * P:W + (b + 1) * P], lambda b, n: kT[:, b:b + n, :])
            jobs = []
            for h in range(MEM_H):
                b = HD * (h % 2)
                for tt in range(TT):
                    jobs.append(dict(qk=[(qT[b:b + HD, h // 2, tt * P:(tt + 1) * P], kT[b:b + HD, h // 2, :])], n=T,
                                     bias=None, scale=HD ** -0.5, dv=HD,
                                     v=[z[:, kb, 2 * W + h * HD:2 * W + (h + 1) * HD] for kb in range(TT)],
                                     out=o_buf[:, tt, h * HD:(h + 1) * HD]))
            attention(jobs)
            to_T(2, lambda b, tt: o_buf[:, tt, b * P:(b + 1) * P], lambda b, n: hT[:, b:b + n, :])
            gemm(hT_of, W // P, a["ca_wo"][l], 0, D, to_sbuf(lambda tt, c, n: o_buf[:, tt, c:c + n]))

        rstd_rows(gate, rs[:, 28:30])
        for l in range(DEPTH):
            g = load_gain(a["sandwich_g"][l, 1, :])
            if l % 2 == 0:
                even_mixer(g)
            else:
                diff_mixer()
            post_norm(o_buf, g)
            g = load_gain(a["sandwich_g"][l, 3, :])
            memory_attention(l)
            post_norm(o_buf, g)
            g = load_gain(a["sandwich_g"][l, 5, :])
            pre_norm(x, col_of[("pre", l, 4)], rs[:, 0:2])
            ffn(a["ffn_wg"][l], a["ffn_wu"][l], a["ffn_wd"][l], rs_of(0), finish_to_o)
            post_norm(o_buf, g)

        bias_h = [gain[:, i // 2, (i % 2) * 512:(i % 2 + 1) * 512].rearrange("p (t k) -> p t k", t=TT)
                  for i in range(4)]
        bias_free = [marks() for _ in range(4)]

        def load_bias(l, h):
            s = h % 4
            rows_n = T // GRID_W

            @block.sync
            def _(sp):
                sp.wait_ge(*table_landed.now())
                sp.wait_ge(*bias_free[s].dve)
                for qr in range(rows_n):
                    tt, part = qr // 2, (qr % 2) * GRID_W
                    first = ((l * NA_H + h) * GRID_W * TBL_W
                             + (NA_WIN_R - 1 - qr) * RPB_C + NA_WIN_C - 1 - TBL_LO)
                    src = bass.AP(tensor=table.tensor, offset=first,
                                  ap=[[TBL_W - 1, GRID_W], [RPB_C, rows_n], [1, GRID_W]])
                    sp.dma_start(bias_h[s][part:part + GRID_W, tt, :].rearrange("p (r c) -> p r c", r=rows_n),
                                 src).then_inc(*gain_landed[s].up(16))
            got = gain_landed[s].now()

            @block.gpsimd
            def _(pool):
                pool.wait_ge(*got)
                for tt in range(TT):
                    pool.tensor_tensor(bias_h[s][:, tt, :], bias_h[s][:, tt, :], C("na"), ALU.add).then_inc(
                        *pool_did.up())

        def silu_into(dst, src):
            @block.scalar
            def _(act):
                act.wait_ge(*pe_did.now())
                act.wait_ge(*act_did.now())
                act.wait_ge(*dve_did.now())
                act.wait_ge(*pool_did.now())
                act.activation(dst, src, ACT.Silu).then_inc(*act_did.up())

        def branch(l, i, w, y, scale=None):
            to_T(4, lambda b, tt: y[:, tt, b * P:(b + 1) * P], lambda b, n: hT2[:, b:b + n, :], scale=scale)
            before = marks()


            def gates(tt, c, n, bank, full):
                @block.scalar
                def _(act):
                    act.wait_ge(*full)
                    act.wait_ge(*before.pe)
                    act.wait_ge(*before.act)
                    act.wait_ge(*before.dve)
                    act.wait_ge(*before.pool)
                    act.activation(gate[:, tt, c:c + n], bank.t[:, 0:n], ACT.Sigmoid,
                                   scale=rs[:, tt:tt + 1]).then_inc(*act_did.up())
                bank.drained = act_did.now()
            g0 = ZC["gates"] + i * D
            gemm(hT_of, KD, a["w_in_2"][l], g0, g0 + D, gates)
            after = marks()

            def mix(tt, c, n, bank, full):
                @block.vector
                def _(dve):
                    dve.wait_ge(*full)
                    dve.wait_ge(*after.pe)
                    dve.wait_ge(*after.act)
                    dve.wait_ge(*after.dve)
                    dve.wait_ge(*after.pool)
                    dst = (o_buf if i == 0 else tmp)[:, tt, c:c + n]
                    dve.tensor_tensor(dst, bank.t[:, 0:n], gate[:, tt, c:c + n], ALU.mult).then_inc(*dve_did.up())
                bank.drained = dve_did.now()
                if i > 0:
                    @block.gpsimd
                    def _(pool):
                        pool.wait_ge(*dve_did.now())
                        mixed = o_buf[:, tt, c:c + n]
                        pool.tensor_tensor(mixed, mixed, tmp[:, tt, c:c + n], ALU.add).then_inc(*pool_did.up())
            gemm(lambda k, tt: hT2[:, k, tt * P:(tt + 1) * P], 4, w, 0, D, mix)

        def neighborhood(l):
            for h in range(4):
                load_bias(l, h)
            for name, c, dstT in (("na_q_norm_2", ZC["naq"], qT), ("na_k_norm_2", ZC["nak"], kT)):
                v = heads_of(c, NA_H)
                r = rs[:, 2:2 + TT * NA_H]
                rstd_heads(v, r, NA_H, HD)
                scale_heads(v, v, r, NA_H)
                gc = col_of[(name, l)] % P
                to_T(4, lambda b, tt: z[:, tt, c + b * P:c + (b + 1) * P], lambda b, n: dstT[:, b:b + n, :],
                     scale=lambda b: cols[:, 1, gc:gc + 1])
            y = sq[:, :, 0:512]
            for half in range(2):
                jobs = []
                for h in range(4 * half, 4 * half + 4):
                    b = HD * (h % 2)
                    for tt in range(TT):
                        jobs.append(dict(qk=[(qT[b:b + HD, h // 2, tt * P:(tt + 1) * P], kT[b:b + HD, h // 2, :])],
                                         n=T, bias=bias_h[h % 4][:, tt, :], scale=HD ** -0.5, dv=HD,
                                         v=[z[:, kb, ZC["nav"] + h * HD:ZC["nav"] + (h + 1) * HD] for kb in range(TT)],
                                         out=y[:, tt, h * HD:(h + 1) * HD]))
                attention(jobs)
                for s in range(4):
                    bias_free[s] = marks()
                if half == 0:
                    for h in range(4, 8):
                        load_bias(l, h)
            branch(l, 0, a["w_br_na_2"][l], y)

        def gated_linear(l):
            NP2 = GLA_H // 2
            NCH = T // GLA_CHUNK
            dirs = (("gla_gf_up_2", "gla_gf_bias_2", ZC["gfl"]), ("gla_gb_up_2", "gla_gb_bias_2", ZC["gbl"]))
            lowT = kT[0:GLA_RANK + 1, 6:8, :]
            before = marks()

            @block.sync
            def _(sp):
                sp.wait_ge(*before.pe)
                sp.wait_ge(*before.act)
                sp.wait_ge(*before.dve)
                sp.wait_ge(*before.pool)
                for d, (w, b, _) in enumerate(dirs):
                    sp.dma_start(up[0:GLA_RANK, d, :], a[w][l]).then_inc(*misc_landed.up(16))
                    sp.dma_start(up[GLA_RANK:GLA_RANK + 1, d, :], a[b][l:l + 1, :]).then_inc(*misc_landed.up(16))

            @block.gpsimd
            def _(pool):
                pool.wait_ge(*before.pe)
                pool.wait_ge(*before.act)
                pool.wait_ge(*before.dve)
                pool.wait_ge(*before.pool)
                pool.memset(lowT, 1.0).then_inc(*pool_did.up())
            to_T(2, lambda d, tt: z[:, tt, dirs[d][2]:dirs[d][2] + GLA_RANK],
                 lambda d, n: kT[0:GLA_RANK, 6 + d:6 + d + n, :], width=GLA_RANK)
            got = misc_landed.now()
            g = tmp[:, :, 0:512]
            b_sum = sq[:, :, 0:512]
            to_end = sq[:, :, 512:1024]
            for tt in range(TT):
                bank = next_bank()

                @block.tensor
                def _(pe):
                    pe.wait_ge(*got)
                    pe.wait_ge(*bank.drained)
                    pe.wait_ge(*act_did.now())
                    pe.wait_ge(*dve_did.now())
                    pe.wait_ge(*pool_did.now())
                    for d in range(2):
                        m = pe.matmul(bank.t[:, d * T:(d + 1) * T], lowT[:, d, tt * P:(tt + 1) * P], up[:, d, :],
                                      start=True, stop=True)
                    m.then_inc(*pe_did.up())
                log_sigmoid(g[:, tt, :], bank.t[:, :], 512, b_sum[:, tt, :], to_end[:, tt, :])
                bank.drained = dve_did.now()
            before = marks()
            e_pos, e_neg, e_end = qT[:, 0:4, :], qT[:, 4:8, :], kT[:, 0:4, :]
            for tt in range(TT):
                for d in range(2):
                    bank = next_bank()

                    @block.tensor
                    def _(pe):
                        pe.wait_ge(*bank.drained)
                        pe.wait_ge(*before.act)
                        pe.wait_ge(*before.dve)
                        pe.wait_ge(*before.pool)
                        gd = g[:, tt, d * T:(d + 1) * T]
                        pe.matmul(bank.t[:, 0:T], C("tri_f" if d == 0 else "tri_b"), gd, start=True, stop=True)
                        m = pe.matmul(bank.t[:, T:2 * T], C("chunk_all"), gd, start=True, stop=True)
                        m.then_inc(*pe_did.up())
                    full = pe_did.now()
                    bs = b_sum[:, tt, d * T:(d + 1) * T]
                    te = to_end[:, tt, d * T:(d + 1) * T]
                    i = tt * 2 + d

                    @block.vector
                    def _(dve):
                        dve.wait_ge(*full)
                        dve.wait_ge(*before.pe)
                        dve.wait_ge(*before.act)
                        dve.wait_ge(*before.dve)
                        dve.wait_ge(*before.pool)
                        dve.tensor_copy(bs, bank.t[:, 0:T]).then_inc(*dve_did.up())
                        dve.wait_ge(*dve_did.now())
                        dve.tensor_tensor(te, bank.t[:, T:2 * T], bs, ALU.subtract).then_inc(*dve_did.up())

                    @block.scalar
                    def _(act):
                        act.wait_ge(*dve_did.now())
                        act.wait_ge(*before.pe)
                        act.wait_ge(*before.act)
                        act.wait_ge(*before.dve)
                        act.wait_ge(*before.pool)
                        act.activation(e_pos[:, i, :], bs, ACT.Exp).then_inc(*act_did.up())
                        act.activation(e_neg[:, i, :], bs, ACT.Exp, scale=-1.0).then_inc(*act_did.up())
                        act.activation(e_end[:, i, :], te, ACT.Exp).then_inc(*act_did.up())
                    bank.drained = dve_did.now()
            dec = stat[:, 0:16]
            bank = next_bank()

            @block.tensor
            def _(pe):
                pe.wait_ge(*bank.drained)
                pe.wait_ge(*before.act)
                pe.wait_ge(*before.dve)
                pe.wait_ge(*before.pool)
                for d in range(2):
                    for pr in range(NP2):
                        for tt in range(TT):
                            c = (d * NP2 + pr) * NCH + tt * 2
                            m = pe.matmul(bank.t[:, c:c + 2], g[:, tt, d * T + pr * P:d * T + (pr + 1) * P],
                                          C("chunk_of"), start=True, stop=True)
                m.then_inc(*pe_did.up())

            @block.scalar
            def _(act):
                act.wait_ge(*pe_did.now())
                act.wait_ge(*act_did.now())
                act.wait_ge(*dve_did.now())
                act.wait_ge(*pool_did.now())
                act.activation(dec, bank.t[:, 0:16], ACT.Exp).then_inc(*act_did.up())
            bank.drained = act_did.now()
            qe, ke, kend = tmp[:, :, 0:512], tmp[:, :, 512:1024], hT2[:, 0:4, :]
            before = marks()
            zq = lambda tt: z[:, tt, ZC["gq"]:ZC["gq"] + T]
            zk = lambda tt: z[:, tt, ZC["gk"]:ZC["gk"] + T]

            @block.vector
            def _(dve):
                dve.wait_ge(*before.pe)
                dve.wait_ge(*before.act)
                dve.wait_ge(*before.dve)
                dve.wait_ge(*before.pool)
                for tt in range(TT):
                    for d in range(2):
                        i = tt * 2 + d
                        dve.scalar_tensor_tensor(qe[:, tt, d * T:(d + 1) * T], zq(tt), GLA_DK ** -0.5, e_pos[:, i, :],
                                                 ALU.mult, ALU.mult).then_inc(*dve_did.up())
                        dve.tensor_tensor(ke[:, tt, d * T:(d + 1) * T], zk(tt), e_neg[:, i, :],
                                          ALU.mult).then_inc(*dve_did.up())

            @block.gpsimd
            def _(pool):
                pool.wait_ge(*before.pe)
                pool.wait_ge(*before.act)
                pool.wait_ge(*before.dve)
                pool.wait_ge(*before.pool)
                for tt in range(TT):
                    for d in range(2):
                        i = tt * 2 + d
                        pool.tensor_tensor(kend[:, i, :], zk(tt), e_end[:, i, :], ALU.mult).then_inc(*pool_did.up())
            qeT, keT = qT[:, 0:4, :], qT[:, 4:8, :]
            to_T(4, lambda b, tt: qe[:, tt, b * P:(b + 1) * P], lambda b, n: qT[:, b:b + n, :])
            to_T(4, lambda b, tt: ke[:, tt, b * P:(b + 1) * P], lambda b, n: qT[:, 4 + b:4 + b + n, :])
            aT = sq[:, :, :].rearrange("p t (d n) -> p t d n", d=2)

            @block.gpsimd
            def _(pool):
                pool.wait_ge(*pe_did.now())
                pool.wait_ge(*act_did.now())
                pool.wait_ge(*dve_did.now())
                pool.wait_ge(*pool_did.now())
                for tt in range(TT):
                    pool.memset(sq[:, tt, :], 0.0).then_inc(*pool_did.up())
            before = marks()
            for d in range(2):
                for par in range(2):
                    bank = next_bank()
                    r0 = par * HD

                    @block.tensor
                    def _(pe):
                        pe.wait_ge(*bank.drained)
                        pe.wait_ge(*before.act)
                        pe.wait_ge(*before.dve)
                        pe.wait_ge(*before.pool)
                        for tt in range(TT):
                            for pr in range(NP2):
                                ts_ = slice(tt * P, (tt + 1) * P)
                                c = (tt * NP2 + pr) * P
                                m = pe.matmul(bank.t[:, c:c + P], keT[r0:r0 + HD, d * 2 + pr, ts_],
                                              qeT[r0:r0 + HD, d * 2 + pr, ts_], start=True, stop=True)
                        m.then_inc(*pe_did.up())

                    @block.vector
                    def _(dve):
                        dve.wait_ge(*pe_did.now())
                        dve.wait_ge(*before.pe)
                        dve.wait_ge(*before.act)
                        dve.wait_ge(*before.dve)
                        dve.wait_ge(*before.pool)
                        keep = C("tri_f" if d == 0 else "strict_b").bitcast(I32)
                        for tt in range(TT):
                            dve.copy_predicated(
                                aT[:, tt, d, :].rearrange("p (r q n) -> p r q n", r=NP2, q=2)[:, :, par, :],
                                keep.unsqueeze(1).broadcast_to([P, NP2, P]),
                                bank.t[:, tt * T:(tt + 1) * T].rearrange("p (r n) -> p r n", r=NP2)).then_inc(
                                *dve_did.up())
                    bank.drained = dve_did.now()
            state = {}
            states = [kT[:, 2 * i:2 * i + 2, :] for i in range(4)] + [hT2[:, 4 + 2 * i:6 + 2 * i, :] for i in range(2)]

            @block.gpsimd
            def _(pool):
                pool.wait_ge(*pe_did.now())
                pool.wait_ge(*act_did.now())
                pool.wait_ge(*dve_did.now())
                pool.wait_ge(*pool_did.now())
                pool.memset(kT[:, :, :], 0.0).then_inc(*pool_did.up())
                pool.memset(hT2[:, 4:8, :], 0.0).then_inc(*pool_did.up())
            order = [(0, 0, 1, 0), (0, 1, 2, 1), (0, 2, 3, 2), (1, 3, 2, 3), (1, 2, 1, 4), (1, 1, 0, 5)]
            before = marks()
            for d, c, nxt, slot in order:
                tt, b0 = c // 2, GLA_CHUNK * (c % 2)
                bank = next_bank()

                @block.tensor
                def _(pe):
                    pe.wait_ge(*bank.drained)
                    pe.wait_ge(*before.act)
                    pe.wait_ge(*before.dve)
                    pe.wait_ge(*before.pool)
                    for pr in range(NP2):
                        m = pe.matmul(bank.t[:, pr * T:(pr + 1) * T],
                                      kend[b0:b0 + GLA_CHUNK, tt * 2 + d, pr * P:(pr + 1) * P],
                                      z[b0:b0 + GLA_CHUNK, tt, ZC["gv"] + pr * T:ZC["gv"] + (pr + 1) * T],
                                      start=True, stop=True)
                    m.then_inc(*pe_did.up())

                @block.vector
                def _(dve):
                    dve.wait_ge(*pe_did.now())
                    dve.wait_ge(*dve_did.now())
                    dve.wait_ge(*before.pe)
                    dve.wait_ge(*before.act)
                    dve.wait_ge(*before.dve)
                    dve.wait_ge(*before.pool)
                    for par in range(2):
                        ps = slice(par * HD, (par + 1) * HD)
                        for pr in range(NP2):
                            src = bank.t[ps, pr * T + par * P:pr * T + (par + 1) * P]
                            at = (ps, pr, slice(par * P, (par + 1) * P))
                            if (d, c) not in state:
                                dve.tensor_copy(states[slot][at], src).then_inc(*dve_did.up())
                            else:
                                col = (d * NP2 + pr) * NCH + c
                                dve.scalar_tensor_tensor(states[slot][at], states[state[(d, c)]][at],
                                                         dec[ps, col:col + 1], src, ALU.mult,
                                                         ALU.add).then_inc(*dve_did.up())
                bank.drained = dve_did.now()
                state[(d, nxt)] = slot
            before = marks()
            og = tmp[:, :, 0:512]
            for tt in range(TT):
                bank = next_bank()

                @block.tensor
                def _(pe):
                    pe.wait_ge(*bank.drained)
                    pe.wait_ge(*before.act)
                    pe.wait_ge(*before.dve)
                    pe.wait_ge(*before.pool)
                    for h in range(GLA_H):
                        vh = z[:, tt, ZC["gv"] + h * P:ZC["gv"] + (h + 1) * P]
                        for d in range(2):
                            m = pe.matmul(bank.t[:, h * P:(h + 1) * P], aT[:, tt, d, h * P:(h + 1) * P], vh,
                                          start=(h == 0 and d == 0), stop=False, skip_group_check=True)
                    for pr in range(NP2):
                        inter = [(d, c) for c in (2 * tt, 2 * tt + 1) for d in range(2) if (d, c) in state]
                        for n, (d, c) in enumerate(inter):
                            r0 = GLA_CHUNK * (c % 2)
                            m = pe.matmul(bank.t[r0:r0 + GLA_CHUNK, pr * T:(pr + 1) * T],
                                          qeT[:, d * 2 + pr, c * GLA_CHUNK:(c + 1) * GLA_CHUNK],
                                          states[state[(d, c)]][:, pr, :],
                                          start=False, stop=(n == len(inter) - 1), skip_group_check=True)
                    m.then_inc(*pe_did.up())

                @block.vector
                def _(dve):
                    dve.wait_ge(*pe_did.now())
                    dve.wait_ge(*before.pe)
                    dve.wait_ge(*before.act)
                    dve.wait_ge(*before.dve)
                    dve.wait_ge(*before.pool)
                    dve.tensor_copy(og[:, tt, :], bank.t[:, :]).then_inc(*dve_did.up())
                bank.drained = dve_did.now()
            ov = og.rearrange("p t (h w) -> p t h w", h=GLA_H)
            r = rs[:, 2:2 + TT * GLA_H]
            rstd_heads(ov, r, GLA_H, GLA_DV)
            scale_heads(ov, ov, r, GLA_H)
            gr = z[:, :, ZC["gr"]:ZC["gr"] + 512]
            silu_into(gr, gr)

            @block.vector
            def _(dve):
                dve.wait_ge(*pe_did.now())
                dve.wait_ge(*act_did.now())
                dve.wait_ge(*dve_did.now())
                dve.wait_ge(*pool_did.now())
                dve.tensor_tensor(og, og, gr, ALU.mult).then_inc(*dve_did.up())
            gc = col_of[("gla_out", l)] % P
            branch(l, 1, a["w_br_gla_2"][l], og, scale=lambda b: cols[:, 1, gc:gc + 1])

        def latent(l):
            q = z[:, :, 0:MLA_H * MLA_QK]
            kv = z[:, :, ZC["gq"]:ZC["gq"] + MLA_H * (MLA_NOPE + MLA_V)]
            for name, c, w, width, dst in (("cq", ZC["cq"], "mla_w_uq_2", MLA_H * MLA_QK, q),
                                           ("ckv", ZC["ckv"], "mla_w_ukv_2", MLA_H * (MLA_NOPE + MLA_V), kv)):
                v = z[:, :, c:c + 2 * P].unsqueeze(2)
                rstd_heads(v, rs[:, 2:4], 1, 2 * P)
                gc = col_of[(name, l)] % P
                to_T(2, lambda b, tt: z[:, tt, c + b * P:c + (b + 1) * P], lambda b, n: hT2[:, b:b + n, :],
                     scale=lambda b: cols[:, 1, gc + b:gc + b + 1])
                gemm(lambda k, tt: hT2[:, k, tt * P:(tt + 1) * P], 2, a[w][l], 0, width,
                     to_sbuf(lambda tt, c_, n: dst[:, tt, c_:c_ + n], rs_of(2)))
            qv = q.rearrange("p t (h w) -> p t h w", h=MLA_H)
            kvv = kv.rearrange("p t (h w) -> p t h w", h=MLA_H)
            kf = tmp[:, :, 0:MLA_H * MLA_QK]
            kfv = kf.rearrange("p t (h w) -> p t h w", h=MLA_H)
            before = marks()

            @block.gpsimd
            def _(pool):
                pool.wait_ge(*before.pe)
                pool.wait_ge(*before.act)
                pool.wait_ge(*before.dve)
                pool.wait_ge(*before.pool)
                for tt in range(TT):
                    pool.tensor_copy(kfv[:, tt, :, 0:MLA_NOPE], kvv[:, tt, :, 0:MLA_NOPE]).then_inc(*pool_did.up())
                    pool.tensor_copy(kfv[:, tt, :, MLA_NOPE:MLA_QK],
                                     z[:, tt, ZC["kr"]:ZC["kr"] + MLA_ROPE].unsqueeze(1).broadcast_to(
                                         [P, MLA_H, MLA_ROPE])).then_inc(*pool_did.up())
            for m, (v, name, buf, dstT) in enumerate(((qv, "mla_q", q, qT), (kfv, "mla_k", kf, kT))):
                r = rs[:, 2:2 + TT * MLA_H]
                rstd_heads(v, r, MLA_H, MLA_QK)
                scale_heads(v, v, r, MLA_H)
                rot = v[:, :, :, MLA_NOPE:MLA_QK]

                @block.vector
                def _(dve):
                    dve.wait_ge(*pe_did.now())
                    dve.wait_ge(*act_did.now())
                    dve.wait_ge(*dve_did.now())
                    dve.wait_ge(*pool_did.now())
                    for tt in range(TT):
                        dve.tensor_tensor(rot[:, tt], rot[:, tt],
                                          rgain[:, l * 2 + m, :].unsqueeze(1).broadcast_to([P, MLA_H, MLA_ROPE]),
                                          ALU.mult).then_inc(*dve_did.up())
                rotate(rot, MLA_H, MLA_ROPE // 2, C("cos2", (TT,)), C("sin2", (TT,)))
                gc = col_of[(name, l)] % P
                to_T(MLA_H, lambda h, tt: v[:, tt, h, 0:MLA_NOPE], lambda b, n: dstT[:, b:b + n, :],
                     scale=lambda b: cols[:, 1, gc:gc + 1])
                to_T(MLA_H, lambda h, tt: v[:, tt, h, MLA_NOPE:MLA_QK], lambda b, n: dstT[0:MLA_ROPE, 4 + b:4 + b + n, :],
                     width=MLA_ROPE)
            y = sq[:, :, 0:512]
            jobs = []
            for h in range(MLA_H):
                for tt in range(TT):
                    ts_ = slice(tt * P, (tt + 1) * P)
                    jobs.append(dict(qk=[(qT[:, h, ts_], kT[:, h, :]),
                                         (qT[0:MLA_ROPE, 4 + h, ts_], kT[0:MLA_ROPE, 4 + h, :])],
                                     n=T, bias=None, scale=MLA_QK ** -0.5, dv=MLA_V,
                                     v=[kvv[:, kb, h, MLA_NOPE:MLA_NOPE + MLA_V] for kb in range(TT)],
                                     out=y[:, tt, h * P:(h + 1) * P]))
            attention(jobs)
            branch(l, 2, a["w_br_mla_2"][l], y)

        def add_x(tt, c, n, bank, full):
            @block.vector
            def _(dve):
                dve.wait_ge(*full)
                dve.wait_ge(*pe_did.now())
                dve.wait_ge(*act_did.now())
                dve.wait_ge(*dve_did.now())
                dve.wait_ge(*pool_did.now())
                xs = x[:, tt, c:c + n]
                dve.tensor_tensor(xs, xs, bank.t[:, 0:n], ALU.add).then_inc(*dve_did.up())
            bank.drained = dve_did.now()

        for l in range(DEPTH):
            pre_norm(x, col_of[("ffn1_norm_2", l)], rs[:, 0:2])
            ffn(a["ffn1_w1_2"][l], a["ffn1_w3_2"][l], a["ffn1_w2_2"][l], rs_of(0), add_half)
            pre_norm(x, col_of[("mix_norm_2", l)], rs[:, 0:2])
            gemm(hT_of, KD, a["w_in_2"][l], 0, ZC["gates"], to_sbuf(lambda tt, c, n: z[:, tt, c:c + n], rs_of(0)))
            neighborhood(l)
            gated_linear(l)
            latent(l)
            to_T(KD, lambda b, tt: o_buf[:, tt, b * P:(b + 1) * P], lambda b, n: hT[:, b:b + n, :])
            gemm(hT_of, KD, a["w_out_2"][l], 0, D, add_x)
            pre_norm(x, col_of[("ffn2_norm_2", l)], rs[:, 0:2])
            ffn(a["ffn2_w1_2"][l], a["ffn2_w3_2"][l], a["ffn2_w2_2"][l], rs_of(0), add_half)

        @block.sync
        def _(sp):
            sp.wait_ge(*pe_did.now())
            sp.wait_ge(*act_did.now())
            sp.wait_ge(*dve_did.now())
            sp.wait_ge(*pool_did.now())
            sp.dma_start(out[0].rearrange("(t p) d -> p t d", p=P), x[:, :, :]).then_inc(*out_landed.up(16))
            sp.wait_ge(*out_landed.now())


def kernel(**inputs):
    from concourse import bacc
    from concourse.bass_utils import run_bass_kernel_spmd

    nc = bacc.Bacc("TRN2", target_bir_lowering=False, num_devices=1)
    arrays, aps = {}, {}
    const, where = constants()
    for name, value in {**inputs, "const": const}.items():
        v = np.ascontiguousarray(value)
        arrays[f"in_{name}"] = v
        aps[name] = nc.dram_tensor(f"in_{name}", v.shape, mybir.dt.from_np(v.dtype), kind="ExternalInput").ap()
    out = nc.dram_tensor("out_0", (1, T, D), F32, kind="ExternalOutput").ap()
    program(nc, aps, where, out)
    r = run_bass_kernel_spmd(nc, [arrays], core_ids=[0])
    return r.results[0]["out_0"]
```

```python
import math
from collections import namedtuple
from contextlib import ExitStack

import numpy as np
import concourse.bass as bass
from concourse import mybir

F32 = mybir.dt.float32
F32R = mybir.dt.float32r
I32 = mybir.dt.int32
ALU = mybir.AluOpType
ACT = mybir.ActivationFunctionType
AX = mybir.AxisListType

P = 128
T = 256
TT = T // P
D = 1024
KD = D // P
HD = 64
EPS = 1e-6
NEG = -1e30

ROPE_HALF = HD // 8
ROPE_THETA = 500000.0
FOX_H = 8
NSA_H = 8
CMP_BLOCK, CMP_STRIDE = 32, 16
NC = (T - CMP_BLOCK) // CMP_STRIDE + 1
D_FF = 2816
MEM_H = 4
DIFF_H = 8
LAM_INIT = 0.8 - 0.6 * math.exp(-0.3 * 1)
DEPTH = 2
EV, at = {}, 0
for _name, _w in (("fq", 512), ("fk", 512), ("fv", 512), ("fl", 8), ("nq", 512), ("kc", 128), ("vc", 128),
                  ("ks", 128), ("vs", 128), ("kw", 128), ("vw", 128), ("gl", 24)):
    EV[_name] = at
    at += _w
EV_IN = at

GRID_W = 64
NA_H = 8
NA_WIN_R, NA_WIN_C = 8, 16
RPB_R, RPB_C = 2 * NA_WIN_R - 1, 2 * NA_WIN_C - 1
GLA_H, GLA_DK, GLA_DV, GLA_CHUNK, GLA_RANK, GLA_TAU = 4, 64, 128, 64, 16, 16.0
MLA_H, MLA_NOPE, MLA_ROPE, MLA_V = 4, 128, 64, 128
MLA_QK = MLA_NOPE + MLA_ROPE
ROPE_THETA_2 = 10000.0
ZC, at = {}, 0
for _name, _w in (("naq", 512), ("nak", 512), ("nav", 512), ("gq", 256), ("gk", 256), ("gv", 512), ("gr", 512),
                  ("gfl", 16), ("gbl", 16), ("cq", 256), ("ckv", 256), ("kr", 64), ("gates", 3 * D)):
    ZC[_name] = at
    at += _w

TBL_LO = (NA_WIN_R - T // GRID_W) * RPB_C + NA_WIN_C - 1 - (GRID_W - 1)
TBL_HI = (NA_WIN_R - 2 + T // GRID_W) * RPB_C + NA_WIN_C - 1 + GRID_W
TBL_W = TBL_HI - TBL_LO

SLOT = 2048
RAW_SLOTS = 6
HI_SLOTS = 3
FF_CHUNK = 256


def constants():
    p = np.arange(P)
    t = np.arange(T)
    parts = {}
    parts["ident"] = np.eye(P)
    tok = np.arange(TT)[:, None] * P + p[None, :]
    parts["causal"] = np.where(t[None, None, :] <= tok.T[:, :, None], 0.0, NEG)
    cmp_end = np.arange(NC) * CMP_STRIDE + CMP_BLOCK - 1
    parts["cmp"] = np.where(cmp_end[None, None, :] <= tok.T[:, :, None], 0.0, NEG)
    qc = p % GRID_W
    kc = t % GRID_W
    c0 = np.clip(qc - NA_WIN_C // 2, 0, GRID_W - NA_WIN_C)
    parts["na"] = np.where((kc[None] >= c0[:, None]) & (kc[None] < c0[:, None] + NA_WIN_C), 0.0, NEG)
    early = {}
    early["upto"] = (tok.T[:, :, None] <= t[None, None, :]) * 1.0
    early["shift"] = (tok.T[:, :, None] == t[None, None, :] + 1) * 1.0
    same = (p[:, None] // GLA_CHUNK) == (p[None, :] // GLA_CHUNK)
    parts["tri_f"] = (same & (p[:, None] <= p[None, :])) / GLA_TAU
    parts["tri_b"] = (same & (p[:, None] >= p[None, :])) / GLA_TAU
    parts["strict_b"] = (same & (p[:, None] > p[None, :])) * 1.0
    parts["chunk_all"] = same / GLA_TAU
    parts["chunk_of"] = ((p[:, None] // GLA_CHUNK) == np.arange(P // GLA_CHUNK)[None, :]) / GLA_TAU
    half = MLA_ROPE // 2
    inv2 = (np.float32(ROPE_THETA_2) ** (-np.arange(half, dtype=np.float32) / np.float32(half))).astype(np.float32)
    ang = tok.T[:, :, None].astype(np.float32) * inv2
    parts["cos2"] = np.cos(ang.astype(np.float64))
    parts["sin2"] = np.sin(ang.astype(np.float64))
    inv = np.float32(ROPE_THETA) ** (-np.arange(0, 2 * ROPE_HALF, 2, dtype=np.float32) / np.float32(2 * ROPE_HALF))
    parts["inv"] = np.broadcast_to(inv[None, :], (P, ROPE_HALF))
    parts["minus_half"] = np.full((P, 16), -0.5)
    parts["one"] = np.ones((P, 1))
    where, arrays = {}, []
    for group in (parts, early):
        cols, c = [], 0
        for name, a in group.items():
            a = np.ascontiguousarray(a, dtype=np.float32).reshape(P, -1)
            where[name] = (c, a.shape[1])
            cols.append(a)
            c += a.shape[1]
        arrays.append(np.concatenate(cols, axis=1))
    return (*arrays, where)




class Signal:

    def __init__(self, sem):
        self.sem, self.n = sem, 0

    def up(self, k=1):
        self.n += k
        return self.sem, k

    def now(self):
        return self.sem, self.n


Marks = namedtuple("Marks", "pe act dve pool")


class Bank:

    def __init__(self, tensor, start):
        self.t, self.drained = tensor, start


class Unit:

    def __init__(self, shape, parts, split=True):
        self.shape, self.parts, self.split = shape, parts, split
        self.used = self.landed = None


def gemm_units(W, lo, hi):
    units = []
    nk = W.shape[0] // P
    for c in range(lo, hi, 512):
        n = min(512, hi - c)
        kk = nk
        while kk * n > SLOT:
            kk //= 2
        for k0 in range(0, nk, kk):
            src = W[k0 * P:(k0 + kk) * P, c:c + n].rearrange("(k p) n -> p k n", p=P)
            units.append(Unit((kk, n), lambda v, src=src: [(v, src)]))
    return units


def ffn_units(wg, wu, wd):
    units = []
    chunks = wd.shape[0] // FF_CHUNK
    for c in range(chunks + 1):
        if c < chunks:
            for k0 in range(0, KD, KD // 2):
                src = [w[k0 * P:(k0 + KD // 2) * P, c * FF_CHUNK:(c + 1) * FF_CHUNK].rearrange(
                    "(k p) n -> p k n", p=P) for w in (wg, wu)]
                units.append(Unit((KD // 2, 2 * FF_CHUNK), lambda v, src=src: [
                    (v[:, :, 0:FF_CHUNK], src[0]), (v[:, :, FF_CHUNK:2 * FF_CHUNK], src[1])]))
        if c >= 1:
            src = wd[(c - 1) * FF_CHUNK:c * FF_CHUNK, :].rearrange("(k p) n -> p k n", p=P)
            units.append(Unit((FF_CHUNK // P, D), lambda v, src=src: [(v, src)]))
    return units


def weight_stream(a):
    units = []
    for l in range(DEPTH):
        if l % 2 == 0:
            units += gemm_units(a["ev_w_in"][0], 0, EV_IN)
            for m in "kv":
                w1 = a[f"ev_cmp_w1_{m}"][0].rearrange("(k p) n -> p k n", p=P)
                w2 = a[f"ev_cmp_w2_{m}"][0].unsqueeze(1)
                units.append(Unit((CMP_BLOCK // 2, P), lambda v, w1=w1: [(v, w1)], split=False))
                units.append(Unit((1, 2 * HD), lambda v, w2=w2: [(v[:, :, 0:HD], w2), (v[:, :, HD:2 * HD], w2)],
                                  split=False))
            units += gemm_units(a["ev_w_out"][0], 0, D)
        else:
            units += gemm_units(a["od_w_in"][0], 0, 3 * D)
            units += gemm_units(a["od_w_out"][0], 0, D)
        for name in ("ca_wk", "ca_wv", "ca_wq", "ca_wo"):
            units += gemm_units(a[name][l], 0, a[name].shape[2])
        units += ffn_units(a["ffn_wg"][l], a["ffn_wu"][l], a["ffn_wd"][l])
    for l in range(DEPTH):
        w_in = a["w_in_2"][l]
        gates = [gemm_units(w_in, ZC["gates"] + i * D, ZC["gates"] + (i + 1) * D) for i in range(3)]
        units += ffn_units(a["ffn1_w1_2"][l], a["ffn1_w3_2"][l], a["ffn1_w2_2"][l])
        units += gemm_units(w_in, 0, ZC["gates"])
        units += gates[0] + gemm_units(a["w_br_na_2"][l], 0, D)
        units += gates[1] + gemm_units(a["w_br_gla_2"][l], 0, D)
        units += gemm_units(a["mla_w_uq_2"][l], 0, MLA_H * MLA_QK)
        units += gemm_units(a["mla_w_ukv_2"][l], 0, MLA_H * (MLA_NOPE + MLA_V))
        units += gates[2] + gemm_units(a["w_br_mla_2"][l], 0, D)
        units += gemm_units(a["w_out_2"][l], 0, D)
        units += ffn_units(a["ffn2_w1_2"][l], a["ffn2_w3_2"][l], a["ffn2_w2_2"][l])
    return units


def program(nc, a, const_where, out):
    ctx = ExitStack()
    with ctx:
        place = {"next": -(-nc.sbuf_base // 32) * 32}

        def sb(name, shape, dt=F32, over=None):
            size = -(-int(np.prod(shape[1:])) * 4 // 32) * 32
            if over is None:
                place[name] = place["next"]
                place["next"] += size
            else:
                place[name] = place[over[0]] + 4 * over[1]
            return nc.alloc_sbuf_tensor_at(name, shape, dt, offset=place[name])

        def signal(name):
            return Signal(ctx.enter_context(nc.semaphore(name)))

        CONST_N = a["const"].shape[1]
        const = sb("const", [P, CONST_N])
        x = sb("x", [P, TT, D])
        h_hi = sb("h_hi", [P, KD, T], F32R)
        h_lo = sb("h_lo", [P, KD, T], F32R)
        hT2 = sb("hT2", [P, KD, T])
        o_buf = sb("o_buf", [P, TT, D])
        early = sb("early", [P, a["early"].shape[1]], over=("o_buf", 0))
        sq = sb("sq", [P, TT, D])
        z = sb("z", [P, TT, ZC["gates"]])
        FF_N = 2 * TT * FF_CHUNK
        ff_hid = sb("ff_hid", [P, 2, TT, FF_CHUNK], over=("z", 0))
        ff_silu = sb("ff_silu", [P, 2, TT, FF_CHUNK], over=("z", FF_N))
        ff_hi = sb("ff_hi", [P, 2, FF_CHUNK // P, T], F32R, over=("z", 2 * FF_N))
        ff_lo = sb("ff_lo", [P, 2, FF_CHUNK // P, T], F32R, over=("z", 3 * FF_N))
        gate = sb("gate", [P, TT, D])
        qT = sb("qT", [P, KD, T])
        kT = sb("kT", [P, KD, T])
        h2_hi = sb("h2_hi", [P, KD, T], F32R, over=("qT", 0))
        h2_lo = sb("h2_lo", [P, KD, T], F32R, over=("kT", 0))
        tmp = sb("tmp", [P, TT, D])
        raw = sb("raw", [P, RAW_SLOTS, SLOT])
        w_lo = sb("w_lo", [P, RAW_SLOTS, SLOT], F32R, over=("raw", 0))
        w_hi = sb("w_hi", [P, HI_SLOTS, SLOT], F32R)
        gain = sb("gain", [P, TT, D])
        smask = sb("smask", [P, 2, T])
        probs = sb("probs", [P, 3, T])
        pT = sb("pT", [P, 2, TT, P])
        rows = sb("rows", [P, 2, P], over=("sq", 0))
        cols = sb("cols", [P, 2, P])
        stat = sb("stat", [P, 64])
        rs = sb("rs", [P, 32])
        jobstat = sb("jobstat", [P, 8, 4])
        rope = sb("rope", [P, 6, TT, ROPE_HALF])
        small = sb("small", [P, 128])
        up = sb("up", [GLA_RANK + 1, 2, T])
        posi = sb("posi", [P, TT], I32)
        rgain = sb("rgain", [P, 4, MLA_ROPE])

        pe_did = signal("pe_did")
        act_did = signal("act_did")
        dve_did = signal("dve_did")
        pool_did = signal("pool_did")
        const_landed = signal("const_landed")
        gain_landed = [signal(f"gain_landed{i}") for i in range(4)]
        slot_landed = [signal(f"slot_landed{i}") for i in range(RAW_SLOTS)]
        out_landed = signal("out_landed")
        misc_landed = signal("misc_landed")
        units = weight_stream(a)
        split_units = [u for u in units if u.split]
        banks = [Bank(ctx.enter_context(nc.psum_tensor(f"bank{i}", [P, 512], F32)), dve_did.now()) for i in range(8)]
        turn = {"bank": 0, "evac": 0, "gain": 0, "taken": 0, "loaded": 0, "parted": 0}

        block = ctx.enter_context(nc.Block())

        def C(name, shape=None, rows_=P):
            c, w = const_where[name]
            v = (early if name in ("upto", "shift") else const)[0:rows_, c:c + w]
            return v if shape is None else v.rearrange("p (a b) -> p a b", a=shape[0])

        ident = C("ident")

        def marks():
            return Marks(pe_did.now(), act_did.now(), dve_did.now(), pool_did.now())

        def next_bank():
            b = banks[turn["bank"] % 8]
            turn["bank"] += 1
            return b


        def load(i):
            u = units[i]
            n = u.shape[0] * u.shape[1]
            slot = i % RAW_SLOTS
            u.raw = raw[:, slot, 0:n].rearrange("p (a b) -> p a b", a=u.shape[0])
            u.lo = w_lo[:, slot, 0:n].rearrange("p (a b) -> p a b", a=u.shape[0])

            @block.sync
            def _(sp):
                if i >= RAW_SLOTS:
                    sp.wait_ge(*units[i - RAW_SLOTS].used)
                for dst, src in u.parts(u.raw):
                    sp.dma_start(dst, src).then_inc(*slot_landed[slot].up(16))
            u.landed = slot_landed[slot].now()

        def part(i):
            u = split_units[i]
            n = u.shape[0] * u.shape[1]
            hi = w_hi[:, i % HI_SLOTS, 0:n]
            u.hi = hi.rearrange("p (a b) -> p a b", a=u.shape[0])
            raw_, lo_ = (v.rearrange("p a b -> p (a b)") for v in (u.raw, u.lo))

            @block.scalar
            def _(act):
                act.wait_ge(*u.landed)
                if i >= HI_SLOTS:
                    act.wait_ge(*split_units[i - HI_SLOTS].used)
                act.copy(hi, raw_).then_inc(*act_did.up())

            @block.vector
            def _(dve):
                dve.wait_ge(*act_did.now())
                dve.tensor_tensor(lo_, raw_, hi.bitcast(F32), ALU.subtract).then_inc(*dve_did.up())
            u.parted = dve_did.now()

        def take():
            def free(of, n, slots):
                return n < len(of) and (n < slots or of[n - slots].used is not None)
            while free(units, turn["loaded"], RAW_SLOTS):
                load(turn["loaded"])
                turn["loaded"] += 1
            while free(split_units, turn["parted"], HI_SLOTS) and split_units[turn["parted"]].landed is not None:
                part(turn["parted"])
                turn["parted"] += 1
            i = turn["taken"]
            turn["taken"] += 1
            return units[i]

        def to_T(nblk, src, dst, width=P, scale=None, group=2, dst_lo=None):
            before = marks()
            for b0 in range(0, nblk, group):
                n = min(group, nblk - b0)
                bank = next_bank()

                @block.tensor
                def _(pe):
                    pe.wait_ge(*bank.drained)
                    if b0 == 0:
                        pe.wait_ge(*before.act)
                        pe.wait_ge(*before.dve)
                        pe.wait_ge(*before.pool)
                    for b in range(n):
                        for tt in range(TT):
                            m = pe.transpose(bank.t[0:width, (b * TT + tt) * P:(b * TT + tt + 1) * P],
                                             src(b0 + b, tt), ident)
                    m.then_inc(*pe_did.up())
                full = pe_did.now()
                ps = bank.t[0:width, 0:n * T].rearrange("p (a b) -> p a b", a=n)
                turn["evac"] += 1
                if turn["evac"] % 2 and dst_lo is None:
                    @block.vector
                    def _(dve):
                        dve.wait_ge(*full)
                        if b0 < 2 * group:
                            dve.wait_ge(*before.act)
                            dve.wait_ge(*before.dve)
                            dve.wait_ge(*before.pool)
                        if scale is None:
                            dve.tensor_copy(dst(b0, n), ps).then_inc(*dve_did.up())
                        else:
                            for b in range(n):
                                dve.tensor_scalar(dst(b0 + b, 1), ps[:, b:b + 1, :], scale(b0 + b), None,
                                                  ALU.mult).then_inc(*dve_did.up())
                    bank.drained = dve_did.now()
                    continue

                @block.scalar
                def _(act):
                    act.wait_ge(*full)
                    if b0 < 2 * group:
                        act.wait_ge(*before.act)
                        act.wait_ge(*before.dve)
                        act.wait_ge(*before.pool)
                    if scale is None:
                        act.copy(dst(b0, n), ps).then_inc(*act_did.up())
                    else:
                        for b in range(n):
                            act.activation(dst(b0 + b, 1), ps[:, b:b + 1, :], ACT.Copy,
                                           scale=scale(b0 + b)).then_inc(*act_did.up())
                bank.drained = act_did.now()
                if dst_lo is None:
                    continue

                @block.vector
                def _(dve):
                    dve.wait_ge(*act_did.now())
                    if scale is None:
                        dve.tensor_tensor(dst_lo(b0, n), ps, dst(b0, n).bitcast(F32),
                                          ALU.subtract).then_inc(*dve_did.up())
                    else:
                        for b in range(n):
                            dve.scalar_tensor_tensor(dst_lo(b0 + b, 1), ps[:, b:b + 1, :], scale(b0 + b),
                                                     dst(b0 + b, 1).bitcast(F32), ALU.mult,
                                                     ALU.subtract).then_inc(*dve_did.up())
                bank.drained = dve_did.now()

        def three_products(pe, out, x_hi, x_lo, u, k, cols_, start, stop):
            pe.matmul(out, x_hi, u.hi[:, k, cols_], start=start, stop=False)
            pe.matmul(out, x_hi, u.lo[:, k, cols_], start=False, stop=False)
            return pe.matmul(out, x_lo, u.hi[:, k, cols_], start=False, stop=stop)

        def gemm(h, nk, width, evac):
            ready = marks()
            for c in range(0, width, 512):
                n = min(512, width - c)
                pair = [next_bank() for _ in range(TT)]
                k0 = 0
                while k0 < nk:
                    u = take()
                    assert u.shape[1] == n

                    @block.tensor
                    def _(pe):
                        if c == 0 and k0 == 0:
                            pe.wait_ge(*ready.act)
                            pe.wait_ge(*ready.dve)
                        if k0 == 0:
                            for bank in pair:
                                pe.wait_ge(*bank.drained)
                        pe.wait_ge(*u.parted)
                        for tt in range(TT):
                            ts_ = slice(tt * P, (tt + 1) * P)
                            for k in range(u.shape[0]):
                                m = three_products(pe, pair[tt].t[:, 0:n], h[0][:, k0 + k, ts_], h[1][:, k0 + k, ts_],
                                                   u, k, slice(0, n), k0 + k == 0, k0 + k == nk - 1)
                        m.then_inc(*pe_did.up())
                    u.used = pe_did.now()
                    k0 += u.shape[0]
                for tt in range(TT):
                    evac(tt, c, n, pair[tt], pe_did.now())

        def to_sbuf(dst, r=None, bias_before=None):
            before = marks()

            def evac(tt, c, n, bank, full):
                if tt == 0:
                    @block.vector
                    def _(dve):
                        dve.wait_ge(*full)
                        dve.wait_ge(*before.pe)
                        dve.wait_ge(*before.act)
                        dve.wait_ge(*before.dve)
                        dve.wait_ge(*before.pool)
                        if r is None:
                            dve.tensor_copy(dst(tt, c, n), bank.t[:, 0:n]).then_inc(*dve_did.up())
                        else:
                            dve.tensor_scalar(dst(tt, c, n), bank.t[:, 0:n], r(tt), None,
                                              ALU.mult).then_inc(*dve_did.up())
                    bank.drained = dve_did.now()
                else:
                    @block.scalar
                    def _(act):
                        act.wait_ge(*full)
                        act.wait_ge(*before.pe)
                        act.wait_ge(*before.act)
                        act.wait_ge(*before.dve)
                        act.wait_ge(*before.pool)
                        if r is None:
                            act.copy(dst(tt, c, n), bank.t[:, 0:n]).then_inc(*act_did.up())
                        else:
                            act.activation(dst(tt, c, n), bank.t[:, 0:n], ACT.Copy,
                                           scale=r(tt)).then_inc(*act_did.up())
                    bank.drained = act_did.now()
            return evac

        def power(dst, n, scale):
            @block.vector
            def _(dve):
                dve.wait_ge(*pe_did.now())
                dve.wait_ge(*act_did.now())
                dve.wait_ge(*dve_did.now())
                dve.wait_ge(*pool_did.now())
                dve.tensor_scalar(dst, dst, scale, EPS, ALU.mult, ALU.add).then_inc(*dve_did.up())

            @block.gpsimd
            def _(pool):
                pool.wait_ge(*pe_did.now())
                pool.wait_ge(*act_did.now())
                pool.wait_ge(*dve_did.now())
                pool.wait_ge(*pool_did.now())
                pool.tensor_tensor(dst, dst, C("minus_half")[:, 0:n], ALU.pow).then_inc(*pool_did.up())

        def rstd_rows(src, dst):
            @block.scalar
            def _(act):
                act.wait_ge(*pe_did.now())
                act.wait_ge(*act_did.now())
                act.wait_ge(*dve_did.now())
                act.wait_ge(*pool_did.now())
                for tt in range(TT):
                    act.activation(sq[:, tt, :], src[:, tt, :], ACT.Square,
                                   accum_out=dst[:, tt:tt + 1]).then_inc(*act_did.up())
            power(dst, TT, 1.0 / D)

        def rstd_heads(src, dst, heads, w):
            v = sq[:, :, 0:heads * w].rearrange("p t (h w) -> p t h w", h=heads)

            @block.scalar
            def _(act):
                act.wait_ge(*pe_did.now())
                act.wait_ge(*act_did.now())
                act.wait_ge(*dve_did.now())
                act.wait_ge(*pool_did.now())
                for tt in range(TT):
                    act.activation(v[:, tt], src[:, tt], ACT.Square).then_inc(*act_did.up())

            @block.vector
            def _(dve):
                dve.wait_ge(*pe_did.now())
                dve.wait_ge(*act_did.now())
                dve.wait_ge(*dve_did.now())
                dve.wait_ge(*pool_did.now())
                for tt in range(TT):
                    dve.tensor_reduce(dst[:, tt * heads:(tt + 1) * heads], v[:, tt], AX.X,
                                      ALU.add).then_inc(*dve_did.up())
            power(dst, TT * heads, 1.0 / w)

        def scale_heads(dst, src, r, heads):
            w = src.shape[3]

            def part(eng, tt):
                return eng.tensor_tensor(dst[:, tt], src[:, tt],
                                         r[:, tt * heads:(tt + 1) * heads].unsqueeze(2).broadcast_to([P, heads, w]),
                                         ALU.mult)
            before = marks()

            @block.vector
            def _(dve):
                dve.wait_ge(*before.pe)
                dve.wait_ge(*before.act)
                dve.wait_ge(*before.dve)
                dve.wait_ge(*before.pool)
                part(dve, 0).then_inc(*dve_did.up())

            @block.gpsimd
            def _(pool):
                pool.wait_ge(*before.pe)
                pool.wait_ge(*before.act)
                pool.wait_ge(*before.dve)
                pool.wait_ge(*before.pool)
                part(pool, 1).then_inc(*pool_did.up())

        def attention(jobs):
            before = marks()
            st = [dict() for _ in jobs]

            def scores(i):
                j, s = jobs[i], st[i]
                bank = s["bank"] = next_bank()

                @block.tensor
                def _(pe):
                    pe.wait_ge(*bank.drained)
                    pe.wait_ge(*before.act)
                    pe.wait_ge(*before.dve)
                    pe.wait_ge(*before.pool)
                    for m, (l, r) in enumerate(j["qk"]):
                        mm = pe.matmul(bank.t[:, 0:j["n"]], l, r, start=(m == 0), stop=(m == len(j["qk"]) - 1))
                    mm.then_inc(*pe_did.up())
                scored = pe_did.now()
                n, js = j["n"], jobstat[:, i % 8, :]

                @block.vector
                def _(dve):
                    dve.wait_ge(*scored)
                    if i >= 2:
                        dve.wait_ge(*st[i - 2]["exped"])
                    if i < 2:
                        dve.wait_ge(*before.pe)
                        dve.wait_ge(*before.act)
                        dve.wait_ge(*before.dve)
                        dve.wait_ge(*before.pool)
                    if j["bias"] is not None:
                        dve.scalar_tensor_tensor(smask[:, i % 2, 0:n], bank.t[:, 0:n], j["scale"], j["bias"],
                                                 ALU.mult, ALU.add).then_inc(*dve_did.up())
                        dve.wait_ge(*dve_did.now())
                        dve.tensor_reduce(js[:, 0:1], smask[:, i % 2, 0:n], AX.X, ALU.max,
                                          negate=True).then_inc(*dve_did.up())
                        if j.get("guard"):
                            dve.wait_ge(*dve_did.now())
                            dve.tensor_scalar(js[:, 0:1], js[:, 0:1], -NEG / 10, None,
                                              ALU.min).then_inc(*dve_did.up())
                    else:
                        dve.tensor_reduce(js[:, 1:2], bank.t[:, 0:n], AX.X, ALU.max,
                                          negate=True).then_inc(*dve_did.up())
                        dve.wait_ge(*dve_did.now())
                        dve.tensor_scalar(js[:, 0:1], js[:, 1:2], j["scale"], None, ALU.mult).then_inc(*dve_did.up())
                maxed = dve_did.now()

                @block.scalar
                def _(act):
                    act.wait_ge(*maxed)
                    if i >= 3:
                        act.wait_ge(*st[i - 3]["turned"])
                    if i < 3:
                        act.wait_ge(*before.pe)
                        act.wait_ge(*before.act)
                        act.wait_ge(*before.dve)
                        act.wait_ge(*before.pool)
                    if j["bias"] is not None:
                        act.activation(probs[:, i % 3, 0:n], smask[:, i % 2, 0:n], ACT.Exp, bias=js[:, 0:1],
                                       accum_out=js[:, 2:3]).then_inc(*act_did.up())
                    else:
                        act.activation(probs[:, i % 3, 0:n], bank.t[:, 0:n], ACT.Exp, bias=js[:, 0:1],
                                       scale=j["scale"], accum_out=js[:, 2:3]).then_inc(*act_did.up())
                s["exped"] = act_did.now()
                bank.drained = act_did.now()

            def turned(i):
                j, s = jobs[i], st[i]
                bank = next_bank()

                @block.tensor
                def _(pe):
                    pe.wait_ge(*s["exped"])
                    pe.wait_ge(*bank.drained)
                    for b, v in enumerate(j["v"]):
                        kb = v.shape[0]
                        m = pe.transpose(bank.t[0:kb, b * P:(b + 1) * P], probs[:, i % 3, b * P:b * P + kb], ident)
                    m.then_inc(*pe_did.up())
                s["turned"] = pe_did.now()
                nb, kb = len(j["v"]), j["v"][0].shape[0]

                @block.scalar
                def _(act):
                    act.wait_ge(*s["turned"])
                    if i >= 2:
                        act.wait_ge(*st[i - 2]["summed"])
                    act.copy(pT[0:kb, i % 2, 0:nb, :],
                             bank.t[0:kb, 0:nb * P].rearrange("p (a b) -> p a b", a=nb)).then_inc(*act_did.up())
                s["copied"] = bank.drained = act_did.now()
                js = jobstat[:, i % 8, :]

                @block.vector
                def _(dve):
                    dve.wait_ge(*s["exped"])
                    if j.get("guard"):
                        dve.tensor_scalar(js[:, 2:3], js[:, 2:3], 1e-30, None, ALU.max).then_inc(*dve_did.up())
                        dve.wait_ge(*dve_did.now())
                    dve.reciprocal(js[:, 3:4], js[:, 2:3]).then_inc(*dve_did.up())
                    if j.get("mul") is not None:
                        dve.wait_ge(*dve_did.now())
                        dve.tensor_tensor(js[:, 3:4], js[:, 3:4], j["mul"], ALU.mult).then_inc(*dve_did.up())
                s["inverse"] = dve_did.now()

            def summed(i):
                j, s = jobs[i], st[i]
                bank = next_bank()

                @block.tensor
                def _(pe):
                    pe.wait_ge(*s["copied"])
                    pe.wait_ge(*bank.drained)
                    for b, v in enumerate(j["v"]):
                        m = pe.matmul(bank.t[:, 0:j["dv"]], pT[0:v.shape[0], i % 2, b, :], v,
                                      start=(b == 0), stop=(b == len(j["v"]) - 1))
                    m.then_inc(*pe_did.up())
                s["summed"] = pe_did.now()
                js = jobstat[:, i % 8, :]

                @block.vector
                def _(dve):
                    dve.wait_ge(*s["summed"])
                    dve.wait_ge(*s["inverse"])
                    if j.get("add"):
                        dve.wait_ge(*st[i - 1]["written"])
                    if j.get("add"):
                        dve.scalar_tensor_tensor(j["out"], bank.t[:, 0:j["dv"]], js[:, 3:4], j["out"],
                                                 ALU.mult, ALU.add).then_inc(*dve_did.up())
                    else:
                        dve.tensor_scalar(j["out"], bank.t[:, 0:j["dv"]], js[:, 3:4], None,
                                          ALU.mult).then_inc(*dve_did.up())
                s["written"] = bank.drained = dve_did.now()

            for i in range(len(jobs) + 2):
                if i < len(jobs):
                    scores(i)
                if 1 <= i <= len(jobs):
                    turned(i - 1)
                if i >= 2:
                    summed(i - 2)

        def ffn(r, finish):
            before = marks()
            NF = D_FF // FF_CHUNK
            KB = FF_CHUNK // P
            pair = [banks[0:2], banks[2:4]]
            acc = banks[4:8]
            turn["bank"] = 0
            hid_done, turned, split, down_done = {}, {}, {}, {}

            def gate_up(c, u, k0):
                @block.tensor
                def _(pe):
                    if k0 == 0:
                        for bank in pair[c % 2]:
                            pe.wait_ge(*bank.drained)
                        if c == 0:
                            pe.wait_ge(*before.act)
                            pe.wait_ge(*before.dve)
                    pe.wait_ge(*u.parted)
                    for tt in range(TT):
                        ts_ = slice(tt * P, (tt + 1) * P)
                        for k in range(u.shape[0]):
                            m = three_products(pe, pair[c % 2][tt].t[:, :], h_hi[:, k0 + k, ts_], h_lo[:, k0 + k, ts_],
                                               u, k, slice(0, 512), k0 + k == 0, k0 + k == KD - 1)
                    m.then_inc(*pe_did.up())
                u.used = pe_did.now()

            def hidden(c):
                full = pe_did.now()
                for tt in range(TT):
                    bank = pair[c % 2][tt]

                    @block.scalar
                    def _(act):
                        act.wait_ge(*full)
                        if c >= 2:
                            act.wait_ge(*hid_done[(c - 2, tt)])
                        elif tt == 0:
                            act.wait_ge(*before.dve)
                            act.wait_ge(*before.pool)
                        act.activation(ff_silu[:, c % 2, tt, :], bank.t[:, 0:FF_CHUNK], ACT.Silu,
                                       scale=r(tt)).then_inc(*act_did.up())

                    @block.vector
                    def _(dve):
                        dve.wait_ge(*act_did.now())
                        if c >= 2:
                            dve.wait_ge(*turned[c - 2])
                        dve.scalar_tensor_tensor(ff_hid[:, c % 2, tt, :], bank.t[:, FF_CHUNK:2 * FF_CHUNK], r(tt),
                                                 ff_silu[:, c % 2, tt, :], ALU.mult, ALU.mult).then_inc(*dve_did.up())
                    hid_done[(c, tt)] = bank.drained = dve_did.now()

            def transposes(c):
                bank = pair[c % 2][0]

                @block.tensor
                def _(pe):
                    pe.wait_ge(*hid_done[(c, 1)])
                    for b in range(KB):
                        for tt in range(TT):
                            m = pe.transpose(bank.t[:, (b * TT + tt) * P:(b * TT + tt + 1) * P],
                                             ff_hid[:, c % 2, tt, b * P:(b + 1) * P], ident)
                    m.then_inc(*pe_did.up())
                turned[c] = pe_did.now()
                ps = bank.t[:, 0:KB * T].rearrange("p (b n) -> p b n", b=KB)

                @block.scalar
                def _(act):
                    act.wait_ge(*turned[c])
                    if c >= 2:
                        act.wait_ge(*down_done[c - 2])
                    act.copy(ff_hi[:, c % 2, :, :], ps).then_inc(*act_did.up())

                @block.vector
                def _(dve):
                    dve.wait_ge(*act_did.now())
                    dve.tensor_tensor(ff_lo[:, c % 2, :, :], ps, ff_hi[:, c % 2, :, :].bitcast(F32),
                                      ALU.subtract).then_inc(*dve_did.up())
                split[c] = bank.drained = dve_did.now()

            def down(c, u):
                @block.tensor
                def _(pe):
                    if c == 0:
                        for bank in acc:
                            pe.wait_ge(*bank.drained)
                    pe.wait_ge(*split[c])
                    pe.wait_ge(*u.parted)
                    for b in range(KB):
                        for tt in range(TT):
                            ts_ = slice(tt * P, (tt + 1) * P)
                            for half in range(2):
                                m = three_products(pe, acc[tt * 2 + half].t[:, :], ff_hi[:, c % 2, b, ts_],
                                                   ff_lo[:, c % 2, b, ts_], u, b, slice(half * 512, (half + 1) * 512),
                                                   c == 0 and b == 0, c == NF - 1 and b == KB - 1)
                    m.then_inc(*pe_did.up())
                u.used = down_done[c] = pe_did.now()

            for c in range(NF + 1):
                if c < NF:
                    gate_up(c, take(), 0)
                if c >= 1:
                    transposes(c - 1)
                if c < NF:
                    gate_up(c, take(), KD // 2)
                    hidden(c)
                if c >= 1:
                    down(c - 1, take())
            for tt in range(TT):
                for half in range(2):
                    finish(tt, half, acc[tt * 2 + half], pe_did.now())

        def add_half(tt, half, bank, full):
            @block.vector
            def _(dve):
                dve.wait_ge(*full)
                dve.wait_ge(*pe_did.now())
                dve.wait_ge(*act_did.now())
                dve.wait_ge(*dve_did.now())
                dve.wait_ge(*pool_did.now())
                xs = x[:, tt, half * 512:(half + 1) * 512]
                dve.scalar_tensor_tensor(xs, bank.t[:, :], 0.5, xs, ALU.mult, ALU.add).then_inc(*dve_did.up())
            bank.drained = dve_did.now()

        def finish_to_o(tt, half, bank, full):
            to_sbuf(lambda t, c, n: o_buf[:, t, half * 512:(half + 1) * 512])(tt, 0, 512, bank, full)

        def hi_of(buf):
            return lambda b, n: buf[:, b:b + n, :]

        def pre_norm(src, col, r):
            rstd_rows(src, r)
            to_T(KD, lambda b, tt: src[:, tt, b * P:(b + 1) * P], hi_of(h_hi), dst_lo=hi_of(h_lo),
                 scale=lambda b: cols[:, col // P, col % P + b:col % P + b + 1])

        def load_gain(src):
            g = turn["gain"] % 2
            turn["gain"] += 1
            before = marks()

            @block.sync
            def _(sp):
                sp.wait_ge(*before.pe)
                sp.wait_ge(*before.act)
                sp.wait_ge(*before.dve)
                sp.wait_ge(*before.pool)
                sp.dma_start(gain[:, g, :], src.partition_broadcast(P)).then_inc(*gain_landed[g].up(16))
            return gain[:, g, :], gain_landed[g].now()

        def post_norm(y, g):
            gv, landed = g
            rstd_rows(y, rs[:, 30:32])
            before = marks()

            @block.vector
            def _(dve):
                dve.wait_ge(*landed)
                dve.wait_ge(*before.pe)
                dve.wait_ge(*before.act)
                dve.wait_ge(*before.dve)
                dve.wait_ge(*before.pool)
                for tt in range(TT):
                    dve.scalar_tensor_tensor(y[:, tt, :], y[:, tt, :], rs[:, 30 + tt:31 + tt], gv,
                                             ALU.mult, ALU.mult).then_inc(*dve_did.up())
                dve.wait_ge(*dve_did.now())
                dve.tensor_tensor(x[:, 0, :], x[:, 0, :], y[:, 0, :], ALU.add).then_inc(*dve_did.up())

            @block.gpsimd
            def _(pool):
                pool.wait_ge(*dve_did.now())
                pool.wait_ge(*before.pe)
                pool.wait_ge(*before.act)
                pool.wait_ge(*before.dve)
                pool.wait_ge(*before.pool)
                pool.tensor_tensor(x[:, 1, :], x[:, 1, :], y[:, 1, :], ALU.add).then_inc(*pool_did.up())

        def rs_of(c):
            return lambda tt: rs[:, c + tt:c + tt + 1]

        h_in, h2_in = (h_hi, h_lo), (h2_hi, h2_lo)

        row_at = [0, P]
        col_of = {}

        @block.scalar
        def _(act):
            act.dma_start(const[:, :], a["const"]).then_inc(*const_landed.up(16))
            act.dma_start(early[:, :], a["early"]).then_inc(*const_landed.up(16))

            def row(name, src, n, tile):
                r = row_at[tile]
                act.dma_start(rows[r % P:r % P + n, tile, :], src.rearrange("(a b) -> a b", a=n)).then_inc(
                    *const_landed.up(16))
                col_of[name] = r
                row_at[tile] += n
            for l in range(DEPTH):
                for g in (0, 2, 4):
                    row(("pre", l, g), a["sandwich_g"][l, g, :], KD, 0)
                row(("mem", l), a["mem_norm_g"][l, :], KD, 0)
                for name in ("ffn1_norm_2", "mix_norm_2", "ffn2_norm_2"):
                    row((name, l), a[name][l, :], KD, 0)
            for name in ("ev_cmp_pos_k", "ev_cmp_pos_v"):
                row(name, a[name][0].rearrange("a b -> (a b)"), CMP_BLOCK // 2, 1)
            row("subln", a["od_subln_g"][0, :], 1, 1)
            for l in range(DEPTH):
                row(("gla_out", l), a["gla_out_norm_2"][l, :], 1, 1)
                row(("cq", l), a["mla_cq_norm_2"][l, :], 2, 1)
                row(("ckv", l), a["mla_ckv_norm_2"][l, :], 2, 1)
                row(("mla_q", l), a["mla_q_norm_2"][l, 0:P], 1, 1)
                row(("mla_k", l), a["mla_k_norm_2"][l, 0:P], 1, 1)
                for m, name in enumerate(("na_q_norm_2", "na_k_norm_2")):
                    r = row_at[1] - P
                    for h in range(2):
                        act.dma_start(rows[r:r + 1, 1, h * HD:(h + 1) * HD], a[name][l:l + 1, :]).then_inc(
                            *const_landed.up(16))
                    col_of[(name, l)] = row_at[1]
                    row_at[1] += 1
                    act.dma_start(rgain[:, l * 2 + m, :],
                                  a[("mla_q_norm_2", "mla_k_norm_2")[m]][l, P:MLA_QK].partition_broadcast(P)).then_inc(
                        *const_landed.up(16))
            act.dma_start(small[:, 0:FOX_H], a["ev_fox_fbias"][0, :].partition_broadcast(P)).then_inc(
                *const_landed.up(16))
            act.dma_start(tmp[:, 0, 0:4 * HD], a["od_lambda"][0].rearrange("a b -> (a b)").partition_broadcast(P)).then_inc(
                *const_landed.up(16))

            with nc.allow_non_contiguous_dma(reason="256 positions, once"):
                act.dma_start(posi[:, :], a["positions"][0, :].rearrange("(t p) -> p t", p=P)).then_inc(
                    *const_landed.up(16))

        table = nc.dram_tensor("bias_table", [DEPTH, NA_H, GRID_W, TBL_W], F32, kind="Internal").ap()
        table_landed = signal("table_landed")

        @block.gpsimd
        def _(pool):
            for l in range(DEPTH):
                flat = a["na_rpb_2"][l].rearrange("h r c -> h (r c)")[:, TBL_LO:TBL_HI]
                pool.dma_start(table[l], flat.unsqueeze(1).broadcast_to([NA_H, GRID_W, TBL_W])).then_inc(
                    *table_landed.up(16))

        @block.sync
        def _(sp):
            sp.dma_start(x[:, :, :], a["x"][0].rearrange("(t p) d -> p t d", p=P)).then_inc(*const_landed.up(16))
            sp.dma_start(gate[:, :, :], a["mem"][0].rearrange("(t p) d -> p t d", p=P)).then_inc(*const_landed.up(16))

        landed = const_landed.now()

        @block.vector
        def _(dve):
            dve.wait_ge(*landed)

        @block.scalar
        def _(act):
            act.wait_ge(*landed)

        @block.gpsimd
        def _(pool):
            pool.wait_ge(*landed)
            pool.memset(rs[:, :], 1.0).then_inc(*pool_did.up())

        used = [row_at[0], row_at[1] - P]
        bank = next_bank()

        @block.tensor
        def _(pe):
            pe.wait_ge(*landed)
            for tile in range(2):
                n = used[tile]
                m = pe.transpose(bank.t[:, tile * P:tile * P + n], rows[0:n, tile, :], ident[0:n, 0:n])
            m.then_inc(*pe_did.up())
        full = pe_did.now()

        @block.vector
        def _(dve):
            dve.wait_ge(*full)
            for tile in range(2):
                dve.tensor_copy(cols[:, tile, 0:used[tile]],
                                bank.t[:, tile * P:tile * P + used[tile]]).then_inc(*dve_did.up())
            dve.wait_ge(*dve_did.now())
            c = col_of["subln"] % P
            dve.tensor_scalar(cols[:, 1, c:c + 1], cols[:, 1, c:c + 1], 1.0 - LAM_INIT, None,
                              ALU.mult).then_inc(*dve_did.up())
        bank.drained = dve_did.now()

        cos1, sin1 = rope[:, 0], rope[:, 1]
        ang, turns, half_a, sin_h = rope[:, 2], rope[:, 3], rope[:, 4], rope[:, 5]
        TWO_PI = 2 * math.pi
        hi = float(np.float32(6.28125))
        mid = float(np.float32(TWO_PI - hi))
        lo_ = float(np.float32(TWO_PI - hi - mid))
        ROUND = float(3 << 22)

        @block.vector
        def _(dve):
            def then(i):
                i.then_inc(*dve_did.up())
                dve.wait_ge(*dve_did.now())
            then(dve.tensor_copy(small[:, 16:16 + TT], posi[:, :]))
            then(dve.tensor_tensor(ang, small[:, 16:16 + TT].unsqueeze(2).broadcast_to([P, TT, ROPE_HALF]),
                                   C("inv").unsqueeze(1).broadcast_to([P, TT, ROPE_HALF]), ALU.mult))
            then(dve.tensor_scalar(turns, ang, 1.0 / TWO_PI, ROUND, ALU.mult, ALU.add))
            then(dve.tensor_scalar(turns, turns, -ROUND, None, ALU.add))
            for part in (hi, mid, lo_):
                then(dve.scalar_tensor_tensor(ang, turns, -part, ang, ALU.mult, ALU.add))
            then(dve.tensor_scalar(ang, ang, math.pi, -math.pi, ALU.min, ALU.max))
            then(dve.tensor_scalar(half_a, ang, 0.5, None, ALU.mult))
            lp = tmp[:, 0, 0:4 * HD].rearrange("p (a b) -> p a b", a=4)
            for m in range(2):
                then(dve.tensor_tensor(tmp[:, 1, m * HD:(m + 1) * HD], lp[:, 2 * m, :], lp[:, 2 * m + 1, :], ALU.mult))
            then(dve.tensor_reduce(small[:, 20:22], tmp[:, 1, 0:2 * HD].rearrange("p (a b) -> p a b", a=2), AX.X,
                                   ALU.add))

        @block.scalar
        def _(act):
            act.wait_ge(*pe_did.now())
            act.wait_ge(*act_did.now())
            act.wait_ge(*dve_did.now())
            act.wait_ge(*pool_did.now())
            act.activation(sin1, ang, ACT.Sin).then_inc(*act_did.up())
            act.activation(sin_h, half_a, ACT.Sin).then_inc(*act_did.up())
            act.activation(small[:, 22:24], small[:, 20:22], ACT.Exp).then_inc(*act_did.up())
        neg_lam = small[:, 25:26]

        @block.vector
        def _(dve):
            dve.wait_ge(*pe_did.now())
            dve.wait_ge(*act_did.now())
            dve.wait_ge(*dve_did.now())
            dve.wait_ge(*pool_did.now())
            dve.tensor_tensor(cos1, sin_h, sin_h, ALU.mult).then_inc(*dve_did.up())
            dve.wait_ge(*dve_did.now())
            dve.tensor_scalar(cos1, cos1, -2.0, 1.0, ALU.mult, ALU.add).then_inc(*dve_did.up())
            dve.tensor_tensor(small[:, 24:25], small[:, 23:24], small[:, 22:23], ALU.subtract).then_inc(*dve_did.up())
            dve.wait_ge(*dve_did.now())
            dve.tensor_scalar(neg_lam, small[:, 24:25], -LAM_INIT, None, ALU.add).then_inc(*dve_did.up())

        def rotate(v, heads, half, cos, sin, second=False):
            x1, x2 = v[:, :, :, 0:half], v[:, :, :, half:2 * half]
            shape = [P, heads, half]
            sz = heads * half
            t = [sq[:, :, m * sz:(m + 1) * sz].rearrange("p t (h w) -> p t h w", h=heads) for m in range(4)]
            before = marks()

            def products(eng, sig, tt, pairs):
                for dst, xx, table in pairs:
                    eng.tensor_tensor(t[dst][:, tt], xx[:, tt], table[:, tt, :].unsqueeze(1).broadcast_to(shape),
                                      ALU.mult).then_inc(*sig.up())

            @block.vector
            def _(dve):
                dve.wait_ge(*before.pe)
                dve.wait_ge(*before.act)
                dve.wait_ge(*before.dve)
                dve.wait_ge(*before.pool)
                for tt in range(TT):
                    products(dve, dve_did, tt, ((0, x1, cos), (1, x2, sin)))

            @block.gpsimd
            def _(pool):
                pool.wait_ge(*before.pe)
                pool.wait_ge(*before.act)
                pool.wait_ge(*before.dve)
                pool.wait_ge(*before.pool)
                for tt in range(TT):
                    products(pool, pool_did, tt, ((2, x2, cos), (3, x1, sin)))
            after = marks()

            @block.vector
            def _(dve):
                dve.wait_ge(*after.pe)
                dve.wait_ge(*after.act)
                dve.wait_ge(*after.dve)
                dve.wait_ge(*after.pool)
                for tt in range(TT):
                    dve.tensor_tensor(x1[:, tt], t[0][:, tt], t[1][:, tt], ALU.subtract).then_inc(*dve_did.up())

            @block.gpsimd
            def _(pool):
                pool.wait_ge(*after.pe)
                pool.wait_ge(*after.act)
                pool.wait_ge(*after.dve)
                pool.wait_ge(*after.pool)
                for tt in range(TT):
                    pool.tensor_tensor(x2[:, tt], t[2][:, tt], t[3][:, tt], ALU.add).then_inc(*pool_did.up())

        def heads_of(c, n, w=HD, buf=z):
            return buf[:, :, c:c + n * w].rearrange("p t (h w) -> p t h w", h=n)

        def log_sigmoid(dst, src, n, t1, t2, from_psum=()):
            @block.scalar
            def _(act):
                act.wait_ge(*pe_did.now())
                act.wait_ge(*act_did.now())
                act.wait_ge(*dve_did.now())
                act.wait_ge(*pool_did.now())
                act.activation(t1, src, ACT.Abs).then_inc(*act_did.up())
                act.wait_ge(*act_did.now())
                act.activation(t2, t1, ACT.Exp, scale=-1.0).then_inc(*act_did.up())
                act.wait_ge(*act_did.now())
                act.activation(t1, t2, ACT.Ln, bias=C("one")).then_inc(*act_did.up())

            @block.vector
            def _(dve):
                dve.wait_ge(*pe_did.now())
                dve.wait_ge(*act_did.now())
                dve.wait_ge(*dve_did.now())
                dve.wait_ge(*pool_did.now())
                dve.scalar_tensor_tensor(dst, src, 0.0, t1, ALU.min, ALU.subtract).then_inc(*dve_did.up())

        causal = C("causal", (TT,))

        def even_mixer(g1):
            pre_norm(x, col_of[("pre", 0, 0)], rs[:, 0:2])
            gemm(h_in, KD, EV_IN, to_sbuf(lambda tt, c, n: z[:, tt, c:c + n], rs_of(0)))
            lf = small[:, 32:48].rearrange("p (t h) -> p t h", t=TT)

            @block.vector
            def _(dve):
                dve.wait_ge(*pe_did.now())
                dve.wait_ge(*act_did.now())
                dve.wait_ge(*dve_did.now())
                dve.wait_ge(*pool_did.now())
                dve.tensor_tensor(lf, z[:, :, EV["fl"]:EV["fl"] + FOX_H],
                                  small[:, 0:FOX_H].unsqueeze(1).broadcast_to([P, TT, FOX_H]),
                                  ALU.add).then_inc(*dve_did.up())
            log_sigmoid(small[:, 80:96], small[:, 32:48], 16, small[:, 48:64], small[:, 64:80])
            lfs = small[:, 80:96].rearrange("p (t h) -> p t h", t=TT)
            bank = next_bank()

            @block.tensor
            def _(pe):
                pe.wait_ge(*bank.drained)
                pe.wait_ge(*act_did.now())
                pe.wait_ge(*dve_did.now())
                pe.wait_ge(*pool_did.now())
                for tt in range(TT):
                    m = pe.matmul(bank.t[0:FOX_H, 0:T], lfs[:, tt, :], C("upto", (TT,))[:, tt, :],
                                  start=(tt == 0), stop=(tt == TT - 1))
                m.then_inc(*pe_did.up())
            c_neg = hT2[0:FOX_H, 7, :]

            @block.vector
            def _(dve):
                dve.wait_ge(*pe_did.now())
                dve.wait_ge(*act_did.now())
                dve.wait_ge(*dve_did.now())
                dve.wait_ge(*pool_did.now())
                dve.tensor_scalar(c_neg, bank.t[0:FOX_H, 0:T], -(HD ** 0.5), None, ALU.mult).then_inc(*dve_did.up())
            bank.drained = dve_did.now()

            rotate(heads_of(EV["nq"], 10), 10, ROPE_HALF, cos1, sin1)
            rotate(heads_of(EV["ks"], 2), 2, ROPE_HALF, cos1, sin1)
            rotate(heads_of(EV["kw"], 2), 2, ROPE_HALF, cos1, sin1)
            sgate = stat[:, 0:TT * 3 * NSA_H].rearrange("p (t h) -> p t h", t=TT)

            @block.scalar
            def _(act):
                act.wait_ge(*pe_did.now())
                act.wait_ge(*act_did.now())
                act.wait_ge(*dve_did.now())
                act.wait_ge(*pool_did.now())
                act.activation(sgate, z[:, :, EV["gl"]:EV["gl"] + 3 * NSA_H], ACT.Sigmoid).then_inc(*act_did.up())
            kd = tmp[:, :, 0:512].rearrange("p t (b c d) -> p t b c d", b=4, c=2)

            @block.gpsimd
            def _(pool):
                pool.wait_ge(*pe_did.now())
                pool.wait_ge(*act_did.now())
                pool.wait_ge(*dve_did.now())
                pool.wait_ge(*pool_did.now())
                for m, name in enumerate(("ks", "kw")):
                    for c in range(2):
                        for tt in range(TT):
                            pool.tensor_copy(kd[:, tt, 2 * m:2 * m + 2, c, :],
                                             heads_of(EV[name], 2)[:, tt]).then_inc(*pool_did.up())
            to_T(4, lambda b, tt: z[:, tt, EV["fq"] + b * P:EV["fq"] + (b + 1) * P], lambda b, n: qT[:, b:b + n, :])
            to_T(4, lambda b, tt: z[:, tt, EV["fk"] + b * P:EV["fk"] + (b + 1) * P], lambda b, n: kT[:, b:b + n, :])
            to_T(4, lambda b, tt: z[:, tt, EV["nq"] + b * P:EV["nq"] + (b + 1) * P],
                 lambda b, n: qT[:, 4 + b:4 + b + n, :])
            to_T(4, lambda b, tt: tmp[:, tt, b * P:(b + 1) * P], lambda b, n: kT[:, 4 + b:4 + b + n, :])

            kcT = hT2[:, 4:6, :].rearrange("p a b -> p (a b)")[:, 0:2 * NC]
            vcmp = hT2[:, 6, 0:2 * HD]
            for m, (name, pos, w1, w2) in enumerate((("kc", "ev_cmp_pos_k", "ev_cmp_w1_k", "ev_cmp_w2_k"),
                                                     ("vc", "ev_cmp_pos_v", "ev_cmp_w1_v", "ev_cmp_w2_v"))):
                win = hT2[:, 2 * m:2 * m + 2, :]
                before = marks()
                for g in range(2):
                    bank = next_bank()

                    @block.tensor
                    def _(pe):
                        pe.wait_ge(*bank.drained)
                        pe.wait_ge(*before.act)
                        pe.wait_ge(*before.dve)
                        pe.wait_ge(*before.pool)
                        for tt in range(TT):
                            src = z[:, tt, EV[name] + g * HD:EV[name] + (g + 1) * HD]
                            pe.matmul(bank.t[0:HD, tt * P:(tt + 1) * P], src, ident, start=True, stop=True)
                        for tt in range(TT):
                            src = z[:, tt, EV[name] + g * HD:EV[name] + (g + 1) * HD]
                            mm = pe.matmul(bank.t[HD:P, 0:T], src, C("shift", (TT,))[:, tt, :],
                                           start=(tt == 0), stop=(tt == TT - 1))
                        mm.then_inc(*pe_did.up())

                    @block.vector
                    def _(dve):
                        dve.wait_ge(*pe_did.now())
                        dve.wait_ge(*before.pe)
                        dve.wait_ge(*before.act)
                        dve.wait_ge(*before.dve)
                        dve.wait_ge(*before.pool)
                        dve.tensor_copy(win[:, g, :], bank.t[:, 0:T]).then_inc(*dve_did.up())
                    bank.drained = dve_did.now()
                NL = CMP_BLOCK // 2
                cw1, cw2 = take(), take()
                bank, bank2 = next_bank(), next_bank()
                pc = col_of[pos] % P

                @block.tensor
                def _(pe):
                    pe.wait_ge(*cw1.landed)
                    pe.wait_ge(*bank.drained)
                    pe.wait_ge(*bank2.drained)
                    pe.wait_ge(*act_did.now())
                    pe.wait_ge(*dve_did.now())
                    pe.wait_ge(*pool_did.now())
                    for l in range(NL):
                        pe.matmul(bank.t[:, 0:2 * NC].rearrange("p (g c) -> p g c", g=2), cw1.raw[:, l, :],
                                  win[:, :, 2 * l:2 * l + CMP_STRIDE * (NC - 1) + 1:CMP_STRIDE],
                                  start=(l == 0), stop=(l == NL - 1))
                    for l in range(NL):
                        mm = pe.matmul(bank2.t[:, 0:1], cw1.raw[:, l, :], cols[:, 1, pc + l:pc + l + 1],
                                       start=(l == 0), stop=(l == NL - 1))
                    mm.then_inc(*pe_did.up())
                cw1.used = pe_did.now()
                hidden = sq[:, 0, m * 32:m * 32 + 2 * NC]
                pos_h = sq[:, 0, 64 + m:65 + m]

                @block.vector
                def _(dve):
                    dve.wait_ge(*pe_did.now())
                    dve.wait_ge(*act_did.now())
                    dve.wait_ge(*dve_did.now())
                    dve.wait_ge(*pool_did.now())
                    dve.tensor_copy(pos_h, bank2.t[:, 0:1]).then_inc(*dve_did.up())
                bank2.drained = dve_did.now()

                @block.scalar
                def _(act):
                    act.wait_ge(*pe_did.now())
                    act.wait_ge(*act_did.now())
                    act.wait_ge(*dve_did.now())
                    act.wait_ge(*pool_did.now())
                    act.activation(hidden, bank.t[:, 0:2 * NC], ACT.Gelu_apprx_tanh, bias=pos_h).then_inc(*act_did.up())
                bank.drained = act_did.now()
                bank3 = next_bank()

                @block.tensor
                def _(pe):
                    pe.wait_ge(*cw2.landed)
                    pe.wait_ge(*bank3.drained)
                    pe.wait_ge(*act_did.now())
                    pe.wait_ge(*dve_did.now())
                    pe.wait_ge(*pool_did.now())
                    if m == 0:
                        mm = pe.matmul(bank3.t[:, 0:2 * NC], cw2.raw[:, 0, :], hidden, start=True, stop=True)
                    else:
                        for g in range(2):
                            mm = pe.matmul(bank3.t[0:NC, g * HD:(g + 1) * HD], hidden[:, g * NC:(g + 1) * NC],
                                           cw2.raw[:, 0, 0:HD], start=True, stop=True)
                    mm.then_inc(*pe_did.up())
                cw2.used = pe_did.now()

                @block.vector
                def _(dve):
                    dve.wait_ge(*pe_did.now())
                    dve.wait_ge(*act_did.now())
                    dve.wait_ge(*dve_did.now())
                    dve.wait_ge(*pool_did.now())
                    if m == 0:
                        dve.tensor_copy(kcT, bank3.t[:, 0:2 * NC]).then_inc(*dve_did.up())
                    else:
                        dve.tensor_copy(vcmp[0:NC, :], bank3.t[0:NC, 0:2 * HD]).then_inc(*dve_did.up())
                bank3.drained = dve_did.now()

            jobs = []
            for h in range(FOX_H):
                b = HD * (h % 2)
                for tt in range(TT):
                    n = (tt + 1) * P
                    jobs.append(dict(
                        qk=[(qT[b:b + HD, h // 2, tt * P:(tt + 1) * P], kT[b:b + HD, h // 2, 0:n]),
                            (ident[0:FOX_H, h:h + 1].broadcast_to([FOX_H, P]), c_neg[:, 0:n])],
                        n=n, bias=causal[:, tt, 0:n], scale=HD ** -0.5, dv=HD,
                        v=[z[:, kb, EV["fv"] + h * HD:EV["fv"] + (h + 1) * HD] for kb in range(tt + 1)],
                        out=o_buf[:, tt, h * HD:(h + 1) * HD]))
            for h in range(NSA_H):
                b, g = HD * (h % 2), h // (NSA_H // 2)
                for tt in range(TT):
                    q = qT[b:b + HD, 4 + h // 2, tt * P:(tt + 1) * P]
                    dst = o_buf[:, tt, 512 + h * HD:512 + (h + 1) * HD]
                    jobs.append(dict(qk=[(q, kcT[b:b + HD, g * NC:(g + 1) * NC])], n=NC,
                                     bias=C("cmp", (TT,))[:, tt, :], scale=HD ** -0.5, dv=HD,
                                     v=[vcmp[0:NC, g * HD:(g + 1) * HD]], out=dst, guard=True,
                                     mul=sgate[:, tt, 3 * h:3 * h + 1]))
                    n = (tt + 1) * P
                    for m, name in enumerate(("vs", "vw")):
                        jobs.append(dict(qk=[(q, kT[b:b + HD, 4 + 2 * m + g, 0:n])], n=n, bias=causal[:, tt, 0:n],
                                         scale=HD ** -0.5, dv=HD,
                                         v=[z[:, kb, EV[name] + g * HD:EV[name] + (g + 1) * HD] for kb in range(tt + 1)],
                                         out=dst, add=True, mul=sgate[:, tt, 3 * h + 1 + m:3 * h + 2 + m]))
            attention(jobs)
            project_o()

        def project_o():
            to_T(KD, lambda b, tt: o_buf[:, tt, b * P:(b + 1) * P], hi_of(h_hi), dst_lo=hi_of(h_lo))
            gemm(h_in, KD, D, to_sbuf(lambda tt, c, n: o_buf[:, tt, c:c + n]))

        def diff_mixer():
            pre_norm(x, col_of[("pre", 1, 0)], rs[:, 0:2])
            gemm(h_in, KD, 3 * D, to_sbuf(lambda tt, c, n: z[:, tt, c:c + n], rs_of(0)))
            rotate(heads_of(0, 32), 32, ROPE_HALF, cos1, sin1)
            to_T(KD, lambda b, tt: z[:, tt, b * P:(b + 1) * P], lambda b, n: qT[:, b:b + n, :])
            to_T(KD, lambda b, tt: z[:, tt, D + b * P:D + (b + 1) * P], lambda b, n: kT[:, b:b + n, :])
            jobs = []
            for h in range(DIFF_H):
                for tt in range(TT):
                    n = (tt + 1) * P
                    for m in range(2):
                        b = HD * m
                        jobs.append(dict(qk=[(qT[b:b + HD, h, tt * P:(tt + 1) * P], kT[b:b + HD, h, 0:n])], n=n,
                                         bias=causal[:, tt, 0:n], scale=HD ** -0.5, dv=2 * HD,
                                         v=[z[:, kb, 2 * D + h * P:2 * D + (h + 1) * P] for kb in range(tt + 1)],
                                         out=o_buf[:, tt, h * P:(h + 1) * P], add=(m == 1),
                                         mul=neg_lam if m == 1 else None))
            attention(jobs)
            ov = o_buf[:, :, :].rearrange("p t (h w) -> p t h w", h=DIFF_H)
            rstd_heads(ov, rs[:, 2:2 + TT * DIFF_H], DIFF_H, P)
            scale_heads(ov, ov, rs[:, 2:2 + TT * DIFF_H], DIFF_H)
            c = col_of["subln"] % P
            to_T(KD, lambda b, tt: o_buf[:, tt, b * P:(b + 1) * P], hi_of(h_hi), dst_lo=hi_of(h_lo),
                 scale=lambda b: cols[:, 1, c:c + 1])
            gemm(h_in, KD, D, to_sbuf(lambda tt, c, n: o_buf[:, tt, c:c + n]))

        def memory_attention(l):
            W = MEM_H * HD
            c = col_of[("mem", l)]
            to_T(KD, lambda b, tt: gate[:, tt, b * P:(b + 1) * P], hi_of(h2_hi), dst_lo=hi_of(h2_lo),
                 scale=lambda b: cols[:, 0, c + b:c + b + 1])
            gemm(h2_in, KD, W, to_sbuf(lambda tt, c, n: z[:, tt, W + c:W + c + n], rs_of(28)))
            gemm(h2_in, KD, W, to_sbuf(lambda tt, c, n: z[:, tt, 2 * W + c:2 * W + c + n], rs_of(28)))
            pre_norm(x, col_of[("pre", l, 2)], rs[:, 0:2])
            gemm(h_in, KD, W, to_sbuf(lambda tt, c, n: z[:, tt, c:c + n], rs_of(0)))
            to_T(2, lambda b, tt: z[:, tt, b * P:(b + 1) * P], lambda b, n: qT[:, b:b + n, :])
            to_T(2, lambda b, tt: z[:, tt, W + b * P:W + (b + 1) * P], lambda b, n: kT[:, b:b + n, :])
            jobs = []
            for h in range(MEM_H):
                b = HD * (h % 2)
                for tt in range(TT):
                    jobs.append(dict(qk=[(qT[b:b + HD, h // 2, tt * P:(tt + 1) * P], kT[b:b + HD, h // 2, :])], n=T,
                                     bias=None, scale=HD ** -0.5, dv=HD,
                                     v=[z[:, kb, 2 * W + h * HD:2 * W + (h + 1) * HD] for kb in range(TT)],
                                     out=o_buf[:, tt, h * HD:(h + 1) * HD]))
            attention(jobs)
            to_T(2, lambda b, tt: o_buf[:, tt, b * P:(b + 1) * P], hi_of(h_hi), dst_lo=hi_of(h_lo))
            gemm(h_in, W // P, D, to_sbuf(lambda tt, c, n: o_buf[:, tt, c:c + n]))

        rstd_rows(gate, rs[:, 28:30])
        for l in range(DEPTH):
            g = load_gain(a["sandwich_g"][l, 1, :])
            if l % 2 == 0:
                even_mixer(g)
            else:
                diff_mixer()
            post_norm(o_buf, g)
            g = load_gain(a["sandwich_g"][l, 3, :])
            memory_attention(l)
            post_norm(o_buf, g)
            g = load_gain(a["sandwich_g"][l, 5, :])
            pre_norm(x, col_of[("pre", l, 4)], rs[:, 0:2])
            ffn(rs_of(0), finish_to_o)
            post_norm(o_buf, g)

        bias_h = [gain[:, i // 2, (i % 2) * 512:(i % 2 + 1) * 512].rearrange("p (t k) -> p t k", t=TT)
                  for i in range(4)]
        bias_free = [marks() for _ in range(4)]

        def load_bias(l, h):
            s = h % 4
            rows_n = T // GRID_W

            @block.sync
            def _(sp):
                sp.wait_ge(*table_landed.now())
                sp.wait_ge(*bias_free[s].dve)
                for qr in range(rows_n):
                    tt, part = qr // 2, (qr % 2) * GRID_W
                    first = ((l * NA_H + h) * GRID_W * TBL_W
                             + (NA_WIN_R - 1 - qr) * RPB_C + NA_WIN_C - 1 - TBL_LO)
                    src = bass.AP(tensor=table.tensor, offset=first,
                                  ap=[[TBL_W - 1, GRID_W], [RPB_C, rows_n], [1, GRID_W]])
                    sp.dma_start(bias_h[s][part:part + GRID_W, tt, :].rearrange("p (r c) -> p r c", r=rows_n),
                                 src).then_inc(*gain_landed[s].up(16))
            got = gain_landed[s].now()

            @block.gpsimd
            def _(pool):
                pool.wait_ge(*got)
                for tt in range(TT):
                    pool.tensor_tensor(bias_h[s][:, tt, :], bias_h[s][:, tt, :], C("na"), ALU.add).then_inc(
                        *pool_did.up())

        def silu_into(dst, src):
            @block.scalar
            def _(act):
                act.wait_ge(*pe_did.now())
                act.wait_ge(*act_did.now())
                act.wait_ge(*dve_did.now())
                act.wait_ge(*pool_did.now())
                act.activation(dst, src, ACT.Silu).then_inc(*act_did.up())

        def branch(i, y, scale=None):
            to_T(4, lambda b, tt: y[:, tt, b * P:(b + 1) * P], hi_of(h2_hi), dst_lo=hi_of(h2_lo), scale=scale)
            before = marks()


            def gates(tt, c, n, bank, full):
                @block.scalar
                def _(act):
                    act.wait_ge(*full)
                    act.wait_ge(*before.pe)
                    act.wait_ge(*before.act)
                    act.wait_ge(*before.dve)
                    act.wait_ge(*before.pool)
                    act.activation(gate[:, tt, c:c + n], bank.t[:, 0:n], ACT.Sigmoid,
                                   scale=rs[:, tt:tt + 1]).then_inc(*act_did.up())
                bank.drained = act_did.now()
            gemm(h_in, KD, D, gates)
            after = marks()

            def mix(tt, c, n, bank, full):
                @block.vector
                def _(dve):
                    dve.wait_ge(*full)
                    dve.wait_ge(*after.pe)
                    dve.wait_ge(*after.act)
                    dve.wait_ge(*after.dve)
                    dve.wait_ge(*after.pool)
                    dst = (o_buf if i == 0 else tmp)[:, tt, c:c + n]
                    dve.tensor_tensor(dst, bank.t[:, 0:n], gate[:, tt, c:c + n], ALU.mult).then_inc(*dve_did.up())
                bank.drained = dve_did.now()
                if i > 0:
                    @block.gpsimd
                    def _(pool):
                        pool.wait_ge(*dve_did.now())
                        mixed = o_buf[:, tt, c:c + n]
                        pool.tensor_tensor(mixed, mixed, tmp[:, tt, c:c + n], ALU.add).then_inc(*pool_did.up())
            gemm(h2_in, 4, D, mix)

        def neighborhood(l):
            for h in range(4):
                load_bias(l, h)
            for name, c, dstT in (("na_q_norm_2", ZC["naq"], qT), ("na_k_norm_2", ZC["nak"], kT)):
                v = heads_of(c, NA_H)
                r = rs[:, 2:2 + TT * NA_H]
                rstd_heads(v, r, NA_H, HD)
                scale_heads(v, v, r, NA_H)
                gc = col_of[(name, l)] % P
                to_T(4, lambda b, tt: z[:, tt, c + b * P:c + (b + 1) * P], lambda b, n: dstT[:, b:b + n, :],
                     scale=lambda b: cols[:, 1, gc:gc + 1])
            y = sq[:, :, 0:512]
            for half in range(2):
                jobs = []
                for h in range(4 * half, 4 * half + 4):
                    b = HD * (h % 2)
                    for tt in range(TT):
                        jobs.append(dict(qk=[(qT[b:b + HD, h // 2, tt * P:(tt + 1) * P], kT[b:b + HD, h // 2, :])],
                                         n=T, bias=bias_h[h % 4][:, tt, :], scale=HD ** -0.5, dv=HD,
                                         v=[z[:, kb, ZC["nav"] + h * HD:ZC["nav"] + (h + 1) * HD] for kb in range(TT)],
                                         out=y[:, tt, h * HD:(h + 1) * HD]))
                attention(jobs)
                for s in range(4):
                    bias_free[s] = marks()
                if half == 0:
                    for h in range(4, 8):
                        load_bias(l, h)
            branch(0, y)

        def gated_linear(l):
            NP2 = GLA_H // 2
            NCH = T // GLA_CHUNK
            dirs = (("gla_gf_up_2", "gla_gf_bias_2", ZC["gfl"]), ("gla_gb_up_2", "gla_gb_bias_2", ZC["gbl"]))
            lowT = kT[0:GLA_RANK + 1, 6:8, :]
            before = marks()

            @block.sync
            def _(sp):
                sp.wait_ge(*before.pe)
                sp.wait_ge(*before.act)
                sp.wait_ge(*before.dve)
                sp.wait_ge(*before.pool)
                for d, (w, b, _) in enumerate(dirs):
                    sp.dma_start(up[0:GLA_RANK, d, :], a[w][l]).then_inc(*misc_landed.up(16))
                    sp.dma_start(up[GLA_RANK:GLA_RANK + 1, d, :], a[b][l:l + 1, :]).then_inc(*misc_landed.up(16))

            @block.gpsimd
            def _(pool):
                pool.wait_ge(*before.pe)
                pool.wait_ge(*before.act)
                pool.wait_ge(*before.dve)
                pool.wait_ge(*before.pool)
                pool.memset(lowT, 1.0).then_inc(*pool_did.up())
            to_T(2, lambda d, tt: z[:, tt, dirs[d][2]:dirs[d][2] + GLA_RANK],
                 lambda d, n: kT[0:GLA_RANK, 6 + d:6 + d + n, :], width=GLA_RANK)
            got = misc_landed.now()
            g = tmp[:, :, 0:512]
            b_sum = sq[:, :, 0:512]
            to_end = sq[:, :, 512:1024]
            for tt in range(TT):
                bank = next_bank()

                @block.tensor
                def _(pe):
                    pe.wait_ge(*got)
                    pe.wait_ge(*bank.drained)
                    pe.wait_ge(*act_did.now())
                    pe.wait_ge(*dve_did.now())
                    pe.wait_ge(*pool_did.now())
                    for d in range(2):
                        m = pe.matmul(bank.t[:, d * T:(d + 1) * T], lowT[:, d, tt * P:(tt + 1) * P], up[:, d, :],
                                      start=True, stop=True)
                    m.then_inc(*pe_did.up())
                log_sigmoid(g[:, tt, :], bank.t[:, :], 512, b_sum[:, tt, :], to_end[:, tt, :])
                bank.drained = dve_did.now()
            before = marks()
            e_pos, e_neg, e_end = qT[:, 0:4, :], qT[:, 4:8, :], kT[:, 0:4, :]
            for tt in range(TT):
                for d in range(2):
                    bank = next_bank()

                    @block.tensor
                    def _(pe):
                        pe.wait_ge(*bank.drained)
                        pe.wait_ge(*before.act)
                        pe.wait_ge(*before.dve)
                        pe.wait_ge(*before.pool)
                        gd = g[:, tt, d * T:(d + 1) * T]
                        pe.matmul(bank.t[:, 0:T], C("tri_f" if d == 0 else "tri_b"), gd, start=True, stop=True)
                        m = pe.matmul(bank.t[:, T:2 * T], C("chunk_all"), gd, start=True, stop=True)
                        m.then_inc(*pe_did.up())
                    full = pe_did.now()
                    bs = b_sum[:, tt, d * T:(d + 1) * T]
                    te = to_end[:, tt, d * T:(d + 1) * T]
                    i = tt * 2 + d

                    @block.vector
                    def _(dve):
                        dve.wait_ge(*full)
                        dve.wait_ge(*before.pe)
                        dve.wait_ge(*before.act)
                        dve.wait_ge(*before.dve)
                        dve.wait_ge(*before.pool)
                        dve.tensor_copy(bs, bank.t[:, 0:T]).then_inc(*dve_did.up())
                        dve.wait_ge(*dve_did.now())
                        dve.tensor_tensor(te, bank.t[:, T:2 * T], bs, ALU.subtract).then_inc(*dve_did.up())

                    @block.scalar
                    def _(act):
                        act.wait_ge(*dve_did.now())
                        act.wait_ge(*before.pe)
                        act.wait_ge(*before.act)
                        act.wait_ge(*before.dve)
                        act.wait_ge(*before.pool)
                        act.activation(e_pos[:, i, :], bs, ACT.Exp).then_inc(*act_did.up())
                        act.activation(e_neg[:, i, :], bs, ACT.Exp, scale=-1.0).then_inc(*act_did.up())
                        act.activation(e_end[:, i, :], te, ACT.Exp).then_inc(*act_did.up())
                    bank.drained = dve_did.now()
            dec = stat[:, 0:16]
            bank = next_bank()

            @block.tensor
            def _(pe):
                pe.wait_ge(*bank.drained)
                pe.wait_ge(*before.act)
                pe.wait_ge(*before.dve)
                pe.wait_ge(*before.pool)
                for d in range(2):
                    for pr in range(NP2):
                        for tt in range(TT):
                            c = (d * NP2 + pr) * NCH + tt * 2
                            m = pe.matmul(bank.t[:, c:c + 2], g[:, tt, d * T + pr * P:d * T + (pr + 1) * P],
                                          C("chunk_of"), start=True, stop=True)
                m.then_inc(*pe_did.up())

            @block.scalar
            def _(act):
                act.wait_ge(*pe_did.now())
                act.wait_ge(*act_did.now())
                act.wait_ge(*dve_did.now())
                act.wait_ge(*pool_did.now())
                act.activation(dec, bank.t[:, 0:16], ACT.Exp).then_inc(*act_did.up())
            bank.drained = act_did.now()
            qe, ke, kend = tmp[:, :, 0:512], tmp[:, :, 512:1024], hT2[:, 0:4, :]
            before = marks()
            zq = lambda tt: z[:, tt, ZC["gq"]:ZC["gq"] + T]
            zk = lambda tt: z[:, tt, ZC["gk"]:ZC["gk"] + T]

            @block.vector
            def _(dve):
                dve.wait_ge(*before.pe)
                dve.wait_ge(*before.act)
                dve.wait_ge(*before.dve)
                dve.wait_ge(*before.pool)
                for tt in range(TT):
                    for d in range(2):
                        i = tt * 2 + d
                        dve.scalar_tensor_tensor(qe[:, tt, d * T:(d + 1) * T], zq(tt), GLA_DK ** -0.5, e_pos[:, i, :],
                                                 ALU.mult, ALU.mult).then_inc(*dve_did.up())
                        dve.tensor_tensor(ke[:, tt, d * T:(d + 1) * T], zk(tt), e_neg[:, i, :],
                                          ALU.mult).then_inc(*dve_did.up())

            @block.gpsimd
            def _(pool):
                pool.wait_ge(*before.pe)
                pool.wait_ge(*before.act)
                pool.wait_ge(*before.dve)
                pool.wait_ge(*before.pool)
                for tt in range(TT):
                    for d in range(2):
                        i = tt * 2 + d
                        pool.tensor_tensor(kend[:, i, :], zk(tt), e_end[:, i, :], ALU.mult).then_inc(*pool_did.up())
            qeT, keT = qT[:, 0:4, :], qT[:, 4:8, :]
            to_T(4, lambda b, tt: qe[:, tt, b * P:(b + 1) * P], lambda b, n: qT[:, b:b + n, :])
            to_T(4, lambda b, tt: ke[:, tt, b * P:(b + 1) * P], lambda b, n: qT[:, 4 + b:4 + b + n, :])
            aT = sq[:, :, :].rearrange("p t (d n) -> p t d n", d=2)

            @block.gpsimd
            def _(pool):
                pool.wait_ge(*pe_did.now())
                pool.wait_ge(*act_did.now())
                pool.wait_ge(*dve_did.now())
                pool.wait_ge(*pool_did.now())
                for tt in range(TT):
                    pool.memset(sq[:, tt, :], 0.0).then_inc(*pool_did.up())
            before = marks()
            for d in range(2):
                for par in range(2):
                    bank = next_bank()
                    r0 = par * HD

                    @block.tensor
                    def _(pe):
                        pe.wait_ge(*bank.drained)
                        pe.wait_ge(*before.act)
                        pe.wait_ge(*before.dve)
                        pe.wait_ge(*before.pool)
                        for tt in range(TT):
                            for pr in range(NP2):
                                ts_ = slice(tt * P, (tt + 1) * P)
                                c = (tt * NP2 + pr) * P
                                m = pe.matmul(bank.t[:, c:c + P], keT[r0:r0 + HD, d * 2 + pr, ts_],
                                              qeT[r0:r0 + HD, d * 2 + pr, ts_], start=True, stop=True)
                        m.then_inc(*pe_did.up())

                    @block.vector
                    def _(dve):
                        dve.wait_ge(*pe_did.now())
                        dve.wait_ge(*before.pe)
                        dve.wait_ge(*before.act)
                        dve.wait_ge(*before.dve)
                        dve.wait_ge(*before.pool)
                        keep = C("tri_f" if d == 0 else "strict_b").bitcast(I32)
                        for tt in range(TT):
                            dve.copy_predicated(
                                aT[:, tt, d, :].rearrange("p (r q n) -> p r q n", r=NP2, q=2)[:, :, par, :],
                                keep.unsqueeze(1).broadcast_to([P, NP2, P]),
                                bank.t[:, tt * T:(tt + 1) * T].rearrange("p (r n) -> p r n", r=NP2)).then_inc(
                                *dve_did.up())
                    bank.drained = dve_did.now()
            state = {}
            states = [kT[:, 2 * i:2 * i + 2, :] for i in range(4)] + [hT2[:, 4 + 2 * i:6 + 2 * i, :] for i in range(2)]

            @block.gpsimd
            def _(pool):
                pool.wait_ge(*pe_did.now())
                pool.wait_ge(*act_did.now())
                pool.wait_ge(*dve_did.now())
                pool.wait_ge(*pool_did.now())
                pool.memset(kT[:, :, :], 0.0).then_inc(*pool_did.up())
                pool.memset(hT2[:, 4:8, :], 0.0).then_inc(*pool_did.up())
            order = [(0, 0, 1, 0), (0, 1, 2, 1), (0, 2, 3, 2), (1, 3, 2, 3), (1, 2, 1, 4), (1, 1, 0, 5)]
            before = marks()
            for d, c, nxt, slot in order:
                tt, b0 = c // 2, GLA_CHUNK * (c % 2)
                bank = next_bank()

                @block.tensor
                def _(pe):
                    pe.wait_ge(*bank.drained)
                    pe.wait_ge(*before.act)
                    pe.wait_ge(*before.dve)
                    pe.wait_ge(*before.pool)
                    for pr in range(NP2):
                        m = pe.matmul(bank.t[:, pr * T:(pr + 1) * T],
                                      kend[b0:b0 + GLA_CHUNK, tt * 2 + d, pr * P:(pr + 1) * P],
                                      z[b0:b0 + GLA_CHUNK, tt, ZC["gv"] + pr * T:ZC["gv"] + (pr + 1) * T],
                                      start=True, stop=True)
                    m.then_inc(*pe_did.up())

                @block.vector
                def _(dve):
                    dve.wait_ge(*pe_did.now())
                    dve.wait_ge(*dve_did.now())
                    dve.wait_ge(*before.pe)
                    dve.wait_ge(*before.act)
                    dve.wait_ge(*before.dve)
                    dve.wait_ge(*before.pool)
                    for par in range(2):
                        ps = slice(par * HD, (par + 1) * HD)
                        for pr in range(NP2):
                            src = bank.t[ps, pr * T + par * P:pr * T + (par + 1) * P]
                            at = (ps, pr, slice(par * P, (par + 1) * P))
                            if (d, c) not in state:
                                dve.tensor_copy(states[slot][at], src).then_inc(*dve_did.up())
                            else:
                                col = (d * NP2 + pr) * NCH + c
                                dve.scalar_tensor_tensor(states[slot][at], states[state[(d, c)]][at],
                                                         dec[ps, col:col + 1], src, ALU.mult,
                                                         ALU.add).then_inc(*dve_did.up())
                bank.drained = dve_did.now()
                state[(d, nxt)] = slot
            before = marks()
            og = tmp[:, :, 0:512]
            for tt in range(TT):
                bank = next_bank()

                @block.tensor
                def _(pe):
                    pe.wait_ge(*bank.drained)
                    pe.wait_ge(*before.act)
                    pe.wait_ge(*before.dve)
                    pe.wait_ge(*before.pool)
                    for h in range(GLA_H):
                        vh = z[:, tt, ZC["gv"] + h * P:ZC["gv"] + (h + 1) * P]
                        for d in range(2):
                            m = pe.matmul(bank.t[:, h * P:(h + 1) * P], aT[:, tt, d, h * P:(h + 1) * P], vh,
                                          start=(h == 0 and d == 0), stop=False, skip_group_check=True)
                    for pr in range(NP2):
                        inter = [(d, c) for c in (2 * tt, 2 * tt + 1) for d in range(2) if (d, c) in state]
                        for n, (d, c) in enumerate(inter):
                            r0 = GLA_CHUNK * (c % 2)
                            m = pe.matmul(bank.t[r0:r0 + GLA_CHUNK, pr * T:(pr + 1) * T],
                                          qeT[:, d * 2 + pr, c * GLA_CHUNK:(c + 1) * GLA_CHUNK],
                                          states[state[(d, c)]][:, pr, :],
                                          start=False, stop=(n == len(inter) - 1), skip_group_check=True)
                    m.then_inc(*pe_did.up())

                @block.vector
                def _(dve):
                    dve.wait_ge(*pe_did.now())
                    dve.wait_ge(*before.pe)
                    dve.wait_ge(*before.act)
                    dve.wait_ge(*before.dve)
                    dve.wait_ge(*before.pool)
                    dve.tensor_copy(og[:, tt, :], bank.t[:, :]).then_inc(*dve_did.up())
                bank.drained = dve_did.now()
            ov = og.rearrange("p t (h w) -> p t h w", h=GLA_H)
            r = rs[:, 2:2 + TT * GLA_H]
            rstd_heads(ov, r, GLA_H, GLA_DV)
            scale_heads(ov, ov, r, GLA_H)
            gr = z[:, :, ZC["gr"]:ZC["gr"] + 512]
            silu_into(gr, gr)

            @block.vector
            def _(dve):
                dve.wait_ge(*pe_did.now())
                dve.wait_ge(*act_did.now())
                dve.wait_ge(*dve_did.now())
                dve.wait_ge(*pool_did.now())
                dve.tensor_tensor(og, og, gr, ALU.mult).then_inc(*dve_did.up())
            gc = col_of[("gla_out", l)] % P
            branch(1, og, scale=lambda b: cols[:, 1, gc:gc + 1])

        def latent(l):
            q = z[:, :, 0:MLA_H * MLA_QK]
            kv = z[:, :, ZC["gq"]:ZC["gq"] + MLA_H * (MLA_NOPE + MLA_V)]
            for name, c, width, dst in (("cq", ZC["cq"], MLA_H * MLA_QK, q),
                                        ("ckv", ZC["ckv"], MLA_H * (MLA_NOPE + MLA_V), kv)):
                v = z[:, :, c:c + 2 * P].unsqueeze(2)
                rstd_heads(v, rs[:, 2:4], 1, 2 * P)
                gc = col_of[(name, l)] % P
                to_T(2, lambda b, tt: z[:, tt, c + b * P:c + (b + 1) * P], hi_of(h2_hi), dst_lo=hi_of(h2_lo),
                     scale=lambda b: cols[:, 1, gc + b:gc + b + 1])
                gemm(h2_in, 2, width,
                     to_sbuf(lambda tt, c_, n: dst[:, tt, c_:c_ + n], rs_of(2)))
            qv = q.rearrange("p t (h w) -> p t h w", h=MLA_H)
            kvv = kv.rearrange("p t (h w) -> p t h w", h=MLA_H)
            kf = tmp[:, :, 0:MLA_H * MLA_QK]
            kfv = kf.rearrange("p t (h w) -> p t h w", h=MLA_H)
            before = marks()

            @block.gpsimd
            def _(pool):
                pool.wait_ge(*before.pe)
                pool.wait_ge(*before.act)
                pool.wait_ge(*before.dve)
                pool.wait_ge(*before.pool)
                for tt in range(TT):
                    pool.tensor_copy(kfv[:, tt, :, 0:MLA_NOPE], kvv[:, tt, :, 0:MLA_NOPE]).then_inc(*pool_did.up())
                    pool.tensor_copy(kfv[:, tt, :, MLA_NOPE:MLA_QK],
                                     z[:, tt, ZC["kr"]:ZC["kr"] + MLA_ROPE].unsqueeze(1).broadcast_to(
                                         [P, MLA_H, MLA_ROPE])).then_inc(*pool_did.up())
            for m, (v, name, buf, dstT) in enumerate(((qv, "mla_q", q, qT), (kfv, "mla_k", kf, kT))):
                r = rs[:, 2:2 + TT * MLA_H]
                rstd_heads(v, r, MLA_H, MLA_QK)
                scale_heads(v, v, r, MLA_H)
                rot = v[:, :, :, MLA_NOPE:MLA_QK]

                @block.vector
                def _(dve):
                    dve.wait_ge(*pe_did.now())
                    dve.wait_ge(*act_did.now())
                    dve.wait_ge(*dve_did.now())
                    dve.wait_ge(*pool_did.now())
                    for tt in range(TT):
                        dve.tensor_tensor(rot[:, tt], rot[:, tt],
                                          rgain[:, l * 2 + m, :].unsqueeze(1).broadcast_to([P, MLA_H, MLA_ROPE]),
                                          ALU.mult).then_inc(*dve_did.up())
                rotate(rot, MLA_H, MLA_ROPE // 2, C("cos2", (TT,)), C("sin2", (TT,)))
                gc = col_of[(name, l)] % P
                to_T(MLA_H, lambda h, tt: v[:, tt, h, 0:MLA_NOPE], lambda b, n: dstT[:, b:b + n, :],
                     scale=lambda b: cols[:, 1, gc:gc + 1])
                to_T(MLA_H, lambda h, tt: v[:, tt, h, MLA_NOPE:MLA_QK], lambda b, n: dstT[0:MLA_ROPE, 4 + b:4 + b + n, :],
                     width=MLA_ROPE)
            y = sq[:, :, 0:512]
            jobs = []
            for h in range(MLA_H):
                for tt in range(TT):
                    ts_ = slice(tt * P, (tt + 1) * P)
                    jobs.append(dict(qk=[(qT[:, h, ts_], kT[:, h, :]),
                                         (qT[0:MLA_ROPE, 4 + h, ts_], kT[0:MLA_ROPE, 4 + h, :])],
                                     n=T, bias=None, scale=MLA_QK ** -0.5, dv=MLA_V,
                                     v=[kvv[:, kb, h, MLA_NOPE:MLA_NOPE + MLA_V] for kb in range(TT)],
                                     out=y[:, tt, h * P:(h + 1) * P]))
            attention(jobs)
            branch(2, y)

        def add_x(tt, c, n, bank, full):
            @block.vector
            def _(dve):
                dve.wait_ge(*full)
                dve.wait_ge(*pe_did.now())
                dve.wait_ge(*act_did.now())
                dve.wait_ge(*dve_did.now())
                dve.wait_ge(*pool_did.now())
                xs = x[:, tt, c:c + n]
                dve.tensor_tensor(xs, xs, bank.t[:, 0:n], ALU.add).then_inc(*dve_did.up())
            bank.drained = dve_did.now()

        for l in range(DEPTH):
            pre_norm(x, col_of[("ffn1_norm_2", l)], rs[:, 0:2])
            ffn(rs_of(0), add_half)
            pre_norm(x, col_of[("mix_norm_2", l)], rs[:, 0:2])
            gemm(h_in, KD, ZC["gates"], to_sbuf(lambda tt, c, n: z[:, tt, c:c + n], rs_of(0)))
            neighborhood(l)
            gated_linear(l)
            latent(l)
            to_T(KD, lambda b, tt: o_buf[:, tt, b * P:(b + 1) * P], hi_of(h_hi), dst_lo=hi_of(h_lo))
            gemm(h_in, KD, D, add_x)
            pre_norm(x, col_of[("ffn2_norm_2", l)], rs[:, 0:2])
            ffn(rs_of(0), add_half)

        @block.sync
        def _(sp):
            sp.wait_ge(*pe_did.now())
            sp.wait_ge(*act_did.now())
            sp.wait_ge(*dve_did.now())
            sp.wait_ge(*pool_did.now())
            sp.dma_start(out[0].rearrange("(t p) d -> p t d", p=P), x[:, :, :]).then_inc(*out_landed.up(16))
            sp.wait_ge(*out_landed.now())


def kernel(**inputs):
    from concourse import bacc
    from concourse.bass_utils import run_bass_kernel_spmd

    nc = bacc.Bacc("TRN2", target_bir_lowering=False, num_devices=1)
    arrays, aps = {}, {}
    const, early, where = constants()
    for name, value in {**inputs, "const": const, "early": early}.items():
        v = np.ascontiguousarray(value)
        arrays[f"in_{name}"] = v
        aps[name] = nc.dram_tensor(f"in_{name}", v.shape, mybir.dt.from_np(v.dtype), kind="ExternalInput").ap()
    out = nc.dram_tensor("out_0", (1, T, D), F32, kind="ExternalOutput").ap()
    program(nc, aps, where, out)
    r = run_bass_kernel_spmd(nc, [arrays], core_ids=[0])
    return r.results[0]["out_0"]
```

```python
import math
from collections import namedtuple
from contextlib import ExitStack

import numpy as np
import concourse.bass as bass
from concourse import mybir

F32 = mybir.dt.float32
F32R = mybir.dt.float32r
I32 = mybir.dt.int32
ALU = mybir.AluOpType
ACT = mybir.ActivationFunctionType
AX = mybir.AxisListType

P = 128
T = 256
TT = T // P
D = 1024
KD = D // P
HD = 64
EPS = 1e-6
NEG = -1e30

ROPE_HALF = HD // 8
ROPE_THETA = 500000.0
FOX_H = 8
NSA_H = 8
CMP_BLOCK, CMP_STRIDE = 32, 16
NC = (T - CMP_BLOCK) // CMP_STRIDE + 1
D_FF = 2816
MEM_H = 4
DIFF_H = 8
LAM_INIT = 0.8 - 0.6 * math.exp(-0.3 * 1)
DEPTH = 2
EV, at = {}, 0
for _name, _w in (("fq", 512), ("fk", 512), ("fv", 512), ("fl", 8), ("nq", 512), ("kc", 128), ("vc", 128),
                  ("ks", 128), ("vs", 128), ("kw", 128), ("vw", 128), ("gl", 24)):
    EV[_name] = at
    at += _w
EV_IN = at
EV_STARTS = (2560, 1536, 2048, 0, 512, 1024)

GRID_W = 64
NA_H = 8
NA_WIN_R, NA_WIN_C = 8, 16
RPB_R, RPB_C = 2 * NA_WIN_R - 1, 2 * NA_WIN_C - 1
GLA_H, GLA_DK, GLA_DV, GLA_CHUNK, GLA_RANK, GLA_TAU = 4, 64, 128, 64, 16, 16.0
MLA_H, MLA_NOPE, MLA_ROPE, MLA_V = 4, 128, 64, 128
MLA_QK = MLA_NOPE + MLA_ROPE
ROPE_THETA_2 = 10000.0
ZC, at = {}, 0
for _name, _w in (("naq", 512), ("nak", 512), ("nav", 512), ("gq", 256), ("gk", 256), ("gv", 512), ("gr", 512),
                  ("gfl", 16), ("gbl", 16), ("cq", 256), ("ckv", 256), ("kr", 64), ("gates", 3 * D)):
    ZC[_name] = at
    at += _w

IN_STARTS = (0, 512, 3072, 3584, 1536, 2048, 2560, 1024)

TBL_LO = (NA_WIN_R - T // GRID_W) * RPB_C + NA_WIN_C - 1 - (GRID_W - 1)
TBL_HI = (NA_WIN_R - 2 + T // GRID_W) * RPB_C + NA_WIN_C - 1 + GRID_W
TBL_W = TBL_HI - TBL_LO

SLOT = 2048
RAW_SLOTS = 6
HI_SLOTS = 3
FF_CHUNK = 256
ATT_SLOTS = 4
PREPARE_AT = 3
PIECES = 4
GLA_FILLS = (1, 2, 4, 1, 2)
MLA_FILLS = (2, 0, 2, 0)


def constants():
    p = np.arange(P)
    t = np.arange(T)
    parts = {}
    parts["ident"] = np.eye(P)
    parts["minus_half"] = np.full((P, 16), -0.5)
    parts["one"] = np.ones((P, 1))
    tok = np.arange(TT)[:, None] * P + p[None, :]
    parts["causal"] = np.where(t[None, None, :] <= tok.T[:, :, None], 0.0, NEG)
    cmp_end = np.arange(NC) * CMP_STRIDE + CMP_BLOCK - 1
    parts["cmp"] = np.where(cmp_end[None, None, :] <= tok.T[:, :, None], 0.0, NEG)
    qc = p % GRID_W
    kc = t % GRID_W
    c0 = np.clip(qc - NA_WIN_C // 2, 0, GRID_W - NA_WIN_C)
    parts["na"] = np.where((kc[None] >= c0[:, None]) & (kc[None] < c0[:, None] + NA_WIN_C), 0.0, NEG)
    early = {}
    early["upto"] = (tok.T[:, :, None] <= t[None, None, :]) * 1.0
    early["shift"] = (tok.T[:, :, None] == t[None, None, :] + 1) * 1.0
    same = (p[:, None] // GLA_CHUNK) == (p[None, :] // GLA_CHUNK)
    parts["tri_f"] = (same & (p[:, None] <= p[None, :])) / GLA_TAU
    parts["tri_b"] = (same & (p[:, None] >= p[None, :])) / GLA_TAU
    parts["strict_b"] = (same & (p[:, None] > p[None, :])) * 1.0
    parts["chunk_all"] = same / GLA_TAU
    parts["chunk_of"] = ((p[:, None] // GLA_CHUNK) == np.arange(P // GLA_CHUNK)[None, :]) / GLA_TAU
    half = MLA_ROPE // 2
    inv2 = (np.float32(ROPE_THETA_2) ** (-np.arange(half, dtype=np.float32) / np.float32(half))).astype(np.float32)
    ang = tok.T[:, :, None].astype(np.float32) * inv2
    parts["cos2"] = np.cos(ang.astype(np.float64))
    parts["sin2"] = np.sin(ang.astype(np.float64))
    inv = np.float32(ROPE_THETA) ** (-np.arange(0, 2 * ROPE_HALF, 2, dtype=np.float32) / np.float32(2 * ROPE_HALF))
    parts["inv"] = np.broadcast_to(inv[None, :], (P, ROPE_HALF))
    where, arrays = {}, []
    for group in (parts, early):
        cols, c = [], 0
        for name, a in group.items():
            a = np.ascontiguousarray(a, dtype=np.float32).reshape(P, -1)
            where[name] = (c, a.shape[1])
            cols.append(a)
            c += a.shape[1]
        arrays.append(np.concatenate(cols, axis=1))
    return (*arrays, where)


def small_arrays(inputs):
    tiles, at_, row_of = [[], []], [0, 0], {}

    def row(name, values, tile):
        r = np.asarray(values).reshape(-1, P)
        tiles[tile].append(r)
        row_of[name] = tile * P + at_[tile]
        at_[tile] += r.shape[0]
    for l in range(DEPTH):
        for g in (0, 2, 4):
            row(("pre", l, g), inputs["sandwich_g"][l, g], 0)
        row(("mem", l), inputs["mem_norm_g"][l], 0)
        for name in ("ffn1_norm_2", "mix_norm_2", "ffn2_norm_2"):
            row((name, l), inputs[name][l], 0)
    for name in ("ev_cmp_pos_k", "ev_cmp_pos_v"):
        row(name, inputs[name][0], 1)
    row("subln", inputs["od_subln_g"][0], 1)
    for l in range(DEPTH):
        row(("gla_out", l), inputs["gla_out_norm_2"][l], 1)
        row(("cq", l), inputs["mla_cq_norm_2"][l], 1)
        row(("ckv", l), inputs["mla_ckv_norm_2"][l], 1)
        row(("mla_q", l), inputs["mla_q_norm_2"][l, 0:P], 1)
        row(("mla_k", l), inputs["mla_k_norm_2"][l, 0:P], 1)
        for name in ("na_q_norm_2", "na_k_norm_2"):
            row((name, l), np.concatenate([inputs[name][l], inputs[name][l]]), 1)
    for t, n in zip(tiles, at_):
        t.append(np.zeros((P - n, P), np.float32))
    rows = np.stack([np.concatenate(t) for t in tiles], axis=1)
    vec = np.concatenate([np.asarray(inputs["ev_fox_fbias"][0]), np.asarray(inputs["od_lambda"][0]).reshape(-1)]
                         + [np.asarray(inputs[n][l, P:MLA_QK]) for l in range(DEPTH)
                            for n in ("mla_q_norm_2", "mla_k_norm_2")])
    return rows, vec, row_of




class Signal:

    def __init__(self, sem):
        self.sem, self.n = sem, 0

    def up(self, k=1):
        self.n += k
        return self.sem, k

    def now(self):
        return self.sem, self.n


Marks = namedtuple("Marks", "pe act dve pool")


class Bank:

    def __init__(self, tensor, start):
        self.t, self.drained = tensor, start
        self.held = False


class Ready:

    def __init__(self, groups, n, rest=None):
        self.groups, self.n, self.rest = groups, n, rest

    def upto(self, k):
        return self.groups[min((k - 1) // self.n, len(self.groups) - 1)]

    def have(self, k):
        if self.rest is not None and k > len(self.groups) * self.n:
            rest, self.rest = self.rest, None
            self.groups += rest()


class Unit:

    def __init__(self, shape, parts, split=True):
        self.shape, self.parts, self.split = shape, parts, split
        self.used = self.landed = None


def gemm_units(W, lo, hi):
    units = []
    nk = W.shape[0] // P
    for c in range(lo, hi, 512):
        n = min(512, hi - c)
        kk = nk
        while kk * n > SLOT:
            kk //= 2
        for k0 in range(0, nk, kk):
            src = W[k0 * P:(k0 + kk) * P, c:c + n].rearrange("(k p) n -> p k n", p=P)
            units.append(Unit((kk, n), lambda v, src=src: [(v, src)]))
    return units


def ffn_units(wg, wu, wd):
    units = []
    chunks = wd.shape[0] // FF_CHUNK
    for c in range(chunks + 1):
        if c < chunks:
            for k0 in range(0, KD, KD // 2):
                src = [w[k0 * P:(k0 + KD // 2) * P, c * FF_CHUNK:(c + 1) * FF_CHUNK].rearrange(
                    "(k p) n -> p k n", p=P) for w in (wg, wu)]
                units.append(Unit((KD // 2, 2 * FF_CHUNK), lambda v, src=src: [
                    (v[:, :, 0:FF_CHUNK], src[0]), (v[:, :, FF_CHUNK:2 * FF_CHUNK], src[1])]))
        if c >= 1:
            src = wd[(c - 1) * FF_CHUNK:c * FF_CHUNK, :].rearrange("(k p) n -> p k n", p=P)
            units.append(Unit((FF_CHUNK // P, D), lambda v, src=src: [(v, src)]))
    return units


def weight_stream(a):
    units = []
    for l in range(DEPTH):
        if l % 2 == 0:
            for c in EV_STARTS:
                units += gemm_units(a["ev_w_in"][0], c, min(c + 512, EV_IN))
            for m in "kv":
                w1 = a[f"ev_cmp_w1_{m}"][0].rearrange("(k p) n -> p k n", p=P)
                w2 = a[f"ev_cmp_w2_{m}"][0].unsqueeze(1)
                units.append(Unit((CMP_BLOCK // 2, P), lambda v, w1=w1: [(v, w1)], split=False))
                units.append(Unit((1, 2 * HD), lambda v, w2=w2: [(v[:, :, 0:HD], w2), (v[:, :, HD:2 * HD], w2)],
                                  split=False))
            units += gemm_units(a["ev_w_out"][0], 0, D)
        else:
            units += gemm_units(a["od_w_in"][0], 0, 3 * D)
            units += gemm_units(a["od_w_out"][0], 0, D)
        for name in ("ca_wk", "ca_wv", "ca_wq", "ca_wo"):
            units += gemm_units(a[name][l], 0, a[name].shape[2])
        units += ffn_units(a["ffn_wg"][l], a["ffn_wu"][l], a["ffn_wd"][l])
    for l in range(DEPTH):
        w_in = a["w_in_2"][l]
        gates = [gemm_units(w_in, ZC["gates"] + i * D, ZC["gates"] + (i + 1) * D) for i in range(3)]
        units += ffn_units(a["ffn1_w1_2"][l], a["ffn1_w3_2"][l], a["ffn1_w2_2"][l])
        for c in IN_STARTS:
            units += gemm_units(w_in, c, min(c + 512, ZC["gates"]))
        units += gates[0] + gemm_units(a["w_br_na_2"][l], 0, D)
        units += gates[1] + gemm_units(a["w_br_gla_2"][l], 0, D)
        units += gemm_units(a["mla_w_uq_2"][l], 0, MLA_H * MLA_QK)
        units += gemm_units(a["mla_w_ukv_2"][l], 0, MLA_H * (MLA_NOPE + MLA_V))
        units += gates[2] + gemm_units(a["w_br_mla_2"][l], 0, D)
        units += gemm_units(a["w_out_2"][l], 0, D)
        units += ffn_units(a["ffn2_w1_2"][l], a["ffn2_w3_2"][l], a["ffn2_w2_2"][l])
    return units


def program(nc, a, const_where, col_of, out):
    ctx = ExitStack()
    with ctx:
        place = {"next": -(-nc.sbuf_base // 32) * 32}

        def sb(name, shape, dt=F32, over=None):
            size = -(-int(np.prod(shape[1:])) * 4 // 32) * 32
            if over is None:
                place[name] = place["next"]
                place["next"] += size
            else:
                place[name] = place[over[0]] + 4 * over[1]
            return nc.alloc_sbuf_tensor_at(name, shape, dt, offset=place[name])

        def signal(name):
            return Signal(ctx.enter_context(nc.semaphore(name)))

        CONST_N = a["const"].shape[1]
        const = sb("const", [P, CONST_N])
        x = sb("x", [P, TT, D])
        h_hi = sb("h_hi", [P, KD, T], F32R)
        h_lo = sb("h_lo", [P, KD, T], F32R)
        hT2 = sb("hT2", [P, KD, T])
        o_buf = sb("o_buf", [P, TT, D])
        early = sb("early", [P, a["early"].shape[1]], over=("o_buf", 0))
        sq = sb("sq", [P, TT, D])
        z = sb("z", [P, TT, ZC["gates"]])
        FF_N = 2 * TT * FF_CHUNK
        ff_hid = sb("ff_hid", [P, 2, TT, FF_CHUNK], over=("z", 0))
        ff_silu = sb("ff_silu", [P, 2, TT, FF_CHUNK], over=("z", FF_N))
        ff_hi = sb("ff_hi", [P, 2, FF_CHUNK // P, T], F32R, over=("z", 2 * FF_N))
        ff_lo = sb("ff_lo", [P, 2, FF_CHUNK // P, T], F32R, over=("z", 3 * FF_N))
        gate = sb("gate", [P, TT, D])
        qT = sb("qT", [P, KD, T])
        kT = sb("kT", [P, KD, T])
        h2_hi = sb("h2_hi", [P, KD, T], F32R, over=("qT", 0))
        h2_lo = sb("h2_lo", [P, KD, T], F32R, over=("kT", 0))
        y_hi = sb("y_hi", [P, KD // 2, T], F32R, over=("hT2", 0))
        y_lo = sb("y_lo", [P, KD // 2, T], F32R, over=("hT2", KD // 2 * T))
        tmp = sb("tmp", [P, TT, D])
        raw = sb("raw", [P, RAW_SLOTS, SLOT])
        w_lo = sb("w_lo", [P, RAW_SLOTS, SLOT], F32R, over=("raw", 0))
        w_hi = sb("w_hi", [P, HI_SLOTS, SLOT], F32R)
        gain = sb("gain", [P, TT, D])
        smask = sb("smask", [P, ATT_SLOTS, T])
        probs = sb("probs", [P, ATT_SLOTS, T], over=("tmp", 0))
        pT = sb("pT", [P, ATT_SLOTS, TT, P], over=("tmp", ATT_SLOTS * T))
        rows = sb("rows", [P, 2, P], over=("sq", 0))
        cols = sb("cols", [P, 2, P])
        stat = sb("stat", [P, 64])
        rs = sb("rs", [P, 32])
        jobstat = sb("jobstat", [P, 8, 4])
        rope = sb("rope", [P, 6, TT, ROPE_HALF])
        small = sb("small", [P, 128])
        up = sb("up", [GLA_RANK + 1, 2, T])
        posi = sb("posi", [P, TT], I32)
        vec = sb("vec", [P, FOX_H + 4 * HD + 4 * MLA_ROPE])
        rgain = vec[:, FOX_H + 4 * HD:].rearrange("p (a b) -> p a b", a=4)

        pe_did = signal("pe_did")
        act_did = signal("act_did")
        dve_did = signal("dve_did")
        pool_did = signal("pool_did")
        const_landed = signal("const_landed")
        more_landed = signal("more_landed")
        late_landed = signal("late_landed")
        gain_landed = [signal(f"gain_landed{i}") for i in range(4)]
        slot_landed = [signal(f"slot_landed{i}") for i in range(RAW_SLOTS)]
        out_landed = signal("out_landed")
        misc_landed = signal("misc_landed")
        units = weight_stream(a)
        split_units = [u for u in units if u.split]
        banks = [Bank(ctx.enter_context(nc.psum_tensor(f"bank{i}", [P, 512], F32)), dve_did.now()) for i in range(8)]
        turn = {"bank": 0, "evac": 0, "gain": 0, "taken": 0, "loaded": 0, "parted": 0,
                "normed": pool_did.now(), "under way": iter(())}

        block = ctx.enter_context(nc.Block())

        def C(name, shape=None, rows_=P):
            c, w = const_where[name]
            v = (early if name in ("upto", "shift") else const)[0:rows_, c:c + w]
            return v if shape is None else v.rearrange("p (a b) -> p a b", a=shape[0])

        ident = C("ident")

        def marks():
            return Marks(pe_did.now(), act_did.now(), dve_did.now(), pool_did.now())

        def next_bank():
            while banks[turn["bank"] % 8].held:
                turn["bank"] += 1
            b = banks[turn["bank"] % 8]
            turn["bank"] += 1
            return b

        fillers = []

        def fill(n=1):
            while n > 0 and fillers:
                if next(fillers[0], None) is None:
                    fillers.pop(0)
                else:
                    n -= 1


        def load(i):
            u = units[i]
            n = u.shape[0] * u.shape[1]
            slot = i % RAW_SLOTS
            u.raw = raw[:, slot, 0:n].rearrange("p (a b) -> p a b", a=u.shape[0])
            u.lo = w_lo[:, slot, 0:n].rearrange("p (a b) -> p a b", a=u.shape[0])

            @block.sync
            def _(sp):
                if i >= RAW_SLOTS:
                    sp.wait_ge(*units[i - RAW_SLOTS].used)
                for dst, src in u.parts(u.raw):
                    sp.dma_start(dst, src).then_inc(*slot_landed[slot].up(16))
            u.landed = slot_landed[slot].now()

        def part(i, pieces=1):
            u = split_units[i]
            n = u.shape[0] * u.shape[1]
            hi = w_hi[:, i % HI_SLOTS, 0:n]
            u.hi = hi.rearrange("p (a b) -> p a b", a=u.shape[0])
            raw_, lo_ = (v.rearrange("p a b -> p (a b)") for v in (u.raw, u.lo))
            for p0 in range(0, n, n // pieces):
                cs = slice(p0, p0 + n // pieces)

                @block.scalar
                def _(act):
                    act.wait_ge(*u.landed)
                    if i >= HI_SLOTS:
                        act.wait_ge(*split_units[i - HI_SLOTS].used)
                    act.copy(hi[:, cs], raw_[:, cs]).then_inc(*act_did.up())

                @block.vector
                def _(dve):
                    dve.wait_ge(*act_did.now())
                    dve.tensor_tensor(lo_[:, cs], raw_[:, cs], hi[:, cs].bitcast(F32), ALU.subtract).then_inc(
                        *dve_did.up())
                u.parted = dve_did.now()
                yield True

        def load_ahead():
            while turn["loaded"] < RAW_SLOTS:
                load(turn["loaded"])
                turn["loaded"] += 1

        def prepare_steps(pieces=1):
            def free(of, n, slots):
                return n < len(of) and (n < slots or of[n - slots].used is not None)
            while free(units, turn["loaded"], RAW_SLOTS):
                load(turn["loaded"])
                turn["loaded"] += 1
            while free(split_units, turn["parted"], HI_SLOTS) and split_units[turn["parted"]].landed is not None:
                turn["parted"] += 1
                yield from part(turn["parted"] - 1, pieces)

        def prepare():
            for steps in (turn["under way"], prepare_steps()):
                for _ in steps:
                    pass

        def take():
            prepare()
            i = turn["taken"]
            turn["taken"] += 1
            return units[i]

        def to_T(nblk, src, dst, width=P, scale=None, group=2, dst_lo=None, ready=None, fills=0, after=None):
            before = marks() if after is None else after
            groups = []
            fill(fills)
            for b0 in range(0, nblk, group):
                n = min(group, nblk - b0)
                bank = next_bank()

                @block.tensor
                def _(pe):
                    pe.wait_ge(*bank.drained)
                    if ready is not None:
                        pe.wait_ge(*ready(b0))
                    elif b0 == 0:
                        pe.wait_ge(*before.act)
                        pe.wait_ge(*before.dve)
                        pe.wait_ge(*before.pool)
                    for b in range(n):
                        for tt in range(TT):
                            m = pe.transpose(bank.t[0:width, (b * TT + tt) * P:(b * TT + tt + 1) * P],
                                             src(b0 + b, tt), ident)
                    m.then_inc(*pe_did.up())
                full = pe_did.now()
                ps = bank.t[0:width, 0:n * T].rearrange("p (a b) -> p a b", a=n)
                turn["evac"] += 1
                if turn["evac"] % 2 and dst_lo is None:
                    @block.vector
                    def _(dve):
                        dve.wait_ge(*full)
                        if b0 < 2 * group:
                            dve.wait_ge(*before.act)
                            dve.wait_ge(*before.dve)
                            dve.wait_ge(*before.pool)
                        if scale is None:
                            dve.tensor_copy(dst(b0, n), ps).then_inc(*dve_did.up())
                        else:
                            for b in range(n):
                                dve.tensor_scalar(dst(b0 + b, 1), ps[:, b:b + 1, :], scale(b0 + b), None,
                                                  ALU.mult).then_inc(*dve_did.up())
                    bank.drained = dve_did.now()
                    groups.append(marks())
                    continue

                @block.scalar
                def _(act):
                    act.wait_ge(*full)
                    if b0 < 2 * group:
                        act.wait_ge(*before.act)
                        act.wait_ge(*before.dve)
                        act.wait_ge(*before.pool)
                    if scale is None:
                        act.copy(dst(b0, n), ps).then_inc(*act_did.up())
                    else:
                        for b in range(n):
                            act.activation(dst(b0 + b, 1), ps[:, b:b + 1, :], ACT.Copy,
                                           scale=scale(b0 + b)).then_inc(*act_did.up())
                bank.drained = act_did.now()
                if dst_lo is None:
                    groups.append(marks())
                    continue

                @block.vector
                def _(dve):
                    dve.wait_ge(*act_did.now())
                    if scale is None:
                        dve.tensor_tensor(dst_lo(b0, n), ps, dst(b0, n).bitcast(F32),
                                          ALU.subtract).then_inc(*dve_did.up())
                    else:
                        for b in range(n):
                            dve.scalar_tensor_tensor(dst_lo(b0 + b, 1), ps[:, b:b + 1, :], scale(b0 + b),
                                                     dst(b0 + b, 1).bitcast(F32), ALU.mult,
                                                     ALU.subtract).then_inc(*dve_did.up())
                bank.drained = dve_did.now()
                groups.append(marks())
            return Ready(groups, group)

        def three_products(pe, out, x_hi, x_lo, u, k, cols_, start, stop):
            pe.matmul(out, x_hi, u.hi[:, k, cols_], start=start, stop=False)
            pe.matmul(out, x_hi, u.lo[:, k, cols_], start=False, stop=False)
            return pe.matmul(out, x_lo, u.hi[:, k, cols_], start=False, stop=stop)

        def gemm_steps(h, nk, width, evac, ready, starts=None):
            if isinstance(ready, Marks):
                ready = Ready([ready], nk)
            starts = starts or range(0, width, 512)
            for c in starts:
                n = min(512, width - c)
                pair = [next_bank() for _ in range(TT)]
                for bank in pair:
                    bank.held = True
                k0 = 0
                while k0 < nk:
                    ready.have(k0 + units[turn["taken"]].shape[0])
                    u = take()
                    assert u.shape[1] == n
                    there = ready.upto(k0 + u.shape[0])

                    @block.tensor
                    def _(pe):
                        if c == starts[0]:
                            pe.wait_ge(*there.act)
                            pe.wait_ge(*there.dve)
                        if k0 == 0:
                            for bank in pair:
                                pe.wait_ge(*bank.drained)
                        pe.wait_ge(*u.parted)
                        for tt in range(TT):
                            ts_ = slice(tt * P, (tt + 1) * P)
                            for k in range(u.shape[0]):
                                m = three_products(pe, pair[tt].t[:, 0:n], h[0][:, k0 + k, ts_], h[1][:, k0 + k, ts_],
                                                   u, k, slice(0, n), k0 + k == 0, k0 + k == nk - 1)
                        m.then_inc(*pe_did.up())
                    u.used = pe_did.now()
                    k0 += u.shape[0]
                    if k0 == nk:
                        for tt in range(TT):
                            pair[tt].held = False
                            evac(tt, c, n, pair[tt], pe_did.now())
                    yield True

        def gemm(h, nk, width, evac, ready=None, starts=None):
            for _ in gemm_steps(h, nk, width, evac, ready or marks(), starts):
                pass

        def to_sbuf(dst, r=None):
            before = marks()

            def evac(tt, c, n, bank, full):
                if tt == 0:
                    @block.vector
                    def _(dve):
                        dve.wait_ge(*full)
                        dve.wait_ge(*before.pe)
                        dve.wait_ge(*before.act)
                        dve.wait_ge(*before.dve)
                        dve.wait_ge(*before.pool)
                        dve.wait_ge(*turn["normed"])
                        if r is None:
                            dve.tensor_copy(dst(tt, c, n), bank.t[:, 0:n]).then_inc(*dve_did.up())
                        else:
                            dve.tensor_scalar(dst(tt, c, n), bank.t[:, 0:n], r(tt), None,
                                              ALU.mult).then_inc(*dve_did.up())
                    bank.drained = dve_did.now()
                else:
                    @block.scalar
                    def _(act):
                        act.wait_ge(*full)
                        act.wait_ge(*before.pe)
                        act.wait_ge(*before.act)
                        act.wait_ge(*before.dve)
                        act.wait_ge(*before.pool)
                        act.wait_ge(*turn["normed"])
                        if r is None:
                            act.copy(dst(tt, c, n), bank.t[:, 0:n]).then_inc(*act_did.up())
                        else:
                            act.activation(dst(tt, c, n), bank.t[:, 0:n], ACT.Copy,
                                           scale=r(tt)).then_inc(*act_did.up())
                    bank.drained = act_did.now()
            return evac

        def power(dst, n, scale):
            @block.vector
            def _(dve):
                dve.wait_ge(*act_did.now())
                dve.wait_ge(*dve_did.now())
                dve.tensor_scalar(dst, dst, scale, EPS, ALU.mult, ALU.add).then_inc(*dve_did.up())

            @block.gpsimd
            def _(pool):
                pool.wait_ge(*dve_did.now())
                pool.tensor_tensor(dst, dst, C("minus_half")[:, 0:n], ALU.pow).then_inc(*pool_did.up())

        def rstd_rows(src, dst, start=None, src_ready=None):
            start = start or marks()
            src_ready = src_ready or start.dve

            @block.scalar
            def _(act):
                act.wait_ge(*start.pe)
                act.wait_ge(*start.act)
                act.wait_ge(*start.dve)
                act.wait_ge(*start.pool)
                act.wait_ge(*src_ready)
                for tt in range(TT):
                    act.activation(sq[:, tt, :], src[:, tt, :], ACT.Square,
                                   accum_out=dst[:, tt:tt + 1]).then_inc(*act_did.up())
            power(dst, TT, 1.0 / D)
            turn["normed"] = pool_did.now()

        def rstd_heads(*each):
            before = marks()
            squared = []
            for src, dst, heads, w, squares in each:
                v = squares[:, :, 0:heads * w].rearrange("p t (h w) -> p t h w", h=heads)

                @block.scalar
                def _(act):
                    act.wait_ge(*before.pe)
                    act.wait_ge(*before.act)
                    act.wait_ge(*before.dve)
                    act.wait_ge(*before.pool)
                    for tt in range(TT):
                        act.activation(v[:, tt], src[:, tt], ACT.Square).then_inc(*act_did.up())
                squared.append((v, act_did.now()))
            for (src, dst, heads, w, squares), (v, done) in zip(each, squared):
                @block.vector
                def _(dve):
                    dve.wait_ge(*before.pe)
                    dve.wait_ge(*done)
                    dve.wait_ge(*before.dve)
                    dve.wait_ge(*before.pool)
                    for tt in range(TT):
                        dve.tensor_reduce(dst[:, tt * heads:(tt + 1) * heads], v[:, tt], AX.X,
                                          ALU.add).then_inc(*dve_did.up())
                power(dst, TT * heads, 1.0 / w)

        def scale_heads(dst, src, r, heads):
            w = src.shape[3]

            def part(eng, tt):
                return eng.tensor_tensor(dst[:, tt], src[:, tt],
                                         r[:, tt * heads:(tt + 1) * heads].unsqueeze(2).broadcast_to([P, heads, w]),
                                         ALU.mult)
            before = marks()

            @block.vector
            def _(dve):
                dve.wait_ge(*before.pe)
                dve.wait_ge(*before.act)
                dve.wait_ge(*before.dve)
                dve.wait_ge(*before.pool)
                part(dve, 0).then_inc(*dve_did.up())

            @block.gpsimd
            def _(pool):
                pool.wait_ge(*before.pe)
                pool.wait_ge(*before.act)
                pool.wait_ge(*before.dve)
                pool.wait_ge(*before.pool)
                part(pool, 1).then_inc(*pool_did.up())

        attended = {}

        def attention(jobs, after=None):
            before = after or marks()
            st = [dict() for _ in jobs]

            def scores(i):
                j, s = jobs[i], st[i]
                bank = s["bank"] = next_bank()

                @block.tensor
                def _(pe):
                    pe.wait_ge(*bank.drained)
                    pe.wait_ge(*before.act)
                    pe.wait_ge(*before.dve)
                    pe.wait_ge(*before.pool)
                    if j.get("keys_ready"):
                        pe.wait_ge(*j["keys_ready"]())
                    for m, (l, r) in enumerate(j["qk"]):
                        mm = pe.matmul(bank.t[:, 0:j["n"]], l, r, start=(m == 0), stop=(m == len(j["qk"]) - 1))
                    mm.then_inc(*pe_did.up())
                scored = pe_did.now()
                n, js = j["n"], jobstat[:, i % 8, :]

                @block.vector
                def _(dve):
                    dve.wait_ge(*scored)
                    if i >= ATT_SLOTS:
                        dve.wait_ge(*st[i - ATT_SLOTS]["exped"])
                    if i < 1:
                        dve.wait_ge(*before.pe)
                        dve.wait_ge(*before.act)
                        dve.wait_ge(*before.dve)
                        dve.wait_ge(*before.pool)
                    if j.get("bias_ready"):
                        dve.wait_ge(*j["bias_ready"]())
                    if j["bias"] is not None:
                        dve.scalar_tensor_tensor(smask[:, i % ATT_SLOTS, 0:n], bank.t[:, 0:n], j["scale"], j["bias"],
                                                 ALU.mult, ALU.add).then_inc(*dve_did.up())
                        dve.wait_ge(*dve_did.now())
                        dve.tensor_reduce(js[:, 0:1], smask[:, i % ATT_SLOTS, 0:n], AX.X, ALU.max,
                                          negate=True).then_inc(*dve_did.up())
                        if j.get("guard"):
                            dve.wait_ge(*dve_did.now())
                            dve.tensor_scalar(js[:, 0:1], js[:, 0:1], -NEG / 10, None,
                                              ALU.min).then_inc(*dve_did.up())
                    else:
                        dve.tensor_reduce(js[:, 1:2], bank.t[:, 0:n], AX.X, ALU.max,
                                          negate=True).then_inc(*dve_did.up())
                        dve.wait_ge(*dve_did.now())
                        dve.tensor_scalar(js[:, 0:1], js[:, 1:2], j["scale"], None, ALU.mult).then_inc(*dve_did.up())
                maxed = dve_did.now()
                if j.get("scored"):
                    j["scored"]()

                @block.scalar
                def _(act):
                    act.wait_ge(*maxed)
                    if i >= ATT_SLOTS:
                        act.wait_ge(*st[i - ATT_SLOTS]["turned"])
                    if i < 1:
                        act.wait_ge(*before.pe)
                        act.wait_ge(*before.act)
                        act.wait_ge(*before.dve)
                        act.wait_ge(*before.pool)
                    if j["bias"] is not None:
                        act.activation(probs[:, i % ATT_SLOTS, 0:n], smask[:, i % ATT_SLOTS, 0:n], ACT.Exp, bias=js[:, 0:1],
                                       accum_out=js[:, 2:3]).then_inc(*act_did.up())
                    else:
                        act.activation(probs[:, i % ATT_SLOTS, 0:n], bank.t[:, 0:n], ACT.Exp, bias=js[:, 0:1],
                                       scale=j["scale"], accum_out=js[:, 2:3]).then_inc(*act_did.up())
                s["exped"] = act_did.now()
                bank.drained = maxed if j["bias"] is not None else s["exped"]

            def turned(i):
                j, s = jobs[i], st[i]
                bank = next_bank()

                @block.tensor
                def _(pe):
                    pe.wait_ge(*s["exped"])
                    pe.wait_ge(*bank.drained)
                    for b, v in enumerate(j["v"]):
                        kb = v.shape[0]
                        m = pe.transpose(bank.t[0:kb, b * P:(b + 1) * P], probs[:, i % ATT_SLOTS, b * P:b * P + kb], ident)
                    m.then_inc(*pe_did.up())
                s["turned"] = pe_did.now()
                nb, kb = len(j["v"]), j["v"][0].shape[0]

                @block.scalar
                def _(act):
                    act.wait_ge(*s["turned"])
                    if i >= ATT_SLOTS:
                        act.wait_ge(*st[i - ATT_SLOTS]["summed"])
                    act.copy(pT[0:kb, i % ATT_SLOTS, 0:nb, :],
                             bank.t[0:kb, 0:nb * P].rearrange("p (a b) -> p a b", a=nb)).then_inc(*act_did.up())
                s["copied"] = bank.drained = act_did.now()
                js = jobstat[:, i % 8, :]

                @block.vector
                def _(dve):
                    dve.wait_ge(*s["exped"])
                    if j.get("guard"):
                        dve.tensor_scalar(js[:, 2:3], js[:, 2:3], 1e-30, None, ALU.max).then_inc(*dve_did.up())
                        dve.wait_ge(*dve_did.now())
                    dve.reciprocal(js[:, 3:4], js[:, 2:3]).then_inc(*dve_did.up())
                s["inverse"] = dve_did.now()
                if j.get("mul") is not None:
                    @block.gpsimd
                    def _(pool):
                        pool.wait_ge(*s["inverse"])
                        pool.tensor_tensor(js[:, 3:4], js[:, 3:4], j["mul"], ALU.mult).then_inc(*pool_did.up())
                    s["inverse"] = pool_did.now()

            def summed(i):
                j, s = jobs[i], st[i]
                bank = next_bank()

                @block.tensor
                def _(pe):
                    pe.wait_ge(*s["copied"])
                    pe.wait_ge(*bank.drained)
                    for b, v in enumerate(j["v"]):
                        m = pe.matmul(bank.t[:, 0:j["dv"]], pT[0:v.shape[0], i % ATT_SLOTS, b, :], v,
                                      start=(b == 0), stop=(b == len(j["v"]) - 1))
                    m.then_inc(*pe_did.up())
                s["summed"] = pe_did.now()
                js = jobstat[:, i % 8, :]

                @block.vector
                def _(dve):
                    dve.wait_ge(*s["summed"])
                    dve.wait_ge(*s["inverse"])
                    if j.get("add"):
                        dve.wait_ge(*st[i - 1]["written"])
                    if j.get("add"):
                        dve.scalar_tensor_tensor(j["out"], bank.t[:, 0:j["dv"]], js[:, 3:4], j["out"],
                                                 ALU.mult, ALU.add).then_inc(*dve_did.up())
                    else:
                        dve.tensor_scalar(j["out"], bank.t[:, 0:j["dv"]], js[:, 3:4], None,
                                          ALU.mult).then_inc(*dve_did.up())
                s["written"] = bank.drained = dve_did.now()
                if j.get("then"):
                    j["then"]()

            for i in range(len(jobs) + 3):
                if i == 1:
                    turn["under way"] = prepare_steps(PIECES)
                if i >= PREPARE_AT:
                    next(turn["under way"], None)
                if 2 <= i < len(jobs) + 2:
                    turned(i - 2)
                if i < len(jobs):
                    scores(i)
                if i >= 3:
                    summed(i - 3)
            attended["o"] = marks()

        def ffn(ready, r, finish):
            before = marks()
            NF = D_FF // FF_CHUNK
            KB = FF_CHUNK // P
            pair = [banks[0:2], banks[2:4]]
            acc = banks[4:8]
            turn["bank"] = 0
            hid_done, turned, split, down_done = {}, {}, {}, {}

            def gate_up(c, u, k0):
                there = ready.upto(k0 + u.shape[0])

                @block.tensor
                def _(pe):
                    if k0 == 0:
                        for bank in pair[c % 2]:
                            pe.wait_ge(*bank.drained)
                    if c == 0:
                        pe.wait_ge(*there.act)
                        pe.wait_ge(*there.dve)
                    pe.wait_ge(*u.parted)
                    for tt in range(TT):
                        ts_ = slice(tt * P, (tt + 1) * P)
                        for k in range(u.shape[0]):
                            m = three_products(pe, pair[c % 2][tt].t[:, :], h_hi[:, k0 + k, ts_], h_lo[:, k0 + k, ts_],
                                               u, k, slice(0, 512), k0 + k == 0, k0 + k == KD - 1)
                    m.then_inc(*pe_did.up())
                u.used = pe_did.now()

            def hidden(c):
                full = pe_did.now()
                for tt in range(TT):
                    bank = pair[c % 2][tt]

                    @block.scalar
                    def _(act):
                        act.wait_ge(*full)
                        if c >= 2:
                            act.wait_ge(*hid_done[(c - 2, tt)])
                        elif tt == 0:
                            act.wait_ge(*before.dve)
                            act.wait_ge(*turn["normed"])
                        act.activation(ff_silu[:, c % 2, tt, :], bank.t[:, 0:FF_CHUNK], ACT.Silu,
                                       scale=r(tt)).then_inc(*act_did.up())

                    @block.vector
                    def _(dve):
                        dve.wait_ge(*act_did.now())
                        dve.wait_ge(*turn["normed"])
                        if c >= 2:
                            dve.wait_ge(*turned[c - 2])
                        dve.scalar_tensor_tensor(ff_hid[:, c % 2, tt, :], bank.t[:, FF_CHUNK:2 * FF_CHUNK], r(tt),
                                                 ff_silu[:, c % 2, tt, :], ALU.mult, ALU.mult).then_inc(*dve_did.up())
                    hid_done[(c, tt)] = bank.drained = dve_did.now()

            def transposes(c):
                bank = pair[c % 2][0]

                @block.tensor
                def _(pe):
                    pe.wait_ge(*hid_done[(c, 1)])
                    for b in range(KB):
                        for tt in range(TT):
                            m = pe.transpose(bank.t[:, (b * TT + tt) * P:(b * TT + tt + 1) * P],
                                             ff_hid[:, c % 2, tt, b * P:(b + 1) * P], ident)
                    m.then_inc(*pe_did.up())
                turned[c] = pe_did.now()
                ps = bank.t[:, 0:KB * T].rearrange("p (b n) -> p b n", b=KB)

                @block.scalar
                def _(act):
                    act.wait_ge(*turned[c])
                    if c >= 2:
                        act.wait_ge(*down_done[c - 2])
                    act.copy(ff_hi[:, c % 2, :, :], ps).then_inc(*act_did.up())

                @block.vector
                def _(dve):
                    dve.wait_ge(*act_did.now())
                    dve.tensor_tensor(ff_lo[:, c % 2, :, :], ps, ff_hi[:, c % 2, :, :].bitcast(F32),
                                      ALU.subtract).then_inc(*dve_did.up())
                split[c] = bank.drained = dve_did.now()

            def down(c, u, blocks=range(KB)):
                @block.tensor
                def _(pe):
                    if c == 0:
                        for bank in acc:
                            pe.wait_ge(*bank.drained)
                    pe.wait_ge(*split[c])
                    pe.wait_ge(*u.parted)
                    for b in blocks:
                        for tt in range(TT):
                            ts_ = slice(tt * P, (tt + 1) * P)
                            for half in range(2):
                                m = three_products(pe, acc[tt * 2 + half].t[:, :], ff_hi[:, c % 2, b, ts_],
                                                   ff_lo[:, c % 2, b, ts_], u, b, slice(half * 512, (half + 1) * 512),
                                                   c == 0 and b == 0, c == NF - 1 and b == KB - 1)
                    m.then_inc(*pe_did.up())
                u.used = down_done[c] = pe_did.now()

            for c in range(NF + 1):
                if c < NF:
                    gate_up(c, take(), 0)
                if 1 <= c < NF:
                    transposes(c - 1)
                if c < NF:
                    gate_up(c, take(), KD // 2)
                    hidden(c)
                if c == NF - 1:
                    u = take()
                    down(c - 1, u, range(KB // 2))
                    transposes(c)
                    down(c - 1, u, range(KB // 2, KB))
                elif c >= 1:
                    down(c - 1, take())
            for half in range(2):
                for tt in range(TT):
                    finish(tt, half, acc[tt * 2 + half], pe_did.now())

        x_ready = [const_landed.now()] * 2

        def add_half(tt, half, bank, full):
            @block.vector
            def _(dve):
                dve.wait_ge(*full)
                dve.wait_ge(*act_did.now())
                xs = x[:, tt, half * 512:(half + 1) * 512]
                dve.scalar_tensor_tensor(xs, bank.t[:, :], 0.5, xs, ALU.mult, ALU.add).then_inc(*dve_did.up())
            x_ready[half] = bank.drained = dve_did.now()

        def hi_of(buf):
            return lambda b, n: buf[:, b:b + n, :]

        def pre_norm(src, col, r):
            start = marks()
            HALF = KD // 2

            def half(k0):
                return to_T(HALF, lambda b, tt: src[:, tt, (k0 + b) * P:(k0 + b + 1) * P],
                            lambda b, n: h_hi[:, k0 + b:k0 + b + n, :], dst_lo=lambda b, n: h_lo[:, k0 + b:k0 + b + n, :],
                            scale=lambda b: cols[:, col // P, col % P + k0 + b:col % P + k0 + b + 1],
                            ready=lambda b: x_ready[k0 // HALF], after=start)

            groups = half(0).groups + half(HALF).groups
            rstd_rows(src, r, start, x_ready[1])
            return Ready(groups, 2)

        gain_used = [const_landed.now()] * 2

        def load_gain(src):
            g = turn["gain"] % 2
            turn["gain"] += 1

            @block.sync
            def _(sp):
                sp.wait_ge(*gain_used[g])
                sp.dma_start(gain[:, g, :], src.partition_broadcast(P)).then_inc(*gain_landed[g].up(16))
            return gain[:, g, :], gain_landed[g].now(), g

        class Sublayer:

            def __init__(self, g):
                self.before, self.gain, self.last = marks(), g, []

            def leave(self, tt, c, n, bank, full):
                half = c // 512

                @block.scalar
                def _(act):
                    act.wait_ge(*full)
                    act.wait_ge(*self.before.dve)
                    act.wait_ge(*self.before.pool)
                    act.activation(sq[:, tt, c:c + n], bank.t[:, 0:n], ACT.Square, scale=D ** -0.5,
                                   accum_out=stat[:, 56 + half * 2 + tt:57 + half * 2 + tt]).then_inc(*act_did.up())
                self.squared = act_did.now()
                if half == 0:
                    self.multiply(tt, c, bank, self.squared)
                else:
                    self.last.append((tt, c, bank, self.squared))

            def multiply(self, tt, c, bank, squared):
                gv, landed, _ = self.gain

                @block.vector
                def _(dve):
                    dve.wait_ge(*squared)
                    dve.wait_ge(*landed)
                    dve.tensor_tensor(o_buf[:, tt, c:c + 512], bank.t[:, :], gv[:, c:c + 512],
                                      ALU.mult).then_inc(*dve_did.up())
                bank.drained = dve_did.now()

            def finish(self):
                r = stat[:, 60:62]

                @block.vector
                def _(dve):
                    dve.wait_ge(*self.squared)
                    dve.scalar_tensor_tensor(r, stat[:, 56:58], EPS, stat[:, 58:60], ALU.add,
                                             ALU.add).then_inc(*dve_did.up())
                summed = dve_did.now()
                for one in self.last:
                    self.multiply(*one)

                @block.gpsimd
                def _(pool):
                    pool.wait_ge(*summed)
                    pool.tensor_tensor(r, r, C("minus_half")[:, 0:TT], ALU.pow).then_inc(*pool_did.up())

                @block.vector
                def _(dve):
                    dve.wait_ge(*pool_did.now())
                    dve.wait_ge(*dve_did.now())
                    for half in range(2):
                        cs = slice(half * 512, (half + 1) * 512)
                        for tt in range(TT):
                            dve.scalar_tensor_tensor(x[:, tt, cs], o_buf[:, tt, cs], r[:, tt:tt + 1], x[:, tt, cs],
                                                     ALU.mult, ALU.add).then_inc(*dve_did.up())
                        x_ready[half] = dve_did.now()
                gain_used[self.gain[2]] = dve_did.now()

        def rs_of(c):
            return lambda tt: rs[:, c + tt:c + tt + 1]

        h_in, h2_in = (h_hi, h_lo), (h2_hi, h2_lo)

        FIRST = const_where["one"][0] + 1

        @block.scalar
        def _(act):
            act.dma_start(const[:, 0:FIRST], a["const"][:, 0:FIRST]).then_inc(*const_landed.up(16))
            act.dma_start(rows[:, :, :], a["rows"]).then_inc(*const_landed.up(16))

        @block.sync
        def _(sp):
            sp.dma_start(x[:, :, :], a["x"][0].rearrange("(t p) d -> p t d", p=P)).then_inc(*const_landed.up(16))
        landed = const_landed.now()

        @block.scalar
        def _(act):
            act.dma_start(const[:, FIRST:CONST_N], a["const"][:, FIRST:CONST_N]).then_inc(*more_landed.up(16))
            act.dma_start(vec[:, :], a["vec"].partition_broadcast(P)).then_inc(*more_landed.up(16))
            with nc.allow_non_contiguous_dma(reason="256 positions, once"):
                act.dma_start(posi[:, :], a["positions"][0, :].rearrange("(t p) -> p t", p=P)).then_inc(
                    *more_landed.up(16))
            act.dma_start(early[:, :], a["early"]).then_inc(*late_landed.up(16))
            act.dma_start(gate[:, :, :], a["mem"][0].rearrange("(t p) d -> p t d", p=P)).then_inc(*late_landed.up(16))
        load_ahead()

        table = nc.dram_tensor("bias_table", [DEPTH, NA_H, GRID_W, TBL_W], F32, kind="Internal").ap()
        table_landed = signal("table_landed")

        @block.gpsimd
        def _(pool):
            for l in range(DEPTH):
                flat = a["na_rpb_2"][l].rearrange("h r c -> h (r c)")[:, TBL_LO:TBL_HI]
                pool.dma_start(table[l], flat.unsqueeze(1).broadcast_to([NA_H, GRID_W, TBL_W])).then_inc(
                    *table_landed.up(16))

        @block.vector
        def _(dve):
            dve.wait_ge(*landed)

        @block.scalar
        def _(act):
            act.wait_ge(*landed)

        @block.gpsimd
        def _(pool):
            pool.wait_ge(*landed)
            pool.memset(rs[:, :], 1.0).then_inc(*pool_did.up())

        bank = next_bank()

        @block.tensor
        def _(pe):
            pe.wait_ge(*landed)
            for tile in range(2):
                m = pe.transpose(bank.t[:, tile * P:(tile + 1) * P], rows[:, tile, :], ident)
            m.then_inc(*pe_did.up())
        full = pe_did.now()

        @block.vector
        def _(dve):
            dve.wait_ge(*full)
            for tile in range(2):
                dve.tensor_copy(cols[:, tile, :], bank.t[:, tile * P:(tile + 1) * P]).then_inc(*dve_did.up())
            dve.wait_ge(*dve_did.now())
            c = col_of["subln"] % P
            dve.tensor_scalar(cols[:, 1, c:c + 1], cols[:, 1, c:c + 1], 1.0 - LAM_INIT, None,
                              ALU.mult).then_inc(*dve_did.up())
        bank.drained = dve_did.now()

        def rotate(v, heads, half, cos, sin, work=sq):
            x1, x2 = v[:, :, :, 0:half], v[:, :, :, half:2 * half]
            shape = [P, heads, half]
            sz = heads * half
            t = [work[:, :, m * sz:(m + 1) * sz].rearrange("p t (h w) -> p t h w", h=heads) for m in range(4)]
            before = marks()

            def products(eng, sig, tt, pairs):
                for dst, xx, table in pairs:
                    eng.tensor_tensor(t[dst][:, tt], xx[:, tt], table[:, tt, :].unsqueeze(1).broadcast_to(shape),
                                      ALU.mult).then_inc(*sig.up())

            @block.vector
            def _(dve):
                dve.wait_ge(*before.pe)
                dve.wait_ge(*before.act)
                dve.wait_ge(*before.dve)
                dve.wait_ge(*before.pool)
                for tt in range(TT):
                    products(dve, dve_did, tt, ((0, x1, cos), (1, x2, sin)))

            @block.gpsimd
            def _(pool):
                pool.wait_ge(*before.pe)
                pool.wait_ge(*before.act)
                pool.wait_ge(*before.dve)
                pool.wait_ge(*before.pool)
                for tt in range(TT):
                    products(pool, pool_did, tt, ((2, x2, cos), (3, x1, sin)))
            after = marks()

            @block.vector
            def _(dve):
                dve.wait_ge(*after.pe)
                dve.wait_ge(*after.act)
                dve.wait_ge(*after.dve)
                dve.wait_ge(*after.pool)
                for tt in range(TT):
                    dve.tensor_tensor(x1[:, tt], t[0][:, tt], t[1][:, tt], ALU.subtract).then_inc(*dve_did.up())

            @block.gpsimd
            def _(pool):
                pool.wait_ge(*after.pe)
                pool.wait_ge(*after.act)
                pool.wait_ge(*after.dve)
                pool.wait_ge(*after.pool)
                for tt in range(TT):
                    pool.tensor_tensor(x2[:, tt], t[2][:, tt], t[3][:, tt], ALU.add).then_inc(*pool_did.up())

        def heads_of(c, n, w=HD, buf=z):
            return buf[:, :, c:c + n * w].rearrange("p t (h w) -> p t h w", h=n)

        def log_sigmoid(*each):
            before = marks()

            @block.scalar
            def _(act):
                act.wait_ge(*before.pe)
                act.wait_ge(*before.act)
                act.wait_ge(*before.dve)
                act.wait_ge(*before.pool)
                for dst, src, t1, t2 in each:
                    act.activation(t1, src, ACT.Abs).then_inc(*act_did.up())
                act.wait_ge(*act_did.now())
                for dst, src, t1, t2 in each:
                    act.activation(t2, t1, ACT.Exp, scale=-1.0).then_inc(*act_did.up())
                act.wait_ge(*act_did.now())
                for dst, src, t1, t2 in each:
                    act.activation(t1, t2, ACT.Ln, bias=C("one")).then_inc(*act_did.up())

            @block.vector
            def _(dve):
                dve.wait_ge(*act_did.now())
                dve.wait_ge(*before.pe)
                dve.wait_ge(*before.dve)
                dve.wait_ge(*before.pool)
                for dst, src, t1, t2 in each:
                    dve.scalar_tensor_tensor(dst, src, 0.0, t1, ALU.min, ALU.subtract).then_inc(*dve_did.up())

        causal = C("causal", (TT,))

        cos1, sin1 = rope[:, 0], rope[:, 1]
        ang, turns, half_a, sin_h = rope[:, 2], rope[:, 3], rope[:, 4], rope[:, 5]
        TWO_PI = 2 * math.pi
        hi = float(np.float32(6.28125))
        mid = float(np.float32(TWO_PI - hi))
        lo_ = float(np.float32(TWO_PI - hi - mid))
        ROUND = float(3 << 22)

        neg_lam = small[:, 25:26]

        def rope_tables():

            @block.vector
            def _(dve):
                def then(i):
                    i.then_inc(*dve_did.up())
                    dve.wait_ge(*dve_did.now())
                dve.wait_ge(*more_landed.now())
                dve.wait_ge(*act_did.now())
                then(dve.tensor_copy(small[:, 16:16 + TT], posi[:, :]))
                then(dve.tensor_tensor(ang, small[:, 16:16 + TT].unsqueeze(2).broadcast_to([P, TT, ROPE_HALF]),
                                       C("inv").unsqueeze(1).broadcast_to([P, TT, ROPE_HALF]), ALU.mult))
                then(dve.tensor_scalar(turns, ang, 1.0 / TWO_PI, ROUND, ALU.mult, ALU.add))
                then(dve.tensor_scalar(turns, turns, -ROUND, None, ALU.add))
                for part in (hi, mid, lo_):
                    then(dve.scalar_tensor_tensor(ang, turns, -part, ang, ALU.mult, ALU.add))
                then(dve.tensor_scalar(ang, ang, math.pi, -math.pi, ALU.min, ALU.max))
                then(dve.tensor_scalar(half_a, ang, 0.5, None, ALU.mult))
                lp = vec[:, FOX_H:FOX_H + 4 * HD].rearrange("p (a b) -> p a b", a=4)
                for m in range(2):
                    then(dve.tensor_tensor(tmp[:, 1, m * HD:(m + 1) * HD], lp[:, 2 * m, :], lp[:, 2 * m + 1, :], ALU.mult))
                then(dve.tensor_reduce(small[:, 20:22], tmp[:, 1, 0:2 * HD].rearrange("p (a b) -> p a b", a=2), AX.X,
                                       ALU.add))

            @block.scalar
            def _(act):
                act.wait_ge(*pe_did.now())
                act.wait_ge(*act_did.now())
                act.wait_ge(*dve_did.now())
                act.wait_ge(*pool_did.now())
                act.activation(sin1, ang, ACT.Sin).then_inc(*act_did.up())
                act.activation(sin_h, half_a, ACT.Sin).then_inc(*act_did.up())
                act.activation(small[:, 22:24], small[:, 20:22], ACT.Exp).then_inc(*act_did.up())

            @block.vector
            def _(dve):
                dve.wait_ge(*pe_did.now())
                dve.wait_ge(*act_did.now())
                dve.wait_ge(*dve_did.now())
                dve.wait_ge(*pool_did.now())
                dve.tensor_tensor(cos1, sin_h, sin_h, ALU.mult).then_inc(*dve_did.up())
                dve.wait_ge(*dve_did.now())
                dve.tensor_scalar(cos1, cos1, -2.0, 1.0, ALU.mult, ALU.add).then_inc(*dve_did.up())
                dve.tensor_tensor(small[:, 24:25], small[:, 23:24], small[:, 22:23], ALU.subtract).then_inc(*dve_did.up())
                dve.wait_ge(*dve_did.now())
                dve.tensor_scalar(neg_lam, small[:, 24:25], -LAM_INIT, None, ALU.add).then_inc(*dve_did.up())

        def halves_of_o(scale=None, marks_of=None):
            HALF = KD // 2
            marks_of = marks_of or [marks()] * 2

            def half(k0):
                return to_T(HALF, lambda b, tt: o_buf[:, tt, (k0 + b) * P:(k0 + b + 1) * P],
                            lambda b, n: h_hi[:, k0 + b:k0 + b + n, :], dst_lo=lambda b, n: h_lo[:, k0 + b:k0 + b + n, :],
                            scale=scale, after=marks_of[k0 // HALF]).groups
            if len(marks_of) == 2:
                return Ready(half(0) + half(HALF), 2)
            return Ready(half(0), 2, lambda: half(HALF))

        def even_mixer(post_gain):
            ready = pre_norm(x, col_of[("pre", 0, 0)], rs[:, 0:2])
            lf = small[:, 32:48].rearrange("p (t h) -> p t h", t=TT)
            lfs = small[:, 80:96].rearrange("p (t h) -> p t h", t=TT)
            c_neg = hT2[0:FOX_H, 7, :]
            there = {}

            def log_f():
                @block.vector
                def _(dve):
                    dve.wait_ge(*late_landed.now())
                    dve.wait_ge(*act_did.now())
                    dve.wait_ge(*dve_did.now())
                    dve.tensor_tensor(lf, z[:, :, EV["fl"]:EV["fl"] + FOX_H],
                                      vec[:, 0:FOX_H].unsqueeze(1).broadcast_to([P, TT, FOX_H]),
                                      ALU.add).then_inc(*dve_did.up())
                log_sigmoid((small[:, 80:96], small[:, 32:48], small[:, 48:64], small[:, 64:80]))
                there["lf"] = marks()
                rstd_rows(gate, rs[:, 28:30])

            def sum_log_f():
                bank = next_bank()

                @block.tensor
                def _(pe):
                    pe.wait_ge(*bank.drained)
                    pe.wait_ge(*there["lf"].dve)
                    for tt in range(TT):
                        m = pe.matmul(bank.t[0:FOX_H, 0:T], lfs[:, tt, :], C("upto", (TT,))[:, tt, :],
                                      start=(tt == 0), stop=(tt == TT - 1))
                    m.then_inc(*pe_did.up())

                @block.vector
                def _(dve):
                    dve.wait_ge(*pe_did.now())
                    dve.tensor_scalar(c_neg, bank.t[0:FOX_H, 0:T], -(HD ** 0.5), None, ALU.mult).then_inc(*dve_did.up())
                bank.drained = dve_did.now()

            to_z = to_sbuf(lambda tt, c, n: z[:, tt, c:c + n], rs_of(0))

            def evac(tt, c, n, bank, full):
                to_z(tt, c, n, bank, full)
                if tt < TT - 1:
                    return
                there[c] = marks()
                if c == EV_STARTS[-1]:
                    return
                prepare()
                if c == 2560:
                    rope_tables()
                elif c == 1536:
                    log_f()
                elif c == 2048:
                    sum_log_f()
                    sparse_keys()
                elif c == 512:
                    to_T(4, lambda b, tt: z[:, tt, EV["fq"] + b * P:EV["fq"] + (b + 1) * P],
                         lambda b, n: qT[:, b:b + n, :], after=there[0])
                    to_T(4, lambda b, tt: z[:, tt, EV["nq"] + b * P:EV["nq"] + (b + 1) * P],
                         lambda b, n: qT[:, 4 + b:4 + b + n, :], after=there["nq"])
                    to_T(4, lambda b, tt: tmp[:, tt, b * P:(b + 1) * P], lambda b, n: kT[:, 4 + b:4 + b + n, :],
                         after=there["sparse"])
                    to_T(4, lambda b, tt: z[:, tt, EV["fk"] + b * P:EV["fk"] + (b + 1) * P],
                         lambda b, n: kT[:, b:b + n, :], after=there[512])
                    there["turned"] = marks()
            sgate = stat[:, 0:TT * 3 * NSA_H].rearrange("p (t h) -> p t h", t=TT)
            kd = tmp[:, :, 0:512].rearrange("p t (b c d) -> p t b c d", b=4, c=2)

            def sparse_keys():
                rotate(heads_of(EV["nq"], 10), 10, ROPE_HALF, cos1, sin1)
                there["nq"] = marks()
                rotate(heads_of(EV["ks"], 2), 2, ROPE_HALF, cos1, sin1)
                rotate(heads_of(EV["kw"], 2), 2, ROPE_HALF, cos1, sin1)
                before = marks()

                @block.scalar
                def _(act):
                    act.wait_ge(*before.pe)
                    act.wait_ge(*before.act)
                    act.wait_ge(*before.dve)
                    act.activation(sgate, z[:, :, EV["gl"]:EV["gl"] + 3 * NSA_H], ACT.Sigmoid).then_inc(*act_did.up())

                @block.gpsimd
                def _(pool):
                    pool.wait_ge(*before.act)
                    pool.wait_ge(*before.dve)
                    pool.wait_ge(*before.pool)
                    for m, name in enumerate(("ks", "kw")):
                        for c in range(2):
                            for tt in range(TT):
                                pool.tensor_copy(kd[:, tt, 2 * m:2 * m + 2, c, :],
                                                 heads_of(EV[name], 2)[:, tt]).then_inc(*pool_did.up())
                there["sparse"] = marks()
            gemm(h_in, KD, EV_IN, evac, ready, EV_STARTS)
            kcT = hT2[:, 6, 2 * HD:2 * HD + 2 * NC]
            vcmp = hT2[:, 6, 0:2 * HD]
            NL = CMP_BLOCK // 2
            wins = [hT2[:, 3 * m:3 * m + 3, :] for m in range(2)]

            def compress():
                before = marks()

                @block.gpsimd
                def _(pool):
                    for m, pos in enumerate(("ev_cmp_pos_k", "ev_cmp_pos_v")):
                        pc = col_of[pos] % P
                        pool.memset(wins[m][:, 2, :], 0.0).then_inc(*pool_did.up())
                        pool.wait_ge(*pool_did.now())
                        pool.tensor_copy(wins[m][:, 2, 0:2 * NL:2], cols[:, 1, pc:pc + NL]).then_inc(*pool_did.up())
                posed = pool_did.now()
                for m, name in enumerate(("kc", "vc")):
                    for g in range(2):
                        bank = next_bank()

                        @block.tensor
                        def _(pe):
                            pe.wait_ge(*bank.drained)
                            pe.wait_ge(*before.act)
                            pe.wait_ge(*before.dve)
                            for tt in range(TT):
                                src = z[:, tt, EV[name] + g * HD:EV[name] + (g + 1) * HD]
                                pe.matmul(bank.t[0:HD, tt * P:(tt + 1) * P], src, ident, start=True, stop=True)
                            for tt in range(TT):
                                src = z[:, tt, EV[name] + g * HD:EV[name] + (g + 1) * HD]
                                mm = pe.matmul(bank.t[HD:P, 0:T], src, C("shift", (TT,))[:, tt, :],
                                               start=(tt == 0), stop=(tt == TT - 1))
                            mm.then_inc(*pe_did.up())

                        @block.vector
                        def _(dve):
                            dve.wait_ge(*pe_did.now())
                            dve.tensor_copy(wins[m][:, g, :], bank.t[:, 0:T]).then_inc(*dve_did.up())
                        bank.drained = dve_did.now()
                        yield True
                windowed = dve_did.now()
                second, inner, inner_banks = [], [], []
                for m in range(2):
                    cw1, cw2 = take(), take()
                    bank = next_bank()

                    @block.tensor
                    def _(pe):
                        pe.wait_ge(*cw1.landed)
                        pe.wait_ge(*bank.drained)
                        pe.wait_ge(*windowed)
                        pe.wait_ge(*posed)
                        for l in range(NL):
                            mm = pe.matmul(bank.t[:, 0:3 * NC].rearrange("p (g c) -> p g c", g=3), cw1.raw[:, l, :],
                                           wins[m][:, :, 2 * l:2 * l + CMP_STRIDE * (NC - 1) + 1:CMP_STRIDE],
                                           start=(l == 0), stop=(l == NL - 1))
                        mm.then_inc(*pe_did.up())
                    cw1.used = pe_did.now()
                    pos_h = sq[:, 0, 64 + m:65 + m]

                    @block.vector
                    def _(dve):
                        dve.wait_ge(*before.pool)
                        dve.wait_ge(*pe_did.now())
                        dve.tensor_copy(pos_h, bank.t[:, 2 * NC:2 * NC + 1]).then_inc(*dve_did.up())
                    bank.held = True
                    second.append(cw2)
                    inner_banks.append(bank)
                    yield True
                positioned = dve_did.now()
                for m, bank in enumerate(inner_banks):
                    hidden = sq[:, 0, m * 32:m * 32 + 2 * NC]

                    @block.scalar
                    def _(act):
                        act.wait_ge(*positioned)
                        act.activation(hidden, bank.t[:, 0:2 * NC], ACT.Gelu_apprx_tanh,
                                       bias=sq[:, 0, 64 + m:65 + m]).then_inc(*act_did.up())
                    bank.drained = act_did.now()
                    bank.held = False
                    inner.append((hidden, act_did.now()))
                yield True
                for m, (hidden, active) in enumerate(inner):
                    cw2 = second[m]
                    bank = next_bank()

                    @block.tensor
                    def _(pe):
                        pe.wait_ge(*cw2.landed)
                        pe.wait_ge(*bank.drained)
                        pe.wait_ge(*active)
                        if m == 0:
                            mm = pe.matmul(bank.t[:, 0:2 * NC], cw2.raw[:, 0, :], hidden, start=True, stop=True)
                        else:
                            for g in range(2):
                                mm = pe.matmul(bank.t[0:NC, g * HD:(g + 1) * HD], hidden[:, g * NC:(g + 1) * NC],
                                               cw2.raw[:, 0, 0:HD], start=True, stop=True)
                        mm.then_inc(*pe_did.up())
                    cw2.used = pe_did.now()

                    @block.vector
                    def _(dve):
                        dve.wait_ge(*pe_did.now())
                        if m == 0:
                            dve.tensor_copy(kcT, bank.t[:, 0:2 * NC]).then_inc(*dve_did.up())
                        else:
                            dve.tensor_copy(vcmp[0:NC, :], bank.t[0:NC, 0:2 * HD]).then_inc(*dve_did.up())
                    bank.drained = there["compressed"] = dve_did.now()
                    yield True
            compression = compress()

            def step():
                next(compression, None)

            jobs = []
            for h in range(FOX_H):
                b = HD * (h % 2)
                for tt in range(TT):
                    n = (tt + 1) * P
                    jobs.append(dict(
                        qk=[(qT[b:b + HD, h // 2, tt * P:(tt + 1) * P], kT[b:b + HD, h // 2, 0:n]),
                            (ident[0:FOX_H, h:h + 1].broadcast_to([FOX_H, P]), c_neg[:, 0:n])],
                        n=n, bias=causal[:, tt, 0:n], scale=HD ** -0.5, dv=HD,
                        v=[z[:, kb, EV["fv"] + h * HD:EV["fv"] + (h + 1) * HD] for kb in range(tt + 1)],
                        out=o_buf[:, tt, h * HD:(h + 1) * HD], then=step))
            for h in range(NSA_H):
                b, g = HD * (h % 2), h // (NSA_H // 2)
                for tt in range(TT):
                    q = qT[b:b + HD, 4 + h // 2, tt * P:(tt + 1) * P]
                    dst = o_buf[:, tt, 512 + h * HD:512 + (h + 1) * HD]
                    jobs.append(dict(qk=[(q, kcT[b:b + HD, g * NC:(g + 1) * NC])], n=NC,
                                     bias=C("cmp", (TT,))[:, tt, :], scale=HD ** -0.5, dv=HD,
                                     v=[vcmp[0:NC, g * HD:(g + 1) * HD]], out=dst, guard=True,
                                     keys_ready=lambda: there["compressed"],
                                     mul=sgate[:, tt, 3 * h:3 * h + 1]))
                    n = (tt + 1) * P
                    for m, name in enumerate(("vs", "vw")):
                        jobs.append(dict(qk=[(q, kT[b:b + HD, 4 + 2 * m + g, 0:n])], n=n, bias=causal[:, tt, 0:n],
                                         scale=HD ** -0.5, dv=HD,
                                         v=[z[:, kb, EV[name] + g * HD:EV[name] + (g + 1) * HD] for kb in range(tt + 1)],
                                         out=dst, add=True, mul=sgate[:, tt, 3 * h + 1 + m:3 * h + 2 + m]))
            attention(jobs, there[1024])
            ready = halves_of_o()
            out_ = Sublayer(post_gain)
            gemm(h_in, KD, D, out_.leave, ready)
            return out_

        def diff_mixer(post_gain):
            ready = pre_norm(x, col_of[("pre", 1, 0)], rs[:, 0:2])
            to_z = to_sbuf(lambda tt, c, n: z[:, tt, c:c + n], rs_of(0))
            rotated = []

            def evac(tt, c, n, bank, full):
                to_z(tt, c, n, bank, full)
                if tt < TT - 1:
                    return
                if c == 2560:
                    rotated.append(marks())
                    return
                prepare()
                if c == 1536:
                    rotate(heads_of(0, 32), 32, ROPE_HALF, cos1, sin1)
                    rotated.append(marks())
                elif c == 2048:
                    for first, dstT in ((0, qT), (D, kT)):
                        to_T(KD, lambda b, tt: z[:, tt, first + b * P:first + (b + 1) * P],
                             lambda b, n: dstT[:, b:b + n, :], after=rotated[0])
            gemm(h_in, KD, 3 * D, evac, ready)
            jobs = []
            for h in range(DIFF_H):
                for tt in range(TT):
                    n = (tt + 1) * P
                    for m in range(2):
                        b = HD * m
                        jobs.append(dict(qk=[(qT[b:b + HD, h, tt * P:(tt + 1) * P], kT[b:b + HD, h, 0:n])], n=n,
                                         bias=causal[:, tt, 0:n], scale=HD ** -0.5, dv=2 * HD,
                                         v=[z[:, kb, 2 * D + h * P:2 * D + (h + 1) * P] for kb in range(tt + 1)],
                                         out=o_buf[:, tt, h * P:(h + 1) * P], add=(m == 1),
                                         mul=neg_lam if m == 1 else None))
            ov = o_buf[:, :, :].rearrange("p t (h w) -> p t h w", h=DIFF_H)
            HH = DIFF_H // 2

            def norm(half):
                o = ov[:, :, half * HH:(half + 1) * HH, :]
                r = rs[:, 2 + half * TT * HH:2 + (half + 1) * TT * HH]
                rstd_heads((o, r, HH, P, sq[:, :, half * 512:(half + 1) * 512]))
                scale_heads(o, o, r, HH)
                normed.append(marks())
            normed = []
            jobs[2 * TT * HH + 1]["then"] = lambda: norm(0)
            attention(jobs, rotated[1])
            c = col_of["subln"] % P
            ready = halves_of_o(scale=lambda b: cols[:, 1, c:c + 1], marks_of=normed)
            norm(1)
            out_ = Sublayer(post_gain)
            gemm(h_in, KD, D, out_.leave, ready)
            return out_

        def memory_attention(l, post_gain, post_norm):
            W = MEM_H * HD
            c = col_of[("mem", l)]
            ready = to_T(KD, lambda b, tt: gate[:, tt, b * P:(b + 1) * P], hi_of(h2_hi), dst_lo=hi_of(h2_lo),
                 scale=lambda b: cols[:, 0, c + b:c + b + 1], after=attended["o"])
            prepare()
            post_norm()
            gemm(h2_in, KD, W, to_sbuf(lambda tt, c, n: z[:, tt, W + c:W + c + n], rs_of(28)), ready)
            gemm(h2_in, KD, W, to_sbuf(lambda tt, c, n: z[:, tt, 2 * W + c:2 * W + c + n], rs_of(28)), ready)
            ready = pre_norm(x, col_of[("pre", l, 2)], rs[:, 0:2])
            gemm(h_in, KD, W, to_sbuf(lambda tt, c, n: z[:, tt, c:c + n], rs_of(0)), ready)
            to_T(2, lambda b, tt: z[:, tt, b * P:(b + 1) * P], lambda b, n: qT[:, b:b + n, :])
            to_T(2, lambda b, tt: z[:, tt, W + b * P:W + (b + 1) * P], lambda b, n: kT[:, b:b + n, :])
            jobs = []
            for h in range(MEM_H):
                b = HD * (h % 2)
                for tt in range(TT):
                    jobs.append(dict(qk=[(qT[b:b + HD, h // 2, tt * P:(tt + 1) * P], kT[b:b + HD, h // 2, :])], n=T,
                                     bias=None, scale=HD ** -0.5, dv=HD,
                                     v=[z[:, kb, 2 * W + h * HD:2 * W + (h + 1) * HD] for kb in range(TT)],
                                     out=o_buf[:, tt, h * HD:(h + 1) * HD]))
            attention(jobs)
            to_T(2, lambda b, tt: o_buf[:, tt, b * P:(b + 1) * P], hi_of(h_hi), dst_lo=hi_of(h_lo))
            out_ = Sublayer(post_gain)
            gemm(h_in, W // P, D, out_.leave)
            return out_

        for l in range(DEPTH):
            mixed = (even_mixer if l % 2 == 0 else diff_mixer)(load_gain(a["sandwich_g"][l, 1, :]))
            remembered = memory_attention(l, load_gain(a["sandwich_g"][l, 3, :]), mixed.finish)
            remembered.finish()
            ready = pre_norm(x, col_of[("pre", l, 4)], rs[:, 0:2])
            out_ = Sublayer(load_gain(a["sandwich_g"][l, 5, :]))
            ffn(ready, rs_of(0), lambda tt, half, bank, full: out_.leave(tt, half * 512, 512, bank, full))
            out_.finish()

        bias_h = [gain[:, i // 2, (i % 2) * 512:(i % 2 + 1) * 512].rearrange("p (t k) -> p t k", t=TT)
                  for i in range(4)]
        bias_free = [marks() for _ in range(4)]
        bias_there = {}
        work2 = hT2[:, :, :].rearrange("p (t a) n -> p t (a n)", t=TT)

        def load_bias(l, h):
            s = h % 4
            rows_n = T // GRID_W

            @block.sync
            def _(sp):
                sp.wait_ge(*table_landed.now())
                sp.wait_ge(*bias_free[s].act)
                sp.wait_ge(*bias_free[s].dve)
                sp.wait_ge(*bias_free[s].pool)
                for qr in range(rows_n):
                    tt, part = qr // 2, (qr % 2) * GRID_W
                    first = ((l * NA_H + h) * GRID_W * TBL_W
                             + (NA_WIN_R - 1 - qr) * RPB_C + NA_WIN_C - 1 - TBL_LO)
                    src = bass.AP(tensor=table.tensor, offset=first,
                                  ap=[[TBL_W - 1, GRID_W], [RPB_C, rows_n], [1, GRID_W]])
                    sp.dma_start(bias_h[s][part:part + GRID_W, tt, :].rearrange("p (r c) -> p r c", r=rows_n),
                                 src).then_inc(*gain_landed[s].up(16))
            got = gain_landed[s].now()

            @block.gpsimd
            def _(pool):
                pool.wait_ge(*got)
                for tt in range(TT):
                    pool.tensor_tensor(bias_h[s][:, tt, :], bias_h[s][:, tt, :], C("na"), ALU.add).then_inc(
                        *pool_did.up())
            bias_there[h] = pool_did.now()

        def silu_into(dst, src, after):
            @block.scalar
            def _(act):
                act.wait_ge(*after.pe)
                act.wait_ge(*after.act)
                act.wait_ge(*after.dve)
                act.activation(dst, src, ACT.Silu).then_inc(*act_did.up())

        gate_there, gate_used, mixed = {}, {}, {}

        def start_gates():
            before = marks()

            def gates(tt, c, n, bank, full):
                @block.scalar
                def _(act):
                    act.wait_ge(*full)
                    act.wait_ge(*gate_used.get((tt, c), before.dve))
                    act.activation(gate[:, tt, c:c + n], bank.t[:, 0:n], ACT.Sigmoid,
                                   scale=rs[:, tt:tt + 1]).then_inc(*act_did.up())
                bank.drained = gate_there[(tt, c)] = act_did.now()
            fillers.append(gemm_steps(h_in, KD, D, gates, before))

        def start_branch(i, y, scale=None, fills=0, after=None):
            ready = to_T(4, lambda b, tt: y[:, tt, b * P:(b + 1) * P], hi_of(y_hi), dst_lo=hi_of(y_lo), scale=scale,
                         fills=fills, after=after)
            before = marks()

            def mix(tt, c, n, bank, full):
                mine, sum_ = gate[:, tt, c:c + n], o_buf[:, tt, c:c + n]

                @block.vector
                def _(dve):
                    dve.wait_ge(*full)
                    dve.wait_ge(*gate_there[(tt, c)])
                    dve.wait_ge(*before.dve)
                    dve.tensor_tensor(sum_ if i == 0 else mine, bank.t[:, 0:n], mine, ALU.mult).then_inc(*dve_did.up())
                bank.drained = dve_did.now()
                if i == 0:
                    gate_used[(tt, c)] = mixed[(tt, c)] = dve_did.now()
                    return

                @block.gpsimd
                def _(pool):
                    pool.wait_ge(*dve_did.now())
                    pool.wait_ge(*mixed[(tt, c)])
                    pool.tensor_tensor(sum_, sum_, mine, ALU.add).then_inc(*pool_did.up())
                gate_used[(tt, c)] = mixed[(tt, c)] = pool_did.now()
            fillers.append(gemm_steps((y_hi, y_lo), 4, D, mix, ready))

        def project(l, ready):
            to_z = to_sbuf(lambda tt, c, n: z[:, tt, c:c + n], rs_of(0))
            q, k = heads_of(ZC["naq"], NA_H), heads_of(ZC["nak"], NA_H)
            rq, rk = rs[:, 2:2 + TT * NA_H], stat[:, 16:16 + TT * NA_H]
            normed = []

            def evac(tt, c, n, bank, full):
                to_z(tt, c, n, bank, full)
                if tt < TT - 1:
                    return
                if c == IN_STARTS[-1]:
                    normed.append(marks())
                    return
                prepare()
                if c == 512:
                    rstd_heads((q, rq, NA_H, HD, sq), (k, rk, NA_H, HD, work2))
                elif c == 3072:
                    scale_heads(q, q, rq, NA_H)
                    scale_heads(k, k, rk, NA_H)
                    normed.append(marks())
                elif c == 3584:
                    rstd_heads(*((z[:, :, ZC[name]:ZC[name] + 2 * P].unsqueeze(2), r, 1, 2 * P,
                                  sq[:, :, m * 2 * P:(m + 1) * 2 * P]) for m, (name, r) in enumerate(
                                      (("cq", rs[:, 24:26]), ("ckv", rs[:, 26:28])))))
                elif c == 1536:
                    for h in range(4):
                        load_bias(l, h)
                elif c == 2560:
                    for name, first, dstT in (("na_q_norm_2", ZC["naq"], qT), ("na_k_norm_2", ZC["nak"], kT)):
                        gc = col_of[(name, l)] % P
                        to_T(4, lambda b, tt: z[:, tt, first + b * P:first + (b + 1) * P],
                             lambda b, n: dstT[:, b:b + n, :], scale=lambda b: cols[:, 1, gc:gc + 1], after=normed[0])
            gemm(h_in, KD, ZC["gates"], evac, ready, IN_STARTS)
            return normed[1]

        def neighborhood(l, after):
            y = sq[:, :, 0:512]

            def reload(h):
                bias_free[h] = marks()
                load_bias(l, h + 4)
            jobs = []
            for h in range(NA_H):
                b = HD * (h % 2)
                for tt in range(TT):
                    jobs.append(dict(qk=[(qT[b:b + HD, h // 2, tt * P:(tt + 1) * P], kT[b:b + HD, h // 2, :])],
                                     n=T, bias=bias_h[h % 4][:, tt, :], scale=HD ** -0.5, dv=HD,
                                     v=[z[:, kb, ZC["nav"] + h * HD:ZC["nav"] + (h + 1) * HD] for kb in range(TT)],
                                     out=y[:, tt, h * HD:(h + 1) * HD], bias_ready=lambda h=h: bias_there[h],
                                     scored=(lambda h=h: reload(h)) if h < 4 and tt == TT - 1 else None))
            attention(jobs, after)
            start_gates()
            start_branch(0, y, after=attended["o"])
            start_gates()

        def gated_linear(l):
            NP2 = GLA_H // 2
            NCH = T // GLA_CHUNK
            dirs = (("gla_gf_up_2", "gla_gf_bias_2", ZC["gfl"]), ("gla_gb_up_2", "gla_gb_bias_2", ZC["gbl"]))
            lowT = kT[0:GLA_RANK + 1, 6:8, :]
            before = marks()

            @block.sync
            def _(sp):
                sp.wait_ge(*before.pe)
                sp.wait_ge(*before.act)
                sp.wait_ge(*before.dve)
                sp.wait_ge(*before.pool)
                for d, (w, b, _) in enumerate(dirs):
                    sp.dma_start(up[0:GLA_RANK, d, :], a[w][l]).then_inc(*misc_landed.up(16))
                    sp.dma_start(up[GLA_RANK:GLA_RANK + 1, d, :], a[b][l:l + 1, :]).then_inc(*misc_landed.up(16))

            @block.gpsimd
            def _(pool):
                pool.wait_ge(*before.pe)
                pool.wait_ge(*before.act)
                pool.wait_ge(*before.dve)
                pool.wait_ge(*before.pool)
                pool.memset(lowT, 1.0).then_inc(*pool_did.up())
            to_T(2, lambda d, tt: z[:, tt, dirs[d][2]:dirs[d][2] + GLA_RANK],
                 lambda d, n: kT[0:GLA_RANK, 6 + d:6 + d + n, :], width=GLA_RANK, fills=GLA_FILLS[0])
            got = misc_landed.now()
            g = tmp[:, :, 0:512]
            b_sum = sq[:, :, 0:512]
            to_end = sq[:, :, 512:1024]
            before = marks()
            pair = [next_bank() for _ in range(TT)]
            for tt, bank in enumerate(pair):
                @block.tensor
                def _(pe):
                    pe.wait_ge(*got)
                    pe.wait_ge(*bank.drained)
                    pe.wait_ge(*before.act)
                    pe.wait_ge(*before.dve)
                    pe.wait_ge(*before.pool)
                    for d in range(2):
                        m = pe.matmul(bank.t[:, d * T:(d + 1) * T], lowT[:, d, tt * P:(tt + 1) * P], up[:, d, :],
                                      start=True, stop=True)
                    m.then_inc(*pe_did.up())
            log_sigmoid(*((g[:, tt, :], pair[tt].t[:, :], b_sum[:, tt, :], to_end[:, tt, :]) for tt in range(TT)))
            for bank in pair:
                bank.drained = dve_did.now()
            before = marks()
            fill(GLA_FILLS[1])
            e_pos, e_neg, e_end = qT[:, 0:4, :], qT[:, 4:8, :], kT[:, 0:4, :]
            for tt in range(TT):
                for d in range(2):
                    bank = next_bank()

                    @block.tensor
                    def _(pe):
                        pe.wait_ge(*bank.drained)
                        pe.wait_ge(*before.act)
                        pe.wait_ge(*before.dve)
                        pe.wait_ge(*before.pool)
                        gd = g[:, tt, d * T:(d + 1) * T]
                        pe.matmul(bank.t[:, 0:T], C("tri_f" if d == 0 else "tri_b"), gd, start=True, stop=True)
                        m = pe.matmul(bank.t[:, T:2 * T], C("chunk_all"), gd, start=True, stop=True)
                        m.then_inc(*pe_did.up())
                    full = pe_did.now()
                    bs = b_sum[:, tt, d * T:(d + 1) * T]
                    te = to_end[:, tt, d * T:(d + 1) * T]
                    i = tt * 2 + d

                    @block.vector
                    def _(dve):
                        dve.wait_ge(*full)
                        dve.wait_ge(*before.pe)
                        dve.wait_ge(*before.act)
                        dve.wait_ge(*before.dve)
                        dve.wait_ge(*before.pool)
                        dve.tensor_copy(bs, bank.t[:, 0:T]).then_inc(*dve_did.up())
                        dve.wait_ge(*dve_did.now())
                        dve.tensor_tensor(te, bank.t[:, T:2 * T], bs, ALU.subtract).then_inc(*dve_did.up())

                    @block.scalar
                    def _(act):
                        act.wait_ge(*dve_did.now())
                        act.wait_ge(*before.pe)
                        act.wait_ge(*before.act)
                        act.wait_ge(*before.dve)
                        act.wait_ge(*before.pool)
                        act.activation(e_pos[:, i, :], bs, ACT.Exp).then_inc(*act_did.up())
                        act.activation(e_neg[:, i, :], bs, ACT.Exp, scale=-1.0).then_inc(*act_did.up())
                        act.activation(e_end[:, i, :], te, ACT.Exp).then_inc(*act_did.up())
                    bank.drained = dve_did.now()
            dec = stat[:, 0:16]
            bank = next_bank()

            @block.tensor
            def _(pe):
                pe.wait_ge(*bank.drained)
                pe.wait_ge(*before.act)
                pe.wait_ge(*before.dve)
                pe.wait_ge(*before.pool)
                for d in range(2):
                    for pr in range(NP2):
                        for tt in range(TT):
                            c = (d * NP2 + pr) * NCH + tt * 2
                            m = pe.matmul(bank.t[:, c:c + 2], g[:, tt, d * T + pr * P:d * T + (pr + 1) * P],
                                          C("chunk_of"), start=True, stop=True)
                m.then_inc(*pe_did.up())

            @block.scalar
            def _(act):
                act.wait_ge(*pe_did.now())
                act.wait_ge(*before.dve)
                act.activation(dec, bank.t[:, 0:16], ACT.Exp).then_inc(*act_did.up())
            bank.drained = act_did.now()
            qe, ke = tmp[:, :, 0:512], tmp[:, :, 512:1024]
            spare = gain[:, :, :].rearrange("p t (a n) -> p (t a) n", n=T)
            kend = spare[:, 0:4, :]
            before = marks()
            zq = lambda tt: z[:, tt, ZC["gq"]:ZC["gq"] + T]
            zk = lambda tt: z[:, tt, ZC["gk"]:ZC["gk"] + T]

            @block.vector
            def _(dve):
                dve.wait_ge(*before.pe)
                dve.wait_ge(*before.act)
                dve.wait_ge(*before.dve)
                dve.wait_ge(*before.pool)
                for tt in range(TT):
                    for d in range(2):
                        i = tt * 2 + d
                        dve.scalar_tensor_tensor(qe[:, tt, d * T:(d + 1) * T], zq(tt), GLA_DK ** -0.5, e_pos[:, i, :],
                                                 ALU.mult, ALU.mult).then_inc(*dve_did.up())
                        dve.tensor_tensor(ke[:, tt, d * T:(d + 1) * T], zk(tt), e_neg[:, i, :],
                                          ALU.mult).then_inc(*dve_did.up())

            @block.gpsimd
            def _(pool):
                pool.wait_ge(*before.pe)
                pool.wait_ge(*before.act)
                pool.wait_ge(*before.dve)
                pool.wait_ge(*before.pool)
                for tt in range(TT):
                    pool.memset(sq[:, tt, :], 0.0).then_inc(*pool_did.up())
                for tt in range(TT):
                    for d in range(2):
                        i = tt * 2 + d
                        pool.tensor_tensor(kend[:, i, :], zk(tt), e_end[:, i, :], ALU.mult).then_inc(*pool_did.up())
                pool.wait_ge(*pool_did.now())
                pool.memset(kT[:, :, :], 0.0).then_inc(*pool_did.up())
                pool.memset(spare[:, 4:8, :], 0.0).then_inc(*pool_did.up())
            gr = z[:, :, ZC["gr"]:ZC["gr"] + 512]
            ready_q = marks()
            silu_into(gr, gr, before)
            qeT, keT = qT[:, 0:4, :], qT[:, 4:8, :]
            multiplied = Marks(ready_q.pe, ready_q.act, ready_q.dve, before.pool)
            to_T(4, lambda b, tt: qe[:, tt, b * P:(b + 1) * P], lambda b, n: qT[:, b:b + n, :], fills=GLA_FILLS[2],
                 after=multiplied)
            to_T(4, lambda b, tt: ke[:, tt, b * P:(b + 1) * P], lambda b, n: qT[:, 4 + b:4 + b + n, :],
                 after=multiplied)
            aT = sq[:, :, :].rearrange("p t (d n) -> p t d n", d=2)
            before = marks()
            for d in range(2):
                for par in range(2):
                    bank = next_bank()
                    r0 = par * HD

                    @block.tensor
                    def _(pe):
                        pe.wait_ge(*bank.drained)
                        pe.wait_ge(*before.act)
                        pe.wait_ge(*before.dve)
                        pe.wait_ge(*before.pool)
                        for tt in range(TT):
                            for pr in range(NP2):
                                ts_ = slice(tt * P, (tt + 1) * P)
                                c = (tt * NP2 + pr) * P
                                m = pe.matmul(bank.t[:, c:c + P], keT[r0:r0 + HD, d * 2 + pr, ts_],
                                              qeT[r0:r0 + HD, d * 2 + pr, ts_], start=True, stop=True)
                        m.then_inc(*pe_did.up())

                    @block.vector
                    def _(dve):
                        dve.wait_ge(*pe_did.now())
                        dve.wait_ge(*before.pe)
                        dve.wait_ge(*before.act)
                        dve.wait_ge(*before.dve)
                        dve.wait_ge(*before.pool)
                        keep = C("tri_f" if d == 0 else "strict_b").bitcast(I32)
                        for tt in range(TT):
                            dve.copy_predicated(
                                aT[:, tt, d, :].rearrange("p (r q n) -> p r q n", r=NP2, q=2)[:, :, par, :],
                                keep.unsqueeze(1).broadcast_to([P, NP2, P]),
                                bank.t[:, tt * T:(tt + 1) * T].rearrange("p (r n) -> p r n", r=NP2)).then_inc(
                                *dve_did.up())
                    bank.drained = dve_did.now()
            state = {}
            states = [kT[:, 2 * i:2 * i + 2, :] for i in range(4)] + [spare[:, 4 + 2 * i:6 + 2 * i, :] for i in range(2)]
            order = [(0, 0, 1, 0), (0, 1, 2, 1), (0, 2, 3, 2), (1, 3, 2, 3), (1, 2, 1, 4), (1, 1, 0, 5)]
            before = marks()
            for d, c, nxt, slot in order:
                tt, b0 = c // 2, GLA_CHUNK * (c % 2)
                bank = next_bank()

                @block.tensor
                def _(pe):
                    pe.wait_ge(*bank.drained)
                    pe.wait_ge(*before.act)
                    pe.wait_ge(*before.dve)
                    pe.wait_ge(*before.pool)
                    for pr in range(NP2):
                        m = pe.matmul(bank.t[:, pr * T:(pr + 1) * T],
                                      kend[b0:b0 + GLA_CHUNK, tt * 2 + d, pr * P:(pr + 1) * P],
                                      z[b0:b0 + GLA_CHUNK, tt, ZC["gv"] + pr * T:ZC["gv"] + (pr + 1) * T],
                                      start=True, stop=True)
                    m.then_inc(*pe_did.up())

                @block.vector
                def _(dve):
                    dve.wait_ge(*pe_did.now())
                    dve.wait_ge(*dve_did.now())
                    dve.wait_ge(*before.pe)
                    dve.wait_ge(*before.act)
                    dve.wait_ge(*before.dve)
                    dve.wait_ge(*before.pool)
                    for par in range(2):
                        ps = slice(par * HD, (par + 1) * HD)
                        for pr in range(NP2):
                            src = bank.t[ps, pr * T + par * P:pr * T + (par + 1) * P]
                            at = (ps, pr, slice(par * P, (par + 1) * P))
                            if (d, c) not in state:
                                dve.tensor_copy(states[slot][at], src).then_inc(*dve_did.up())
                            else:
                                col = (d * NP2 + pr) * NCH + c
                                dve.scalar_tensor_tensor(states[slot][at], states[state[(d, c)]][at],
                                                         dec[ps, col:col + 1], src, ALU.mult,
                                                         ALU.add).then_inc(*dve_did.up())
                bank.drained = dve_did.now()
                state[(d, nxt)] = slot
            before = marks()
            fill(GLA_FILLS[3])
            og = tmp[:, :, 0:512]
            for tt in range(TT):
                bank = next_bank()

                @block.tensor
                def _(pe):
                    pe.wait_ge(*bank.drained)
                    pe.wait_ge(*before.act)
                    pe.wait_ge(*before.dve)
                    pe.wait_ge(*before.pool)
                    for h in range(GLA_H):
                        vh = z[:, tt, ZC["gv"] + h * P:ZC["gv"] + (h + 1) * P]
                        for d in range(2):
                            m = pe.matmul(bank.t[:, h * P:(h + 1) * P], aT[:, tt, d, h * P:(h + 1) * P], vh,
                                          start=(h == 0 and d == 0), stop=False, skip_group_check=True)
                    for pr in range(NP2):
                        inter = [(d, c) for c in (2 * tt, 2 * tt + 1) for d in range(2) if (d, c) in state]
                        for n, (d, c) in enumerate(inter):
                            r0 = GLA_CHUNK * (c % 2)
                            m = pe.matmul(bank.t[r0:r0 + GLA_CHUNK, pr * T:(pr + 1) * T],
                                          qeT[:, d * 2 + pr, c * GLA_CHUNK:(c + 1) * GLA_CHUNK],
                                          states[state[(d, c)]][:, pr, :],
                                          start=False, stop=(n == len(inter) - 1), skip_group_check=True)
                    m.then_inc(*pe_did.up())

                @block.vector
                def _(dve):
                    dve.wait_ge(*pe_did.now())
                    dve.wait_ge(*before.pe)
                    dve.wait_ge(*before.act)
                    dve.wait_ge(*before.dve)
                    dve.wait_ge(*before.pool)
                    dve.tensor_copy(og[:, tt, :], bank.t[:, :]).then_inc(*dve_did.up())
                bank.drained = dve_did.now()
            ov = og.rearrange("p t (h w) -> p t h w", h=GLA_H)
            r = rs[:, 2:2 + TT * GLA_H]
            rstd_heads((ov, r, GLA_H, GLA_DV, sq))
            scale_heads(ov, ov, r, GLA_H)

            @block.vector
            def _(dve):
                dve.wait_ge(*pe_did.now())
                dve.wait_ge(*act_did.now())
                dve.wait_ge(*dve_did.now())
                dve.wait_ge(*pool_did.now())
                dve.tensor_tensor(og, og, gr, ALU.mult).then_inc(*dve_did.up())
            gc = col_of[("gla_out", l)] % P
            start_branch(1, og, scale=lambda b: cols[:, 1, gc:gc + 1], fills=GLA_FILLS[4])

        def latent(l):
            start = marks()
            q = z[:, :, 0:MLA_H * MLA_QK]
            kv = z[:, :, ZC["gq"]:ZC["gq"] + MLA_H * (MLA_NOPE + MLA_V)]
            both = (("cq", ZC["cq"], MLA_H * MLA_QK, q), ("ckv", ZC["ckv"], MLA_H * (MLA_NOPE + MLA_V), kv))
            split = []
            for m, (name, c, width, dst) in enumerate(both):
                gc = col_of[(name, l)] % P
                to_T(2, lambda b, tt: z[:, tt, c + b * P:c + (b + 1) * P],
                     lambda b, n: h2_hi[:, 2 * m + b:2 * m + b + n, :],
                     dst_lo=lambda b, n: h2_lo[:, 2 * m + b:2 * m + b + n, :],
                     scale=lambda b: cols[:, 1, gc + b:gc + b + 1], after=start)
                split.append(marks())
            while fillers:
                fill()
            qv = q.rearrange("p t (h w) -> p t h w", h=MLA_H)
            kvv = kv.rearrange("p t (h w) -> p t h w", h=MLA_H)
            kf = tmp[:, :, 0:MLA_H * MLA_QK]
            kfv = kf.rearrange("p t (h w) -> p t h w", h=MLA_H)

            @block.gpsimd
            def _(pool):
                pool.wait_ge(*start.pe)
                pool.wait_ge(*start.act)
                pool.wait_ge(*start.dve)
                pool.wait_ge(*start.pool)
                for tt in range(TT):
                    pool.tensor_copy(kfv[:, tt, :, MLA_NOPE:MLA_QK],
                                     z[:, tt, ZC["kr"]:ZC["kr"] + MLA_ROPE].unsqueeze(1).broadcast_to(
                                         [P, MLA_H, MLA_ROPE])).then_inc(*pool_did.up())
            gemm((h2_hi[:, 0:2, :], h2_lo[:, 0:2, :]), 2, both[0][2],
                 to_sbuf(lambda tt, c, n: q[:, tt, c:c + n], rs_of(24)), split[0])
            r_q, r_k = rs[:, 6:6 + TT * MLA_H], rs[:, 16:16 + TT * MLA_H]
            before = marks()

            def evac_kv(tt, c, n, bank, full):
                heads = slice(c // (MLA_NOPE + MLA_V), (c + n) // (MLA_NOPE + MLA_V))
                ps = bank.t[:, 0:n].rearrange("p (h w) -> p h w", w=MLA_NOPE + MLA_V)
                r = rs[:, 26 + tt:27 + tt]
                key, value = kfv[:, tt, heads, 0:MLA_NOPE], kvv[:, tt, heads, MLA_NOPE:MLA_NOPE + MLA_V]
                if tt == 0:
                    @block.vector
                    def _(dve):
                        dve.wait_ge(*full)
                        dve.wait_ge(*before.pe)
                        dve.wait_ge(*before.act)
                        dve.wait_ge(*before.dve)
                        dve.wait_ge(*before.pool)
                        dve.tensor_scalar(key, ps[:, :, 0:MLA_NOPE], r, None, ALU.mult).then_inc(*dve_did.up())
                        dve.tensor_scalar(value, ps[:, :, MLA_NOPE:MLA_NOPE + MLA_V], r, None,
                                          ALU.mult).then_inc(*dve_did.up())
                    bank.drained = dve_did.now()
                else:
                    @block.scalar
                    def _(act):
                        act.wait_ge(*full)
                        act.wait_ge(*before.pe)
                        act.wait_ge(*before.act)
                        act.wait_ge(*before.dve)
                        act.wait_ge(*before.pool)
                        act.activation(key, ps[:, :, 0:MLA_NOPE], ACT.Copy, scale=r).then_inc(*act_did.up())
                        act.activation(value, ps[:, :, MLA_NOPE:MLA_NOPE + MLA_V], ACT.Copy,
                                       scale=r).then_inc(*act_did.up())
                    bank.drained = act_did.now()
            gemm((h2_hi[:, 2:4, :], h2_lo[:, 2:4, :]), 2, both[1][2], evac_kv, split[1])
            start_gates()
            pair = ((qv, "mla_q", r_q, qT, sq), (kfv, "mla_k", r_k, kT, gain[:, :, :]))
            rstd_heads((qv, r_q, MLA_H, MLA_QK, sq), (kfv, r_k, MLA_H, MLA_QK, gain[:, :, :]))
            for v, name, r, dstT, work in pair:
                scale_heads(v, v, r, MLA_H)
            scaled = marks()

            @block.vector
            def _(dve):
                dve.wait_ge(*scaled.dve)
                dve.wait_ge(*scaled.pool)
                for m, (v, name, r, dstT, work) in enumerate(pair):
                    for tt in range(TT):
                        rot = v[:, tt, :, MLA_NOPE:MLA_QK]
                        dve.tensor_tensor(rot, rot, rgain[:, l * 2 + m, :].unsqueeze(1).broadcast_to(
                            [P, MLA_H, MLA_ROPE]), ALU.mult).then_inc(*dve_did.up())
            for v, name, r, dstT, work in pair:
                rotate(v[:, :, :, MLA_NOPE:MLA_QK], MLA_H, MLA_ROPE // 2, C("cos2", (TT,)), C("sin2", (TT,)), work)
            rotated = marks()
            for m, (v, name, r, dstT, work) in enumerate(pair):
                gc = col_of[(name, l)] % P
                to_T(MLA_H, lambda h, tt: v[:, tt, h, 0:MLA_NOPE], lambda b, n: dstT[:, b:b + n, :],
                     scale=lambda b: cols[:, 1, gc:gc + 1], fills=MLA_FILLS[m], after=scaled)
            for m, (v, name, r, dstT, work) in enumerate(pair):
                to_T(MLA_H, lambda h, tt: v[:, tt, h, MLA_NOPE:MLA_QK], lambda b, n: dstT[0:MLA_ROPE, 4 + b:4 + b + n, :],
                     width=MLA_ROPE, fills=MLA_FILLS[2 + m], after=rotated)
            y = sq[:, :, 0:512]
            jobs = []
            for h in range(MLA_H):
                for tt in range(TT):
                    ts_ = slice(tt * P, (tt + 1) * P)
                    jobs.append(dict(qk=[(qT[:, h, ts_], kT[:, h, :]),
                                         (qT[0:MLA_ROPE, 4 + h, ts_], kT[0:MLA_ROPE, 4 + h, :])],
                                     n=T, bias=None, scale=MLA_QK ** -0.5, dv=MLA_V,
                                     v=[kvv[:, kb, h, MLA_NOPE:MLA_NOPE + MLA_V] for kb in range(TT)],
                                     out=y[:, tt, h * P:(h + 1) * P]))
            bias_free[:] = [rotated] * 4
            attention(jobs)
            start_branch(2, y)
            while fillers:
                fill()

        def add_x(tt, c, n, bank, full):
            @block.vector
            def _(dve):
                dve.wait_ge(*full)
                dve.wait_ge(*act_did.now())
                xs = x[:, tt, c:c + n]
                dve.tensor_tensor(xs, xs, bank.t[:, 0:n], ALU.add).then_inc(*dve_did.up())
            x_ready[c // 512] = bank.drained = dve_did.now()

        for l in range(DEPTH):
            ready = pre_norm(x, col_of[("ffn1_norm_2", l)], rs[:, 0:2])
            ffn(ready, rs_of(0), add_half)
            ready = pre_norm(x, col_of[("mix_norm_2", l)], rs[:, 0:2])
            neighborhood(l, project(l, ready))
            gated_linear(l)
            latent(l)
            by_half = [Marks(pe_did.now(), act_did.now(), dve_did.now(), mixed[(TT - 1, c)]) for c in (0, 512)]
            gemm(h_in, KD, D, add_x, halves_of_o(marks_of=by_half))
            ready = pre_norm(x, col_of[("ffn2_norm_2", l)], rs[:, 0:2])
            ffn(ready, rs_of(0), add_half)

        @block.sync
        def _(sp):
            for half in range(2):
                cs = slice(half * 512, (half + 1) * 512)
                sp.wait_ge(*x_ready[half])
                sp.dma_start(out[0].rearrange("(t p) d -> p t d", p=P)[:, :, cs], x[:, :, cs]).then_inc(
                    *out_landed.up(16))
            sp.wait_ge(*pe_did.now())
            sp.wait_ge(*act_did.now())
            sp.wait_ge(*dve_did.now())
            sp.wait_ge(*pool_did.now())
            sp.wait_ge(*out_landed.now())


def kernel(**inputs):
    from concourse import bacc
    from concourse.bass_utils import run_bass_kernel_spmd

    nc = bacc.Bacc("TRN2", target_bir_lowering=False, num_devices=1)
    arrays, aps = {}, {}
    const, early, where = constants()
    rows, vec, col_of = small_arrays(inputs)
    for name, value in {**inputs, "const": const, "early": early, "rows": rows, "vec": vec}.items():
        v = np.ascontiguousarray(value)
        arrays[f"in_{name}"] = v
        aps[name] = nc.dram_tensor(f"in_{name}", v.shape, mybir.dt.from_np(v.dtype), kind="ExternalInput").ap()
    out = nc.dram_tensor("out_0", (1, T, D), F32, kind="ExternalOutput").ap()
    program(nc, aps, where, col_of, out)
    r = run_bass_kernel_spmd(nc, [arrays], core_ids=[0])
    return r.results[0]["out_0"]
```
